# Optimizing a Trainium2 kernel written in Bass

```python
import jax, jax.numpy as jnp
from jax import lax
import numpy as np

D_MODEL = 1024
BATCH = 1
SEQ = 512
DEPTH = 1
DEC_BATCH = 1
DEC_SEQ = 32
PAST_LEN = 512

CHUNK = 64
ATT_HEADS = 8
ATT_HD = 64
ATT_LEFT = 8
ATT_CTX = ATT_LEFT * CHUNK
ATT_BAND = (ATT_LEFT + 1) * CHUNK
MAX_REL = 128
ML_HEADS = 4
ML_DK = 128
ML_DV = 128
PEER_HEADS = 8
PEER_NKEYS = 128
PEER_EXPERTS = PEER_NKEYS * PEER_NKEYS
PEER_DKEY = 128
PEER_TOPK = 16
PEER_BLOCK = 256
EPS = 1e-6
NEG = -1e30

ATT_W = ATT_HEADS * ATT_HD
ML_QK = ML_HEADS * ML_DK
ML_W = ML_HEADS * ML_DV
IN_SIZES = (ATT_W, ATT_W, ATT_W, ML_QK, ML_QK, ML_W, ML_W, ML_HEADS, ML_HEADS, D_MODEL, D_MODEL)
IN_COLS = sum(IN_SIZES)
SPLIT_POINTS = tuple(int(s) for s in np.cumsum(IN_SIZES)[:-1])

kernel_name = 'hybrid_chunk_attn_mlstm_peer_step'

def rmsnorm(x, g):
    xf = x.astype(jnp.float32)
    y = xf * lax.rsqrt(jnp.mean(xf * xf, axis=-1, keepdims=True) + EPS)
    return (y * g.astype(jnp.float32)).astype(x.dtype)

def _project(xn, w_in, b_in, f_bias):
    z = xn @ w_in + b_in
    aq, ak, av, mq, mk, mv, mo, mi, mf, ga, gb = jnp.split(z, SPLIT_POINTS, axis=-1)
    lead = xn.shape[:-1]
    att = tuple(t.reshape(lead + (ATT_HEADS, ATT_HD)) for t in (aq, ak, av))
    f32 = jnp.float32
    mq = mq.reshape(lead + (ML_HEADS, ML_DK)).astype(f32)
    mk = mk.reshape(lead + (ML_HEADS, ML_DK)).astype(f32) * (ML_DK ** -0.5)
    mv = mv.reshape(lead + (ML_HEADS, ML_DV)).astype(f32)
    ig = mi.astype(f32)
    lf = jax.nn.log_sigmoid(mf.astype(f32) + f_bias.astype(f32))
    return att, (mq, mk, mv, ig, lf), mo, ga, gb

def _rel_bias(table, d):
    return jnp.transpose(table[jnp.clip(d, -MAX_REL, MAX_REL) + MAX_REL], (2, 0, 1))

def _attend(q, kb, vb, bias, valid):
    s = jnp.einsum('blhd,bkhd->bhlk', q, kb).astype(jnp.float32) * (ATT_HD ** -0.5) + bias
    s = jnp.where(valid, s, NEG)
    p = jax.nn.softmax(s, axis=-1).astype(vb.dtype)
    return jnp.einsum('bhlk,bkhd->blhd', p, vb)

def chunk_attention_prompt(q, k, v, table):
    B, S = q.shape[:2]
    nc = S // CHUNK
    pad = ((0, 0), (ATT_CTX, 0), (0, 0), (0, 0))
    kp = jnp.pad(k, pad)
    vp = jnp.pad(v, pad)
    qc = jnp.moveaxis(q.reshape(B, nc, CHUNK, ATT_HEADS, ATT_HD), 1, 0)
    d = jnp.arange(CHUNK)[:, None] + ATT_CTX - jnp.arange(ATT_BAND)[None, :]
    bias = _rel_bias(table, d)

    def one_chunk(args):
        c, qb = args
        start = c * CHUNK
        kb = lax.dynamic_slice_in_dim(kp, start, ATT_BAND, axis=1)
        vb = lax.dynamic_slice_in_dim(vp, start, ATT_BAND, axis=1)
        valid = (start + jnp.arange(ATT_BAND)) >= ATT_CTX
        return _attend(qb, kb, vb, bias, valid)

    out = lax.map(one_chunk, (jnp.arange(nc), qc))
    return jnp.moveaxis(out, 0, 1).reshape(B, S, ATT_W)

def chunk_attention_sample(q, k, v, cache_k, cache_v, table):
    B, T = q.shape[:2]
    P = cache_k.shape[1]
    kall = jnp.concatenate([cache_k.astype(k.dtype), k], axis=1)
    vall = jnp.concatenate([cache_v.astype(v.dtype), v], axis=1)
    d = jnp.arange(T)[:, None] + P - jnp.arange(P + T)[None, :]
    bias = _rel_bias(table, d)
    out = _attend(q, kall, vall, bias, jnp.ones((P + T,), dtype=bool))
    return out.reshape(B, T, ATT_W)

def mlstm_chunk(state, q, k, v, ig, lf):
    C, n, m = state
    L = q.shape[2]
    b = jnp.cumsum(lf, axis=-1)
    a = b + m[..., None]
    D = b[..., :, None] - b[..., None, :] + ig[..., None, :]
    D = jnp.where(jnp.tril(jnp.ones((L, L), dtype=bool)), D, NEG)
    m_t = jnp.maximum(a, jnp.max(D, axis=-1))
    w_inter = jnp.exp(a - m_t)
    W = jnp.exp(D - m_t[..., None])
    Wqk = W * jnp.einsum('bhtd,bhsd->bhts', q, k)
    num = w_inter[..., None] * jnp.einsum('bhtd,bhde->bhte', q, C) + jnp.einsum('bhts,bhse->bhte', Wqk, v)
    den = w_inter * jnp.einsum('bhtd,bhd->bht', q, n) + jnp.sum(Wqk, axis=-1)
    h = num / jnp.maximum(jnp.abs(den), jnp.exp(-m_t))[..., None]
    m_new = m_t[..., -1]
    decay = jnp.exp(a[..., -1] - m_new)
    wl = W[..., -1, :]
    C_new = decay[..., None, None] * C + jnp.einsum('bhs,bhsd,bhse->bhde', wl, k, v)
    n_new = decay[..., None] * n + jnp.einsum('bhs,bhsd->bhd', wl, k)
    return (C_new, n_new, m_new), h

def mlstm_prompt(mq, mk, mv, ig, lf):
    B, S = mq.shape[:2]
    nc = S // CHUNK

    def to_chunks(t):
        t = jnp.moveaxis(t.reshape((B, nc, CHUNK) + t.shape[2:]), 1, 0)
        return jnp.swapaxes(t, 2, 3)

    f32 = jnp.float32
    init = (jnp.zeros((B, ML_HEADS, ML_DK, ML_DV), f32), jnp.zeros((B, ML_HEADS, ML_DK), f32),
            jnp.full((B, ML_HEADS), NEG, f32))
    xs = (to_chunks(mq), to_chunks(mk), to_chunks(mv), to_chunks(ig), to_chunks(lf))
    state, h = lax.scan(lambda st, c: mlstm_chunk(st, *c), init, xs)
    h = jnp.swapaxes(jnp.moveaxis(h, 0, 1), 2, 3).reshape(B, S, ML_W)
    return state, h

def mlstm_sample(mq, mk, mv, ig, lf, C, n, m):
    B, T = mq.shape[:2]
    f32 = jnp.float32
    state = (C.astype(f32), n.astype(f32), m.astype(f32))
    sw = lambda t: jnp.swapaxes(t, 1, 2)
    state, h = mlstm_chunk(state, sw(mq), sw(mk), sw(mv), sw(ig), sw(lf))
    return state, jnp.swapaxes(h, 1, 2).reshape(B, T, ML_W)

def _merge(att_out, h, mo, ga, gb, w_att_branch, w_ml_branch, w_out):
    dt = att_out.dtype
    ml_out = (jax.nn.sigmoid(mo.astype(jnp.float32)) * h).astype(dt)
    a = att_out @ w_att_branch
    b = ml_out @ w_ml_branch
    merged = jax.nn.sigmoid(ga) * a + jax.nn.sigmoid(gb) * b
    return merged @ w_out

def peer_ffn(xn, wq, sub_keys, expert_u, expert_v):
    lead = xn.shape[:-1]
    xf = xn.reshape(-1, D_MODEL)
    N = xf.shape[0]
    nblk = -(-N // PEER_BLOCK)
    xb_all = jnp.pad(xf, ((0, nblk * PEER_BLOCK - N), (0, 0))).reshape(nblk, PEER_BLOCK, D_MODEL)

    def block(xb):
        nb = xb.shape[0]
        q = (xb @ wq).reshape(nb, PEER_HEADS, 2, PEER_DKEY // 2)
        s = jnp.einsum('nhpd,hpkd->nhpk', q, sub_keys).astype(jnp.float32)
        sv, si = lax.top_k(s, PEER_TOPK)
        cand = (sv[:, :, 0, :, None] + sv[:, :, 1, None, :]).reshape(nb, PEER_HEADS, PEER_TOPK * PEER_TOPK)
        cidx = (si[:, :, 0, :, None] * PEER_NKEYS + si[:, :, 1, None, :]).reshape(nb, PEER_HEADS, PEER_TOPK * PEER_TOPK)
        fv, fi = lax.top_k(cand, PEER_TOPK)
        eidx = jnp.take_along_axis(cidx, fi, axis=-1)
        g = jax.nn.softmax(fv, axis=-1)
        u = expert_u[eidx]
        vv = expert_v[eidx]
        act = jax.nn.gelu(jnp.einsum('nhkd,nd->nhk', u, xb).astype(jnp.float32), approximate=False)
        return jnp.einsum('nhk,nhkd->nd', (g * act).astype(xb.dtype), vv)

    out = lax.map(block, xb_all).reshape(-1, D_MODEL)[:N]
    return out.reshape(lead + (D_MODEL,))

def setup_inputs(seed: int = 0) -> dict:
    key = jax.random.key(seed)
    ks = jax.random.split(key, 24)
    nrm = lambda k, s, sc: jax.random.normal(k, s, jnp.float32) * sc
    P = min(ATT_CTX, PAST_LEN)
    return {
        'x_prompt': nrm(ks[0], (BATCH, SEQ, D_MODEL), 1.0),
        'x_sample': nrm(ks[1], (DEC_BATCH, DEC_SEQ, D_MODEL), 1.0),
        'cache_att_k': nrm(ks[2], (DEPTH, DEC_BATCH, P, ATT_HEADS, ATT_HD), 1.0),
        'cache_att_v': nrm(ks[3], (DEPTH, DEC_BATCH, P, ATT_HEADS, ATT_HD), 1.0),
        'state_mlstm_C': nrm(ks[4], (DEPTH, DEC_BATCH, ML_HEADS, ML_DK, ML_DV), 0.3),
        'state_mlstm_n': nrm(ks[5], (DEPTH, DEC_BATCH, ML_HEADS, ML_DK), 0.3),
        'state_mlstm_m': nrm(ks[6], (DEPTH, DEC_BATCH, ML_HEADS), 1.0),
        'norm1_g': 1.0 + nrm(ks[7], (DEPTH, D_MODEL), 0.02),
        'w_in': nrm(ks[8], (DEPTH, D_MODEL, IN_COLS), D_MODEL ** -0.5),
        'b_in': nrm(ks[9], (DEPTH, IN_COLS), 0.02),
        'ml_f_bias': jnp.linspace(3.0, 6.0, ML_HEADS, dtype=jnp.float32)[None, :] + nrm(ks[10], (DEPTH, ML_HEADS), 0.1),
        'att_rel_bias': nrm(ks[11], (DEPTH, 2 * MAX_REL + 1, ATT_HEADS), 0.1),
        'w_att_branch': nrm(ks[12], (DEPTH, ATT_W, D_MODEL), ATT_W ** -0.5),
        'w_ml_branch': nrm(ks[13], (DEPTH, ML_W, D_MODEL), ML_W ** -0.5),
        'w_out': nrm(ks[14], (DEPTH, D_MODEL, D_MODEL), D_MODEL ** -0.5),
        'norm2_g': 1.0 + nrm(ks[15], (DEPTH, D_MODEL), 0.02),
        'peer_wq': nrm(ks[16], (DEPTH, D_MODEL, PEER_HEADS * PEER_DKEY), D_MODEL ** -0.5),
        'peer_sub_keys': nrm(ks[17], (DEPTH, PEER_HEADS, 2, PEER_NKEYS, PEER_DKEY // 2), (PEER_DKEY // 2) ** -0.5),
        'peer_u': nrm(ks[18], (DEPTH, PEER_EXPERTS, D_MODEL), D_MODEL ** -0.5),
        'peer_v': nrm(ks[19], (DEPTH, PEER_EXPERTS, D_MODEL), 0.25),
        'final_g': 1.0 + nrm(ks[20], (D_MODEL,), 0.02),
    }

def reference(x_prompt, x_sample, cache_att_k, cache_att_v, state_mlstm_C, state_mlstm_n, state_mlstm_m,
              norm1_g, w_in, b_in, ml_f_bias, att_rel_bias, w_att_branch, w_ml_branch, w_out,
              norm2_g, peer_wq, peer_sub_keys, peer_u, peer_v, final_g):
    xp = x_prompt
    xs = x_sample
    kp_l, vp_l, Cp_l, np_l, mp_l = [], [], [], [], []
    ks_l, vs_l, Cs_l, ns_l, ms_l = [], [], [], [], []
    for l in range(DEPTH):
        xn = rmsnorm(xp, norm1_g[l])
        (aq, ak, av), (mq, mk, mv, ig, lf), mo, ga, gb = _project(xn, w_in[l], b_in[l], ml_f_bias[l])
        att = chunk_attention_prompt(aq, ak, av, att_rel_bias[l])
        (Cn, nn_, mn), h = mlstm_prompt(mq, mk, mv, ig, lf)
        xp = xp + _merge(att, h, mo, ga, gb, w_att_branch[l], w_ml_branch[l], w_out[l])
        xp = xp + peer_ffn(rmsnorm(xp, norm2_g[l]), peer_wq[l], peer_sub_keys[l], peer_u[l], peer_v[l])
        keep = min(ATT_CTX, xp.shape[1])
        kp_l.append(ak[:, -keep:])
        vp_l.append(av[:, -keep:])
        Cp_l.append(Cn)
        np_l.append(nn_)
        mp_l.append(mn)
        xn = rmsnorm(xs, norm1_g[l])
        (aq, ak, av), (mq, mk, mv, ig, lf), mo, ga, gb = _project(xn, w_in[l], b_in[l], ml_f_bias[l])
        att = chunk_attention_sample(aq, ak, av, cache_att_k[l], cache_att_v[l], att_rel_bias[l])
        (Cn, nn_, mn), h = mlstm_sample(mq, mk, mv, ig, lf, state_mlstm_C[l], state_mlstm_n[l], state_mlstm_m[l])
        xs = xs + _merge(att, h, mo, ga, gb, w_att_branch[l], w_ml_branch[l], w_out[l])
        xs = xs + peer_ffn(rmsnorm(xs, norm2_g[l]), peer_wq[l], peer_sub_keys[l], peer_u[l], peer_v[l])
        ks_l.append(ak)
        vs_l.append(av)
        Cs_l.append(Cn)
        ns_l.append(nn_)
        ms_l.append(mn)
    y_prompt = rmsnorm(xp, final_g)
    y_sample = rmsnorm(xs, final_g)
    return (y_prompt, y_sample,
            jnp.stack(kp_l), jnp.stack(vp_l), jnp.stack(Cp_l), jnp.stack(np_l), jnp.stack(mp_l),
            jnp.stack(ks_l), jnp.stack(vs_l), jnp.stack(Cs_l), jnp.stack(ns_l), jnp.stack(ms_l))


_drawn_inputs = setup_inputs


def setup_inputs(seed=0):
    import zlib

    import numpy as np

    out = dict(_drawn_inputs(seed))
    spreads = {}
    factors = {'att_rel_bias': 7.175, 'norm2_g': 3.885, 'final_g': 2.943}
    for name, (base, spread) in spreads.items():
        noise = np.random.default_rng([zlib.crc32(name.encode()), seed]).standard_normal(out[name].shape)
        drawn = base * np.exp(spread * noise) if base else spread * noise
        out[name] = __import__('jax').numpy.asarray(drawn.astype(out[name].dtype))
    for name, factor in factors.items():
        out[name] = (out[name] * factor).astype(out[name].dtype)
    return out
```

```python
from contextlib import ExitStack

import concourse.bass as bass
from concourse import mybir
from concourse.bass import ds

ALU = mybir.AluOpType
ACT = mybir.ActivationFunctionType
F32 = mybir.dt.float32
U32 = mybir.dt.uint32
AX = mybir.AxisListType

P = 128
D = 1024
KD = D // P
S = 512
TS = 32
T = S + TS
HALF = T // 2
ROWS = [P, P, P, P, TS]
NT = len(ROWS)
AH, AD = 8, 64
MH = 4
BW = S + P
MAX_REL = 128
NEG = -1e30
LOWEST = -3.0e38
EPS = 1e-6
PH, NK, TOPK = 8, 128, 16
CHUNK = 64
ML_SCALE = float(P) ** -0.5
GRP = 32
NGRP = T // GRP
AQ, AK, AV, MQ, MK, MV, MO, GATES, GA, GB = 0, 512, 1024, 1536, 2048, 2560, 3072, 3584, 3592, 4616


class Shared:
    pass


def bcast(ap, axis, n):
    u = ap.unsqueeze(axis)
    shape = list(u.shape)
    shape[axis] = n
    return u.broadcast_to(shape)


def linker(eng, sem):
    count = [0]

    def link(ins):
        count[0] += 1
        ins.then_inc(sem, 1)
        eng.wait_ge(sem, count[0])
    return link


def program(nc, x_prompt, x_sample, cache_att_k, cache_att_v, state_mlstm_C, state_mlstm_n, state_mlstm_m,
            norm1_g, w_in, b_in, ml_f_bias, att_rel_bias, w_att_branch, w_ml_branch, w_out,
            norm2_g, peer_wq, peer_sub_keys, peer_u, peer_v, final_g,
            y_prompt, y_sample, att_k_prompt, att_v_prompt, C_prompt, n_prompt, m_prompt,
            att_k_sample, att_v_sample, C_sample, n_sample, m_sample):
    with ExitStack() as whole:
        def holder(stack):
            return lambda name, shape, dt=F32: stack.enter_context(nc.sbuf_tensor(name, shape, dt))

        keep = holder(whole)
        k = Shared()
        k.sem = lambda name: whole.enter_context(nc.semaphore(name))
        k.ps = whole.enter_context(nc.psum_tensor("ps", [P, 8, 512], F32))
        k.ident = keep("ident", [P, P])
        k.iota = keep("iota_row", [P, P])
        k.ones = keep("ones", [P, P])
        k.x = keep("x", [P, NT, D])
        k.ss = keep("ss", [P, 8])
        k.rstd = keep("rstd", [P, 8])
        k.line_dram = nc.dram_tensor("rel_line", (AH, P, BW + P), F32, kind="Internal").ap()
        k.route_dram = nc.dram_tensor("routing", (NGRP, P, P, GRP), F32, kind="Internal").ap()
        with ExitStack() as early:
            hold = holder(early)
            k.xnT = hold("xnT", [P, KD, T])
            k.aqT = hold("aqT", [P, 4, T])
            k.mqT = hold("mqT", [P, MH, T])
            with ExitStack() as now:
                project(nc, k, holder(now), x_prompt, x_sample, cache_att_k, cache_att_v, state_mlstm_C,
                        state_mlstm_n, state_mlstm_m, norm1_g, w_in, b_in, ml_f_bias, att_rel_bias,
                        att_k_prompt, att_v_prompt, C_prompt, n_prompt, m_prompt,
                        att_k_sample, att_v_sample, C_sample, n_sample, m_sample)
            with ExitStack() as now:
                merge(nc, k, holder(now), w_in, b_in, w_att_branch, w_ml_branch, w_out)
        k.xn2T = keep("xn2T", [P, KD, T])
        with ExitStack() as late:
            k.chosen = holder(late)("chosen", [P, 3, T])
            with ExitStack() as now:
                retrieve(nc, k, holder(now), norm2_g, peer_wq, peer_sub_keys)
            with ExitStack() as now:
                route(nc, k, holder(now))
        k.acc = keep("acc", [P, KD, T])
        with ExitStack() as now:
            experts(nc, k, holder(now), peer_u, peer_v)
        with ExitStack() as now:
            finish(nc, k, holder(now), final_g, y_prompt, y_sample)


def project(nc, k, hold, x_prompt, x_sample, cache_att_k, cache_att_v, state_mlstm_C, state_mlstm_n,
            state_mlstm_m, norm1_g, w_in, b_in, ml_f_bias, att_rel_bias,
            att_k_prompt, att_v_prompt, C_prompt, n_prompt, m_prompt,
            att_k_sample, att_v_sample, C_sample, n_sample, m_sample):
    ps, x, xnT, aqT, mqT, ident = k.ps, k.x, k.xnT, k.aqT, k.mqT, k.ident
    sem = k.sem
    akT = hold("akT", [P, 4, T])
    mkT = hold("mkT", [P, MH, T])
    ak_nat = hold("ak_nat", [P, NT, 512])
    av_nat = hold("av_nat", [P, NT, 512])
    mk_nat = hold("mk_nat", [P, NT, 512])
    mv_nat = hold("mv_nat", [P, NT, 512])
    kc_nat = ak_nat[:, 0:4, :]
    kcT = hold("kcT", [P, 4, S])
    w = hold("w", [P, 2, KD, 512])
    row = w[0:MH, 0, :, :].rearrange("p a b -> p (a b)")[:, 0:7 * T].rearrange("p (r t) -> p r t", r=7)
    vc = w[:, 1, 0:4, :]
    late = w[:, 1, 4:8, :].rearrange("p a b -> p (a b)")
    pT = late[:, 0:10 * P].rearrange("p (b s n) -> p b s n", b=2, s=5)
    em_bc = late[:, 10 * P:10 * P + S]
    w_gate = hold("w_gate", [P, KD, 8])
    bias = hold("bias", [P, AH, BW])
    xn = bias[:, :, :].rearrange("p h j -> p (h j)").rearrange("p (t d) -> p t d", t=NT)
    g1 = hold("g1", [P, KD])
    b_col = hold("b_col", [P, 28])
    b_av = hold("b_av", [P, 512])
    b_mv = hold("b_mv", [P, 512])
    table = hold("table", [P, 2, AH])
    flip = hold("flip", [P, P])
    line = hold("line", [AH, BW + P])
    heads = hold("heads", [MH, MH, P])
    small = hold("small", [MH, 8])
    c_col = hold("c_col", [P, NT, MH])
    work = hold("work", [P, 4, T])
    vw = hold("vw", [P, 2, P + 1])
    samp = hold("samp", [P, 4, TS])
    state = hold("state", [P, MH, P + 1])
    n_rep = hold("n_rep", [P, P])
    c_out = hold("c_out", [P, MH, P + 1])
    amax = hold("amax", [P, 4])
    asum = hold("asum", [P, 4])

    x_loaded, const_loaded, cache_loaded, tab_loaded = sem("x_loaded"), sem("const_loaded"), sem("cache_loaded"), sem("tab_loaded")
    w_loaded = [sem("w_loaded0"), sem("w_loaded1")]
    vc_loaded, wg_loaded, line_stored, bias_loaded, stored = sem("vc_loaded"), sem("wg_loaded"), sem("line_stored"), sem("bias_loaded"), sem("stored")
    pool_const, vec_const = sem("pool_const"), sem("vec_const")
    squared, rooted, vec_chain = sem("squared"), sem("rooted"), sem("vec_chain")
    normed, line_done = sem("normed"), sem("line_done")
    unit_done, vec_evicted, act_evicted = sem("unit_done"), sem("vec_evicted"), sem("act_evicted")
    gate_vec, gate_act = sem("gate_vec"), sem("gate_act")
    c_turned, c_copied = sem("c_turned"), sem("c_copied")
    ml_rows, ml_em, ml_qk, ml_gap, ml_w, ml_masked, ml_wqk, ml_vw = (sem(n) for n in (
        "ml_rows", "ml_em", "ml_qk", "ml_gap", "ml_w", "ml_masked", "ml_wqk", "ml_vw"))
    ml_used, ml_sample, ml_head = sem("ml_used"), sem("ml_sample"), sem("ml_head")
    at_scored, at_max, at_exp, at_norm, at_turned, at_copied, at_pv, at_out = (sem(n) for n in (
        "at_scored", "at_max", "at_exp", "at_norm", "at_turned", "at_copied", "at_pv", "at_out"))
    at_added = sem("at_added")
    bias_masked = sem("bias_masked")

    units = [("xn", (t, g), "vec") for t in range(NT) for g in range(2)]
    units += [("cache", s, "act") for s in range(4)]
    units += [("line", i, "act") for i in range(2)]
    chunks = [("mq", MQ, mqT, "act"), ("mk", MK, mkT, "vec"), ("mv", MV, mv_nat, "vec"),
              ("aq", AQ, aqT, "vec"), ("ak", AK, akT, "act"), ("av", AV, av_nat, "vec")]
    for c, (name, _, _, who) in enumerate(chunks):
        if name in ("mv", "av"):
            units += [(name, (c, t), who) for t in range(NT)]
        else:
            units += [(name, (c, m, h), who) for m in range(4) for h in range(2)]
    units += [("gate", (i, h), "act") for i in range(2) for h in range(2)]
    units += [("mk_turn", t, "act") for t in range(NT)] + [("ak_turn", t, "act") for t in range(NT)]
    BANKS = 4

    def evicted(u):
        who = units[u][2]
        return {"vec": vec_evicted, "act": act_evicted}[who], sum(v[2] == who for v in units[:u + 1])

    def last(name):
        return max(u for u, v in enumerate(units) if v[0] == name)

    DMAS_OUT = 4 + 6

    def wqk_of(q):
        return pT[:, q % 2, :, :].rearrange("p s n -> p (s n)")

    with nc.Block() as block:
        @block.sync
        def _(sp):
            sp.dma_start(x[:, 0:4, :], x_prompt[0].rearrange("(t p) d -> p t d", p=P)).then_inc(x_loaded, 16)
            sp.dma_start(x[0:TS, 4, :], x_sample[0]).then_inc(x_loaded, 16)
            sp.dma_start(g1[:, :], norm1_g[0].rearrange("(k p) -> p k", p=P)).then_inc(const_loaded, 16)
            sp.dma_start(kc_nat, cache_att_k[0, 0].rearrange("(s p) h d -> p s (h d)", p=P)).then_inc(cache_loaded, 16)
            sp.dma_start(table[:, 0, :], att_rel_bias[0, 1:P + 1, :]).then_inc(tab_loaded, 16)
            sp.dma_start(table[:, 1, :], att_rel_bias[0, P + 1:2 * P + 1, :]).then_inc(tab_loaded, 16)
            sp.dma_start(w_gate[:, :, :], w_in[0, :, GATES:GA].rearrange("(k p) n -> p k n", p=P)).then_inc(wg_loaded, 16)
            sp.dma_start(b_col[:, :], b_in[0, 0:GATES].rearrange("(m p) -> p m", p=P)).then_inc(const_loaded, 16)
            sp.dma_start(small[:, 0:2], b_in[0, GATES:GA].rearrange("(i h) -> h i", h=MH)).then_inc(const_loaded, 16)
            sp.dma_start(small[:, 2:3], ml_f_bias.rearrange("a h -> h a")).then_inc(const_loaded, 16)
            sp.dma_start(small[:, 3:4], state_mlstm_m[0].rearrange("a h -> h a")).then_inc(const_loaded, 16)
            sp.dma_start(b_av[:, :], b_in[0, AV:AV + 512].partition_broadcast(P)).then_inc(const_loaded, 16)
            sp.dma_start(b_mv[:, :], b_in[0, MV:MV + 512].partition_broadcast(P)).then_inc(const_loaded, 16)
            for c, (_, col, _, _) in enumerate(chunks):
                if c >= 2:
                    sp.wait_ge(unit_done, last(chunks[c - 2][0]) + 1)
                sp.dma_start(w[:, c % 2, :, :], w_in[0, :, col:col + 512].rearrange("(k p) n -> p k n", p=P)
                             ).then_inc(w_loaded[c % 2], 16)
                if c == 1:
                    sp.dma_start(state[:, :, 0:P], state_mlstm_C[0, 0].rearrange("h d e -> d h e")).then_inc(const_loaded, 16)
                    sp.dma_start(state[:, :, P], state_mlstm_n[0, 0].rearrange("h d -> d h")).then_inc(const_loaded, 16)
                    sp.wait_ge(line_done, 1)
                    sp.dma_start(k.line_dram, bcast(line[:, :], 1, P)).then_inc(line_stored, 16)
                    sp.wait_ge(line_stored, 16)
                    sp.wait_ge(unit_done, last("xn") + 1)
                    for h in range(AH):
                        sp.dma_start(bias[:, h, :], bass.AP(k.line_dram.tensor, h * P * (BW + P) + P, [[BW + P - 1, P], [1, BW]])
                                     ).then_inc(bias_loaded, 16)
            sp.wait_ge(unit_done, last("av") + 1)
            sp.dma_start(vc, cache_att_v[0, 0].rearrange("(s p) h d -> p s (h d)", p=P)).then_inc(vc_loaded, 16)
            n_done, n_val = evicted(last("ak_turn"))
            sp.wait_ge(n_done, n_val)
            sp.dma_start(att_k_prompt[0, 0].rearrange("(t p) h d -> p t (h d)", p=P), ak_nat[:, 0:4, :]).then_inc(stored, 16)
            sp.dma_start(att_k_sample[0, 0].rearrange("p h d -> p (h d)"), ak_nat[0:TS, 4, :]).then_inc(stored, 16)
            n_done, n_val = evicted(last("av"))
            sp.wait_ge(n_done, n_val)
            sp.dma_start(att_v_prompt[0, 0].rearrange("(t p) h d -> p t (h d)", p=P), av_nat[:, 0:4, :]).then_inc(stored, 16)
            sp.dma_start(att_v_sample[0, 0].rearrange("p h d -> p (h d)"), av_nat[0:TS, 4, :]).then_inc(stored, 16)
            sp.wait_ge(ml_head, 2 * MH)
            sp.dma_start(C_prompt[0, 0].rearrange("h d e -> d h e"), c_out[:, :, 0:P]).then_inc(stored, 16)
            sp.dma_start(n_prompt[0, 0].rearrange("h d -> d h"), c_out[:, :, P]).then_inc(stored, 16)
            sp.dma_start(m_prompt[0].rearrange("a h -> h a"), row[:, 4, S - 1:S]).then_inc(stored, 16)
            sp.dma_start(C_sample[0, 0].rearrange("h d e -> d h e"), state[:, :, 0:P]).then_inc(stored, 16)
            sp.dma_start(n_sample[0, 0].rearrange("h d -> d h"), state[:, :, P]).then_inc(stored, 16)
            sp.dma_start(m_sample[0].rearrange("a h -> h a"), row[:, 4, T - 1:T]).then_inc(stored, 16)
            sp.wait_ge(stored, 16 * DMAS_OUT)

        @block.gpsimd
        def _(pool):
            nc.gpsimd.memset(ident[:, :], 0.0).then_inc(pool_const, 1)
            nc.gpsimd.memset(flip[:, :], 0.0).then_inc(pool_const, 1)
            nc.gpsimd.memset(heads[:, :, :], 0.0).then_inc(pool_const, 1)
            pool.wait_ge(pool_const, 3)
            nc.gpsimd.affine_select(out=ident[:, :], in_=ident[:, :], compare_op=ALU.not_equal, fill=1.0, base=0,
                                    pattern=[[-1, P]], channel_multiplier=1).then_inc(pool_const, 1)
            nc.gpsimd.affine_select(out=flip[:, :], in_=flip[:, :], compare_op=ALU.not_equal, fill=1.0, base=1 - P,
                                    pattern=[[1, P]], channel_multiplier=1).then_inc(pool_const, 1)
            nc.gpsimd.affine_select(out=heads[:, :, :], in_=heads[:, :, :], compare_op=ALU.not_equal, fill=1.0, base=0,
                                    pattern=[[-1, MH], [0, P]], channel_multiplier=1).then_inc(pool_const, 1)
            nc.gpsimd.iota(k.iota[:, :], pattern=[[1, P]], base=0, channel_multiplier=0,
                           allow_small_or_imprecise_dtypes=True).then_inc(pool_const, 1)
            q = 0
            for h in range(MH):
                for s in range(NT):
                    n = ROWS[s]
                    lo = P * s if s < 4 else 0
                    pool.wait_ge(ml_w, q + 1)
                    diag = work[0:n, q % 2, lo:lo + n]
                    nc.gpsimd.affine_select(out=diag, in_=diag, compare_op=ALU.is_ge, fill=0.0, base=0,
                                            pattern=[[1, n]], channel_multiplier=-1).then_inc(ml_masked, 1)
                    q += 1

        @block.scalar
        def _(act):
            act.wait_ge(x_loaded, 32)
            act.wait_ge(vec_const, 2)
            for t in range(NT):
                r = ROWS[t]
                nc.scalar.activation(xn[0:r, t, :], x[0:r, t, :], ACT.Square, accum_out=k.ss[0:r, t:t + 1]).then_inc(squared, 1)
            act.wait_ge(vec_chain, 1)
            nc.scalar.activation(k.ss[:, 0:NT], k.rstd[:, 0:NT], ACT.Sqrt).then_inc(rooted, 1)
            act.wait_ge(const_loaded, 144)
            act.wait_ge(cache_loaded, 16)
            for u, (kind, arg, who) in enumerate(units):
                if who != "act":
                    continue
                act.wait_ge(unit_done, u + 1)
                b = u % BANKS
                if kind == "cache":
                    ins = nc.scalar.copy(kcT[:, :, arg * P:(arg + 1) * P], ps[:, b, :].rearrange("p (g n) -> p g n", g=4))
                elif kind == "line":
                    at = BW - P * arg
                    ins = nc.scalar.copy(line[:, at:at + P], ps[0:AH, b, 0:P])
                elif kind == "gate":
                    i, h = arg
                    ins = nc.scalar.activation(row[:, i, h * HALF:(h + 1) * HALF], ps[0:MH, b, 0:HALF], ACT.Identity,
                                               bias=small[:, i:i + 1])
                elif kind in ("mk_turn", "ak_turn"):
                    if kind == "ak_turn" and arg == 0:
                        ev, n = evicted(last("cache"))
                        act.wait_ge(ev, n)
                    r = ROWS[arg]
                    dst = mk_nat if kind == "mk_turn" else ak_nat
                    ins = nc.scalar.copy(dst[0:r, arg, :], ps[0:r, b, :])
                else:
                    c, m, h = arg
                    col = chunks[c][1] // P + m
                    ins = nc.scalar.activation(chunks[c][2][:, m, h * HALF:(h + 1) * HALF], ps[:, b, 0:HALF], ACT.Identity,
                                               bias=b_col[:, col:col + 1])
                ins.then_inc(act_evicted, 1)
            act.wait_ge(gate_vec, 1)
            nc.scalar.activation(row[:, 3, :], row[:, 2, :], ACT.Exp, scale=-1.0).then_inc(gate_act, 1)
            act.wait_ge(gate_vec, 2)
            nc.scalar.activation(row[:, 3, :], row[:, 2, :], ACT.Ln).then_inc(gate_act, 1)
            act.wait_ge(gate_vec, 3)
            nc.scalar.activation(row[:, 6, :], row[:, 4, :], ACT.Exp, scale=-1.0).then_inc(gate_act, 1)
            nc.scalar.activation(row[:, 0, S:T], row[:, 2, S:T], ACT.Exp, scale=-1.0).then_inc(gate_act, 1)
            q = 0
            for h in range(MH):
                act.wait_ge(ml_rows, h + 1)
                if h >= 1:
                    act.wait_ge(ml_head, 2 * h)
                nc.scalar.copy(em_bc[:, :], ps[:, 2, :]).then_inc(ml_em, 1)
                nc.scalar.copy(samp[:, 0:2, :], ps[:, 1, TS:3 * TS].rearrange("p (a n) -> p a n", a=2)).then_inc(ml_em, 1)
                for s in range(NT):
                    n = ROWS[s]
                    lo, hi = (P * s, S) if s < 4 else (0, TS)
                    act.wait_ge(ml_gap, q + 1)
                    if q >= 2:
                        act.wait_ge(ml_wqk, q - 1)
                        act.wait_ge(ml_vw, q - 1)
                    nc.scalar.activation(work[0:n, q % 2, lo:hi], work[0:n, 2 + q % 2, lo:hi], ACT.Exp, scale=-1.0).then_inc(ml_w, 1)
                    q += 1
            def exp_scores(u):
                h, t = divmod(u, NT)
                r, n = ROWS[t], (t + 1) * P if t < 4 else T
                act.wait_ge(at_max, u + 1)
                if u >= 2:
                    act.wait_ge(at_turned, u - 1)
                nc.scalar.activation(work[0:r, u % 2, 0:n], work[0:r, 2 + u % 2, 0:n], ACT.Exp, bias=amax[0:r, u % 2:u % 2 + 1],
                                     accum_out=asum[0:r, u % 2:u % 2 + 1]).then_inc(at_exp, 1)

            def copy_turned(u):
                h, t = divmod(u, NT)
                act.wait_ge(at_turned, u + 1)
                if u >= 2:
                    act.wait_ge(at_pv, u - 1)
                if t < 4:
                    nc.scalar.copy(pT[:, u % 2, 0:t + 1, :], ps[:, 6, 0:(t + 1) * P].rearrange("p (s n) -> p s n", n=P)).then_inc(at_copied, 1)
                else:
                    nc.scalar.copy(pT[:, u % 2, 0:4, 0:TS], ps[:, 6, 0:4 * TS].rearrange("p (s n) -> p s n", n=TS))
                    nc.scalar.copy(pT[0:TS, u % 2, 4, 0:TS], ps[0:TS, 6, 4 * TS:5 * TS]).then_inc(at_copied, 1)
            for u in range(AH * NT + 1):
                if u < AH * NT:
                    exp_scores(u)
                if u >= 1:
                    copy_turned(u - 1)

        @block.vector
        def _(dve):
            nc.vector.memset(k.ones[:, :], 1.0).then_inc(vec_const, 1)
            nc.vector.memset(k.ss[:, :], 1.0).then_inc(vec_const, 1)
            dve.wait_ge(squared, NT)
            link = linker(dve, vec_chain)
            link(nc.vector.tensor_scalar(k.rstd[:, 0:NT], k.ss[:, 0:NT], 1.0 / D, EPS, ALU.mult, ALU.add))
            dve.wait_ge(rooted, 1)
            link(nc.vector.reciprocal(k.rstd[:, 0:NT], k.ss[:, 0:NT]))
            for t in range(NT):
                r = ROWS[t]
                nc.vector.tensor_scalar(xn[0:r, t, :], x[0:r, t, :], k.rstd[0:r, t:t + 1], None, ALU.mult).then_inc(normed, 1)
            dve.wait_ge(const_loaded, 144)
            for u, (kind, arg, who) in enumerate(units):
                if kind == "mk" and arg == (1, 0, 0):
                    ev, n = evicted(last("line"))
                    dve.wait_ge(ev, n)
                    nc.vector.tensor_scalar(line[:, 0:S].rearrange("p (a b) -> p a b", b=P), bcast(k.ones[0:AH, :], 1, S // P),
                                            line[:, S:S + 1], None, ALU.mult).then_inc(line_done, 1)
                if who != "vec":
                    continue
                dve.wait_ge(unit_done, u + 1)
                b = u % BANKS
                if kind == "xn":
                    t, g = arg
                    r = ROWS[t]
                    ins = nc.vector.tensor_tensor(xnT[:, 4 * g:4 * g + 4, t * P:t * P + r],
                                                  ps[:, b, :].rearrange("p (g n) -> p g n", g=4)[:, :, 0:r],
                                                  bcast(g1[:, 4 * g:4 * g + 4], 2, r), ALU.mult)
                elif kind in ("mv", "av"):
                    c, t = arg
                    r = ROWS[t]
                    ins = nc.vector.tensor_tensor(chunks[c][2][0:r, t, :], ps[0:r, b, :], (b_mv if kind == "mv" else b_av)[0:r, :], ALU.add)
                else:
                    c, m, h = arg
                    col = chunks[c][1] // P + m
                    ins = nc.vector.tensor_scalar(chunks[c][2][:, m, h * HALF:(h + 1) * HALF], ps[:, b, 0:HALF],
                                                  b_col[:, col:col + 1], ML_SCALE if kind == "mk" else AD ** -0.5, ALU.add, ALU.mult)
                ins.then_inc(vec_evicted, 1)
            ev, n = evicted(last("gate"))
            dve.wait_ge(ev, n)
            link(nc.vector.tensor_scalar(row[:, 1, :], row[:, 1, :], small[:, 2:3], None, ALU.add))
            link(nc.vector.tensor_scalar(row[:, 4, :], row[:, 1, :], -1.0, None, ALU.mult))
            nc.vector.tensor_tensor(row[:, 2, :], row[:, 1, :], row[:, 4, :], ALU.max).then_inc(gate_vec, 1)
            dve.wait_ge(gate_act, 1)
            nc.vector.tensor_scalar(row[:, 2, :], row[:, 3, :], 1.0, None, ALU.add).then_inc(gate_vec, 1)
            dve.wait_ge(gate_act, 2)
            link(nc.vector.scalar_tensor_tensor(out=row[:, 2, :], in0=row[:, 1, :], scalar=0.0, in1=row[:, 3, :], op0=ALU.min, op1=ALU.subtract))
            link(nc.vector.memset(row[:, 5, :], 1.0))
            for lo, hi in ((0, S), (S, T)):
                link(nc.vector.tensor_tensor_scan(row[:, 3, lo:hi], row[:, 5, lo:hi], row[:, 2, lo:hi], 0.0, ALU.mult, ALU.add))
            link(nc.vector.tensor_tensor(row[:, 1, :], row[:, 0, :], row[:, 3, :], ALU.subtract))
            for lo, hi, first in ((0, S, NEG), (S, T, small[:, 3:4])):
                link(nc.vector.tensor_tensor_scan(row[:, 5, lo:hi], row[:, 1, lo:hi], row[:, 1, lo:hi], first, ALU.max, ALU.max))
            link(nc.vector.tensor_tensor(row[:, 4, :], row[:, 3, :], row[:, 5, :], ALU.add))
            nc.vector.tensor_scalar(row[:, 2, S:T], row[:, 5, S:T], small[:, 3:4], None, ALU.subtract).then_inc(gate_vec, 1)
            dve.wait_ge(c_turned, 1)
            nc.vector.tensor_copy(c_col[:, 0:4, :], ps[:, 7, 0:16].rearrange("p (t h) -> p t h", h=MH)).then_inc(c_copied, 1)
            nc.vector.tensor_copy(c_col[0:TS, 4, :], ps[0:TS, 7, 16:20]).then_inc(c_copied, 1)
            dve.wait_ge(c_copied, 2)

            def gap(q):
                h, s = divmod(q, NT)
                n = ROWS[s]
                lo, hi = (P * s, S) if s < 4 else (0, TS)
                if s == 0:
                    dve.wait_ge(ml_rows, h + 1)
                if q >= 2:
                    dve.wait_ge(ml_w, q - 1)
                nc.vector.tensor_scalar(work[0:n, 2 + q % 2, lo:hi], ps[0:n, 0 if s < 4 else 1, lo:hi], c_col[0:n, s, h:h + 1], 0.0,
                                        ALU.subtract, ALU.max).then_inc(ml_gap, 1)

            def weigh(q):
                h, s = divmod(q, NT)
                n = ROWS[s]
                lo, hi = (P * s, S) if s < 4 else (0, TS)
                dve.wait_ge(ml_masked, q + 1)
                dve.wait_ge(ml_qk, q + 1)
                if q >= 2:
                    dve.wait_ge(ml_used, q - 1)
                end = work[0:n, q % 2, hi - 1:hi]
                nc.vector.tensor_scalar(vw[0:n, q % 2, 0:P], mv_nat[0:n, s, h * P:(h + 1) * P], end, None, ALU.mult)
                nc.vector.tensor_copy(vw[0:n, q % 2, P:P + 1], end).then_inc(ml_vw, 1)
                nc.vector.tensor_tensor(wqk_of(q)[0:n, lo:hi], work[0:n, q % 2, lo:hi], ps[0:n, 3 + q % 2, lo:hi], ALU.mult).then_inc(ml_wqk, 1)

            for h in range(MH):
                dve.wait_ge(ml_em, 2 * h + 2)
                dve.wait_ge(ml_qk, NT * h + 1)
                link(nc.vector.tensor_tensor(samp[:, 2, :], mqT[:, h, S:T], samp[:, 0, :], ALU.mult))
                nc.vector.tensor_scalar(n_rep[:, :], k.ones[:, :], state[:, h, P:P + 1], None, ALU.mult).then_inc(ml_sample, 1)
                gap(NT * h)
                for s in range(NT):
                    if s + 1 < NT:
                        gap(NT * h + s + 1)
                    weigh(NT * h + s)
                dve.wait_ge(ml_used, NT * h + 4)
                link(nc.vector.scalar_tensor_tensor(out=em_bc[:, :], in0=ps[:, 6, :], scalar=-1.0, in1=em_bc[:, :], op0=ALU.mult, op1=ALU.max))
                link(nc.vector.tensor_tensor(em_bc[:, :], ps[:, 6, :], em_bc[:, :], ALU.max))
                link(nc.vector.reciprocal(em_bc[:, :], em_bc[:, :]))
                nc.vector.tensor_tensor(mqT[:, h, 0:S], ps[:, 5, :], em_bc[:, :], ALU.mult)
                nc.vector.tensor_copy(c_out[:, h, :], ps[:, 7, 0:P + 1]).then_inc(ml_head, 1)
                dve.wait_ge(ml_used, NT * h + 5)
                link(nc.vector.scalar_tensor_tensor(out=samp[:, 1, :], in0=ps[:, 2, TS:2 * TS], scalar=-1.0, in1=samp[:, 1, :], op0=ALU.mult, op1=ALU.max))
                link(nc.vector.tensor_tensor(samp[:, 1, :], ps[:, 2, TS:2 * TS], samp[:, 1, :], ALU.max))
                link(nc.vector.reciprocal(samp[:, 1, :], samp[:, 1, :]))
                nc.vector.tensor_tensor(mqT[:, h, S:T], ps[:, 2, 0:TS], samp[:, 1, :], ALU.mult)
                nc.vector.scalar_tensor_tensor(out=state[:, h, :], in0=state[:, h, :], scalar=samp[:, 0, TS - 1:TS], in1=ps[:, 2, 128:129 + P],
                                               op0=ALU.mult, op1=ALU.add).then_inc(ml_head, 1)
            dve.wait_ge(bias_loaded, 16 * AH)
            nc.vector.memset(bias[0:CHUNK, :, BW - CHUNK:BW], NEG).then_inc(bias_masked, 1)
            dve.wait_ge(bias_masked, 1)

            def add_bias(u):
                h, t = divmod(u, NT)
                r, n = ROWS[t], (t + 1) * P if t < 4 else S
                off = BW - n if t < 4 else 0
                dve.wait_ge(at_scored, u + 1)
                if u >= 2:
                    dve.wait_ge(at_exp, u - 1)
                sc = work[0:r, 2 + u % 2, :]
                ins = nc.vector.tensor_tensor(sc[:, 0:n], ps[0:r, 4 + u % 2, 0:n], bias[0:r, h, off:off + n], ALU.add)
                n_inc = 1
                if t == 4:
                    ins.then_inc(at_added, 1)
                    ins = nc.vector.tensor_tensor(sc[:, S:T], ps[0:TS, 3, 0:TS], bias[0:TS, h, S:T], ALU.add)
                ins.then_inc(at_added, 1)
                dve.wait_ge(at_added, u + 1 + sum(1 for v in range(u + 1) if v % NT == 4))
                nc.vector.tensor_reduce(amax[0:r, u % 2:u % 2 + 1], sc[:, 0:n if t < 4 else T], AX.X, ALU.max, negate=True).then_inc(at_max, 1)

            def normalise(u):
                h, t = divmod(u, NT)
                r, n = ROWS[t], (t + 1) * P if t < 4 else T
                dve.wait_ge(at_exp, u + 1)
                link(nc.vector.reciprocal(asum[0:r, 2 + u % 2:3 + u % 2], asum[0:r, u % 2:u % 2 + 1]))
                nc.vector.tensor_scalar(work[0:r, u % 2, 0:n], work[0:r, u % 2, 0:n], asum[0:r, 2 + u % 2:3 + u % 2], None, ALU.mult).then_inc(at_norm, 1)

            def take_out(u):
                h, t = divmod(u, NT)
                r, lo = ROWS[t], AD * (h % 2)
                dve.wait_ge(at_pv, u + 1)
                nc.vector.tensor_copy(aqT[lo:lo + AD, h // 2, t * P:t * P + r], ps[lo:lo + AD, 7, 0:r]).then_inc(at_out, 1)
            for u in range(AH * NT + 2):
                if u < AH * NT:
                    add_bias(u)
                if 1 <= u <= AH * NT:
                    normalise(u - 1)
                if u >= 2:
                    take_out(u - 2)

        @block.tensor
        def _(pe):
            pe.wait_ge(pool_const, 7)
            pe.wait_ge(tab_loaded, 32)
            pe.wait_ge(cache_loaded, 16)
            pe.wait_ge(wg_loaded, 16)
            pe.wait_ge(vec_const, 2)
            for u, (kind, arg, who) in enumerate(units):
                if u >= BANKS:
                    pe.wait_ge(*evicted(u - BANKS))
                b = u % BANKS
                if kind == "xn":
                    t, g = arg
                    r = ROWS[t]
                    pe.wait_ge(normed, t + 1)
                    for i in range(4):
                        kk = 4 * g + i
                        ins = nc.tensor.transpose(ps[:, b, i * P:i * P + r], xn[0:r, t, kk * P:(kk + 1) * P], ident[0:r, 0:r])
                elif kind == "cache":
                    for i in range(4):
                        ins = nc.tensor.transpose(ps[:, b, i * P:(i + 1) * P], kc_nat[:, arg, i * P:(i + 1) * P], ident[:, :])
                elif kind == "line":
                    ins = nc.tensor.matmul(ps[0:AH, b, 0:P], table[:, arg, :], flip[:, :], start=True, stop=True)
                elif kind == "gate":
                    i, h = arg
                    for kk in range(KD):
                        ins = nc.tensor.matmul(ps[0:MH, b, 0:HALF], w_gate[:, kk, i * MH:(i + 1) * MH], xnT[:, kk, h * HALF:(h + 1) * HALF],
                                               start=(kk == 0), stop=(kk == KD - 1))
                elif kind in ("mk_turn", "ak_turn"):
                    src = mkT if kind == "mk_turn" else akT
                    r = ROWS[arg]
                    if arg == 0:
                        pe.wait_ge(*evicted(last(kind[:2])))
                    for i in range(4):
                        ins = nc.tensor.transpose(ps[0:r, b, i * P:(i + 1) * P], src[:, i, arg * P:arg * P + r], ident[:, :])
                else:
                    c = arg[0]
                    if c == 0:
                        pe.wait_ge(*evicted(last("xn")))
                    pe.wait_ge(w_loaded[c % 2], 16 * (c // 2 + 1))
                    if kind in ("mv", "av"):
                        r = ROWS[arg[1]]
                        for kk in range(KD):
                            ins = nc.tensor.matmul(ps[0:r, b, :], xnT[:, kk, arg[1] * P:arg[1] * P + r], w[:, c % 2, kk, :],
                                                   start=(kk == 0), stop=(kk == KD - 1))
                    else:
                        _, m, h = arg
                        for kk in range(KD):
                            ins = nc.tensor.matmul(ps[:, b, 0:HALF], w[:, c % 2, kk, m * P:(m + 1) * P], xnT[:, kk, h * HALF:(h + 1) * HALF],
                                                   start=(kk == 0), stop=(kk == KD - 1))
                ins.then_inc(unit_done, 1)
            for u in range(len(units) - BANKS, len(units)):
                pe.wait_ge(*evicted(u))
            pe.wait_ge(gate_vec, 3)
            for t in range(NT):
                r = ROWS[t]
                ins = nc.tensor.transpose(ps[0:r, 7, t * MH:(t + 1) * MH], row[:, 1, t * P:t * P + r], ident[0:MH, 0:MH])
            ins.then_inc(c_turned, 1)
            pe.wait_ge(gate_act, 4)

            def scores(q):
                h, s = divmod(q, NT)
                n = ROWS[s]
                lo, hi = (P * s, S) if s < 4 else (0, TS)
                if q >= 2:
                    pe.wait_ge(ml_wqk, q - 1)
                nc.tensor.matmul(ps[0:n, 3 + q % 2, lo:hi], mkT[:, h, s * P:s * P + n], mqT[:, h, (s * P if s < 4 else S):(S if s < 4 else T)],
                                 start=True, stop=True).then_inc(ml_qk, 1)
            for h in range(MH):
                if h == 0:
                    pe.wait_ge(c_copied, 2)
                else:
                    pe.wait_ge(ml_head, 2 * h)
                nc.tensor.matmul(ps[:, 0, :], heads[:, h, :], row[:, 5, 0:S], start=True, stop=True)
                for i, r in enumerate((5, 0, 6)):
                    nc.tensor.matmul(ps[:, 1, i * TS:(i + 1) * TS], heads[:, h, :], row[:, r, S:T], start=True, stop=True)
                nc.tensor.matmul(ps[:, 2, :], heads[:, h, :], row[:, 6, 0:S], start=True, stop=True).then_inc(ml_rows, 1)
                scores(NT * h)
                for s in range(NT):
                    q = NT * h + s
                    n = ROWS[s]
                    if s + 1 < NT:
                        scores(q + 1)
                    pe.wait_ge(ml_wqk, q + 1)
                    pe.wait_ge(ml_vw, q + 1)
                    wqk = wqk_of(q)
                    vh = mv_nat[0:n, s, h * P:(h + 1) * P]
                    kh = mk_nat[0:n, s, h * P:(h + 1) * P]
                    if s < 4:
                        nc.tensor.matmul(ps[:, 5, s * P:S], vh, wqk[:, s * P:S], start=(s == 0), stop=(s == 3))
                        nc.tensor.matmul(ps[:, 6, s * P:S], k.ones[:, :], wqk[:, s * P:S], start=(s == 0), stop=(s == 3))
                        nc.tensor.matmul(ps[:, 7, 0:P + 1], kh, vw[:, q % 2, :], start=(s == 0), stop=(s == 3)).then_inc(ml_used, 1)
                    else:
                        pe.wait_ge(ml_sample, h + 1)
                        pe.wait_ge(ml_em, 2 * h + 2)
                        nc.tensor.matmul(ps[:, 2, 0:TS], vh, wqk[0:n, 0:TS], start=True, stop=False)
                        nc.tensor.matmul(ps[:, 2, 0:TS], state[:, h, 0:P], samp[:, 2, :], start=False, stop=True)
                        nc.tensor.matmul(ps[:, 2, TS:2 * TS], k.ones[0:n, :], wqk[0:n, 0:TS], start=True, stop=False)
                        nc.tensor.matmul(ps[:, 2, TS:2 * TS], n_rep[:, :], samp[:, 2, :], start=False, stop=True)
                        nc.tensor.matmul(ps[:, 2, P:2 * P + 1], kh, vw[0:n, q % 2, :], start=True, stop=True).then_inc(ml_used, 1)
            pe.wait_ge(ml_head, 2 * MH)

            def att_scores(u):
                h, t = divmod(u, NT)
                r, n, lo = ROWS[t], (t + 1) * P, AD * (h % 2)
                if u >= 2:
                    pe.wait_ge(at_max, u - 1)
                qh = aqT[lo:lo + AD, h // 2, t * P:t * P + r]
                if t < 4:
                    nc.tensor.matmul(ps[0:r, 4 + u % 2, 0:n], qh, akT[lo:lo + AD, h // 2, 0:n], start=True, stop=True).then_inc(at_scored, 1)
                else:
                    nc.tensor.matmul(ps[0:r, 4 + u % 2, 0:S], qh, kcT[lo:lo + AD, h // 2, :], start=True, stop=True)
                    nc.tensor.matmul(ps[0:r, 3, 0:TS], qh, akT[lo:lo + AD, h // 2, S:T], start=True, stop=True).then_inc(at_scored, 1)

            def turn(u):
                h, t = divmod(u, NT)
                r = ROWS[t]
                pe.wait_ge(at_norm, u + 1)
                if u >= 1:
                    pe.wait_ge(at_copied, u)
                for s in range(t + 1):
                    n = ROWS[s]
                    ins = nc.tensor.transpose(ps[0:n, 6, s * r:(s + 1) * r], work[0:r, u % 2, s * P:s * P + n], ident[0:r, 0:r])
                ins.then_inc(at_turned, 1)

            def weigh_values(u):
                h, t = divmod(u, NT)
                r, lo = ROWS[t], AD * (h % 2)
                if t == 4:
                    pe.wait_ge(vc_loaded, 16)
                pe.wait_ge(at_copied, u + 1)
                if u >= 1:
                    pe.wait_ge(at_out, u)
                for s in range(t + 1):
                    n = ROWS[s]
                    v = (av_nat if t < 4 or s == 4 else vc)[0:n, s, h * AD:(h + 1) * AD]
                    ins = nc.tensor.matmul(ps[lo:lo + AD, 7, 0:r], v, pT[0:n, u % 2, s, 0:r], start=(s == 0), stop=(s == t))
                ins.then_inc(at_pv, 1)
            for u in range(AH * NT + 2):
                if u < AH * NT:
                    att_scores(u)
                if 1 <= u <= AH * NT:
                    turn(u - 1)
                if u >= 2:
                    weigh_values(u - 2)




def merge(nc, k, hold, w_in, b_in, w_att_branch, w_ml_branch, w_out):
    ps, x, xnT, aqT, mqT = k.ps, k.x, k.xnT, k.aqT, k.mqT
    sem = k.sem
    RING = 4
    w = hold("w2", [P, RING, KD, 512])
    w_att = hold("w_att", [P, 4, D])
    w_ml = hold("w_ml", [P, 4, D])
    b_mo = hold("b_mo", [P, 4])
    b_gates = hold("b_gates", [P, 16])
    sig = hold("sig", [P, 4, 512])
    merged = hold("merged", [P, KD, T])
    w_loaded = [sem(f"merge_w_loaded{i}") for i in range(RING)]
    b_loaded, branch_loaded = sem("merge_b_loaded"), sem("branch_loaded")
    mo_done, mo_sig, mo_used = sem("mo_done"), sem("mo_sig"), sem("mo_used")
    g_done, g_sig, a_done, a_used, summed = sem("g_done"), sem("g_sig"), sem("a_done"), sem("a_used"), sem("summed")
    out_done, out_added = sem("out_done"), sem("out_added")
    chunks = [w_in[0, :, c:c + 512] for c in (MO, GA, GB, GA + 512, GB + 512)] + [w_out[0, :, 0:512], w_out[0, :, 512:1024]]
    with nc.Block() as block:
        @block.sync
        def _(sp):
            for c in range(len(chunks)):
                if c == 1:
                    sp.dma_start(b_mo[:, :], b_in[0, MO:GATES].rearrange("(m p) -> p m", p=P)).then_inc(b_loaded, 16)
                    sp.dma_start(b_gates[:, :], b_in[0, GA:GA + 2 * D].rearrange("(m p) -> p m", p=P)).then_inc(b_loaded, 16)
                    sp.dma_start(w_att[:, :, :], w_att_branch[0].rearrange("(k p) n -> p k n", p=P)).then_inc(branch_loaded, 16)
                    sp.dma_start(w_ml[:, :, :], w_ml_branch[0].rearrange("(k p) n -> p k n", p=P)).then_inc(branch_loaded, 16)
                if c == 4:
                    sp.wait_ge(mo_done, 8)
                if c in (5, 6):
                    sp.wait_ge(a_done, 2 * 4 * 2)
                sp.dma_start(w[:, c % RING, :, :], chunks[c].rearrange("(k p) n -> p k n", p=P)).then_inc(w_loaded[c % RING], 16)

        @block.tensor
        def _(pe):
            pe.wait_ge(w_loaded[0], 16)
            for u in range(8):
                m, h = divmod(u, 2)
                if u >= 4:
                    pe.wait_ge(mo_sig, u - 3)
                for kk in range(KD):
                    ins = nc.tensor.matmul(ps[:, u % 4, 0:HALF], w[:, 0, kk, m * P:(m + 1) * P], xnT[:, kk, h * HALF:(h + 1) * HALF],
                                           start=(kk == 0), stop=(kk == KD - 1))
                ins.then_inc(mo_done, 1)
            pe.wait_ge(mo_sig, 8)
            pe.wait_ge(branch_loaded, 32)
            for u in range(16):
                j, h = divmod(u, 2)
                cols = slice(h * HALF, (h + 1) * HALF)
                for g in range(2):
                    c = 1 + g + 2 * (j // 4)
                    if j % 4 == 0 and h == 0:
                        pe.wait_ge(w_loaded[c % RING], 16 * (c // RING + 1))
                    if u >= 1:
                        pe.wait_ge(g_sig, 2 * (u - 1) + g + 1)
                    for kk in range(KD):
                        ins = nc.tensor.matmul(ps[:, g, 0:HALF], w[:, c % RING, kk, (j % 4) * P:(j % 4 + 1) * P], xnT[:, kk, cols],
                                               start=(kk == 0), stop=(kk == KD - 1))
                    ins.then_inc(g_done, 1)
                if u == 0:
                    pe.wait_ge(mo_used, 8)
                for g, (wb, src) in enumerate(((w_att, aqT), (w_ml, mqT))):
                    if u >= 2:
                        pe.wait_ge(a_used, 2 * (u - 2) + g + 1)
                    for kk in range(4):
                        ins = nc.tensor.matmul(ps[:, 4 + 2 * (u % 2) + g, 0:HALF], wb[:, kk, j * P:(j + 1) * P], src[:, kk, cols],
                                               start=(kk == 0), stop=(kk == 3))
                    ins.then_inc(a_done, 1)
            pe.wait_ge(summed, 16)
            for c in (5, 6):
                pe.wait_ge(w_loaded[c % RING], 16 * (c // RING + 1))
            for u in range(2 * NT):
                t, h = divmod(u, 2)
                r = ROWS[t]
                if u >= 4:
                    pe.wait_ge(out_added, u - 3)
                for kk in range(KD):
                    ins = nc.tensor.matmul(ps[0:r, u % 4, :], merged[:, kk, t * P:t * P + r], w[:, (5 + h) % RING, kk, :],
                                           start=(kk == 0), stop=(kk == KD - 1))
                ins.then_inc(out_done, 1)

        @block.scalar
        def _(act):
            act.wait_ge(b_loaded, 32)
            for u in range(8):
                m, h = divmod(u, 2)
                act.wait_ge(mo_done, u + 1)
                if u >= 4:
                    act.wait_ge(mo_used, u - 3)
                nc.scalar.activation(sig[:, u % 4, 0:HALF], ps[:, u % 4, 0:HALF], ACT.Sigmoid, bias=b_mo[:, m:m + 1]).then_inc(mo_sig, 1)
            act.wait_ge(mo_used, 8)
            for u in range(16):
                j = u // 2
                for g in range(2):
                    act.wait_ge(g_done, 2 * u + g + 1)
                    if u >= 2:
                        act.wait_ge(summed, u - 1)
                    nc.scalar.activation(sig[:, 2 * (u % 2) + g, 0:HALF], ps[:, g, 0:HALF], ACT.Sigmoid,
                                         bias=b_gates[:, 8 * g + j:8 * g + j + 1]).then_inc(g_sig, 1)

        @block.vector
        def _(dve):
            for u in range(8):
                m, h = divmod(u, 2)
                dve.wait_ge(mo_sig, u + 1)
                hT = mqT[:, m, h * HALF:(h + 1) * HALF]
                nc.vector.tensor_tensor(hT, hT, sig[:, u % 4, 0:HALF], ALU.mult).then_inc(mo_used, 1)
            for u in range(16):
                for g in range(2):
                    dve.wait_ge(g_sig, 2 * u + g + 1)
                    dve.wait_ge(a_done, 2 * u + g + 1)
                    gate = sig[:, 2 * (u % 2) + g, 0:HALF]
                    nc.vector.tensor_tensor(sig[:, 2 * (u % 2) + g, 0:HALF], ps[:, 4 + 2 * (u % 2) + g, 0:HALF], gate, ALU.mult).then_inc(a_used, 1)
                dve.wait_ge(a_used, 2 * u + 2)
                j, h = divmod(u, 2)
                nc.vector.tensor_tensor(merged[:, j, h * HALF:(h + 1) * HALF], sig[:, 2 * (u % 2), 0:HALF], sig[:, 2 * (u % 2) + 1, 0:HALF],
                                        ALU.add).then_inc(summed, 1)
            for u in range(2 * NT):
                t, h = divmod(u, 2)
                r = ROWS[t]
                dve.wait_ge(out_done, u + 1)
                xs = x[0:r, t, h * 512:(h + 1) * 512]
                nc.vector.tensor_tensor(xs, ps[0:r, u % 4, :], xs, ALU.add).then_inc(out_added, 1)


def retrieve(nc, k, hold, norm2_g, peer_wq, peer_sub_keys):
    ps, x, xn2T, ident, chosen = k.ps, k.x, k.xn2T, k.ident, k.chosen
    sem = k.sem
    w = hold("wq", [P, 2, KD, 512])
    g2 = hold("g2", [P, KD])
    xn = hold("xn_b", [P, NT, D])
    sk = hold("sk", [P, PH, P])
    skT = hold("skT", [P, PH, NK])
    qT = hold("qT", [P, PH, T])
    sc = hold("sc", [P, 2, 2, PH, NK])
    rest = hold("rest", [P, 2, PH, NK])
    sv = hold("sv", [P, 2, PH, TOPK])
    si = hold("si", [P, 2, PH, TOPK], U32)
    sif = hold("sif", [P, 2, PH, TOPK])
    fv = hold("fv", [P, PH, TOPK])
    fi = hold("fi", [P, PH, TOPK], U32)
    pos = hold("pos", [P, 2, PH, TOPK], U32)
    posf = hold("posf", [P, 2, PH, TOPK])
    one_hot = hold("one_hot", [P, PH, TOPK, TOPK])
    picked = hold("picked", [P, 2, 3, P])
    total = hold("total", [P, 2, PH])
    loaded, wq_loaded = sem("retrieve_loaded"), sem("wq_loaded")
    squared, rooted, chain, normed = sem("squared2"), sem("rooted2"), sem("chain2"), sem("normed2")
    turned, vec_out, sk_done, sk_out = sem("turned2"), sem("vec_out2"), sem("sk_done"), sem("sk_out")
    q_done, q_out, s_done, s_out = sem("q_done"), sem("q_out"), sem("s_done"), sem("s_out")
    tile_sorted, gap_done, exp_done, pick_done, pick_turned, pick_out = (sem(n) for n in (
        "tile_sorted", "gap_done", "exp_done", "pick_done", "pick_turned", "pick_out"))
    with nc.Block() as block:
        @block.sync
        def _(sp):
            sp.dma_start(g2[:, :], norm2_g[0].rearrange("(k p) -> p k", p=P)).then_inc(loaded, 16)
            sp.dma_start(sk[:, :, :].rearrange("n h (s d) -> n h s d", s=2), peer_sub_keys[0].rearrange("h s n d -> n h s d")).then_inc(loaded, 16)
            for c in range(2):
                sp.dma_start(w[:, c, :, :], peer_wq[0, :, c * 512:(c + 1) * 512].rearrange("(k p) n -> p k n", p=P)).then_inc(wq_loaded, 16)

        @block.scalar
        def _(act):
            for t in range(NT):
                r = ROWS[t]
                nc.scalar.activation(xn[0:r, t, :], x[0:r, t, :], ACT.Square, accum_out=k.ss[0:r, t:t + 1]).then_inc(squared, 1)
            act.wait_ge(chain, 1)
            nc.scalar.activation(k.ss[:, 0:NT], k.rstd[:, 0:NT], ACT.Sqrt).then_inc(rooted, 1)
            for g in range(2):
                act.wait_ge(sk_done, g + 1)
                nc.scalar.copy(skT[:, 4 * g:4 * g + 4, :], ps[:, 6 + g, :].rearrange("p (h n) -> p h n", h=4)).then_inc(sk_out, 1)
            for u in range(2 * PH):
                act.wait_ge(q_done, u + 1)
                m, h = divmod(u, 2)
                nc.scalar.copy(qT[:, m, h * HALF:(h + 1) * HALF], ps[:, u % 4, 0:HALF]).then_inc(q_out, 1)

            def take_scores(t):
                r = ROWS[t]
                act.wait_ge(s_done, t + 1)
                if t >= 2:
                    act.wait_ge(tile_sorted, t - 1)
                nc.scalar.copy(sc[0:r, t % 2].rearrange("p s h n -> p (s h n)"), ps[0:r, 4:8, :].rearrange("p b n -> p (b n)")).then_inc(s_out, 1)

            take_scores(0)
            for t in range(NT):
                r = ROWS[t]
                if t + 1 < NT:
                    take_scores(t + 1)
                act.wait_ge(gap_done, t + 1)
                w3 = picked[0:r, t % 2, 2, :]
                nc.scalar.activation(w3, w3, ACT.Exp).then_inc(exp_done, 1)
                act.wait_ge(pick_turned, t + 1)
                nc.scalar.copy(chosen[:, :, t * P:t * P + r], ps[:, t % 2, 0:3 * P].rearrange("p (a n) -> p a n", a=3)[:, :, 0:r]).then_inc(pick_out, 1)

        @block.tensor
        def _(pe):
            for u in range(2 * NT):
                t, g = divmod(u, 2)
                r = ROWS[t]
                pe.wait_ge(normed, t + 1)
                if u >= 4:
                    pe.wait_ge(vec_out, u - 3)
                for i in range(4):
                    kk = 4 * g + i
                    ins = nc.tensor.transpose(ps[:, u % 4, i * P:i * P + r], xn[0:r, t, kk * P:(kk + 1) * P], ident[0:r, 0:r])
                ins.then_inc(turned, 1)
            pe.wait_ge(loaded, 32)
            for g in range(2):
                for i in range(4):
                    ins = nc.tensor.transpose(ps[:, 6 + g, i * P:(i + 1) * P], sk[:, 4 * g + i, :], ident[:, :])
                ins.then_inc(sk_done, 1)
            pe.wait_ge(vec_out, 2 * NT)
            pe.wait_ge(wq_loaded, 32)
            for u in range(2 * PH):
                m, h = divmod(u, 2)
                if u >= 4:
                    pe.wait_ge(q_out, u - 3)
                for kk in range(KD):
                    ins = nc.tensor.matmul(ps[:, u % 4, 0:HALF], w[:, m // 4, kk, (m % 4) * P:(m % 4 + 1) * P], xn2T[:, kk, h * HALF:(h + 1) * HALF],
                                           start=(kk == 0), stop=(kk == KD - 1))
                ins.then_inc(q_done, 1)
            pe.wait_ge(q_out, 2 * PH)
            pe.wait_ge(sk_out, 2)

            def score(t):
                r = ROWS[t]
                if t >= 1:
                    pe.wait_ge(s_out, t)
                for h in range(PH):
                    for s in range(2):
                        lo = CHUNK * s
                        ins = nc.tensor.matmul(ps[0:r, 4 + 2 * s + h // 4, (h % 4) * NK:(h % 4 + 1) * NK], qT[lo:lo + CHUNK, h, t * P:t * P + r],
                                               skT[lo:lo + CHUNK, h, :], start=True, stop=True)
                ins.then_inc(s_done, 1)
            score(0)
            for t in range(NT):
                r = ROWS[t]
                if t + 1 < NT:
                    score(t + 1)
                pe.wait_ge(pick_done, t + 1)
                if t >= 2:
                    pe.wait_ge(pick_out, t - 1)
                for i in range(3):
                    ins = nc.tensor.transpose(ps[:, t % 2, i * P:i * P + r], picked[0:r, t % 2, i, :], ident[0:r, 0:r])
                ins.then_inc(pick_turned, 1)

        @block.vector
        def _(dve):
            link = linker(dve, chain)
            dve.wait_ge(squared, NT)
            link(nc.vector.tensor_scalar(k.rstd[:, 0:NT], k.ss[:, 0:NT], 1.0 / D, EPS, ALU.mult, ALU.add))
            dve.wait_ge(rooted, 1)
            link(nc.vector.reciprocal(k.rstd[:, 0:NT], k.ss[:, 0:NT]))
            for t in range(NT):
                r = ROWS[t]
                nc.vector.tensor_scalar(xn[0:r, t, :], x[0:r, t, :], k.rstd[0:r, t:t + 1], None, ALU.mult).then_inc(normed, 1)
            dve.wait_ge(loaded, 32)
            for u in range(2 * NT):
                t, g = divmod(u, 2)
                r = ROWS[t]
                dve.wait_ge(turned, u + 1)
                nc.vector.tensor_tensor(xn2T[:, 4 * g:4 * g + 4, t * P:t * P + r], ps[:, u % 4, :].rearrange("p (g n) -> p g n", g=4)[:, :, 0:r],
                                        bcast(g2[:, 4 * g:4 * g + 4], 2, r), ALU.mult).then_inc(vec_out, 1)

            def top16(rows, values, left, best, index, done=None):
                for v, b in zip(values, best):
                    ins = nc.vector.max(b[:, 0:8], v)
                link(ins)
                for v, l, b in zip(values, left, best):
                    ins = nc.vector.match_replace(l, b[:, 0:8], v, LOWEST)
                link(ins)
                for v, b, i in zip(values, best, index):
                    ins = nc.vector.max_index(i[:, 0:8], b[:, 0:8], v)
                if done is not None:
                    ins.then_inc(done, 1)
                for l, b in zip(left, best):
                    ins = nc.vector.max(b[:, 8:16], l)
                link(ins)
                for l, b, i in zip(left, best, index):
                    ins = nc.vector.max_index(i[:, 8:16], b[:, 8:16], l)
                link(ins)

            for t in range(NT):
                r = ROWS[t]
                dve.wait_ge(s_out, t + 1)
                both = [(s, h) for s in range(2) for h in range(PH)]
                top16(r, [sc[0:r, t % 2, s, h, :] for s, h in both], [rest[0:r, s, h, :] for s, h in both],
                      [sv[0:r, s, h, :] for s, h in both], [si[0:r, s, h, :] for s, h in both], tile_sorted)
                link(nc.vector.tensor_copy(sif[0:r], si[0:r]))
                pair = rest[0:r].rearrange("p s h n -> p (s h n)").rearrange("p (h a b) -> p h a b", h=PH, a=TOPK)
                pair2 = one_hot[0:r].rearrange("p h a b -> p h (a b)")
                link(nc.vector.tensor_tensor(pair, bcast(sv[0:r, 0], 3, TOPK), bcast(sv[0:r, 1], 2, TOPK), ALU.add))
                pairf = rest[0:r].rearrange("p s h n -> p (s h n)").rearrange("p (h m) -> p h m", h=PH)
                top16(r, [pairf[:, h, :] for h in range(PH)], [pair2[:, h, :] for h in range(PH)],
                      [fv[0:r, h, :] for h in range(PH)], [fi[0:r, h, :] for h in range(PH)])
                if t >= 2:
                    dve.wait_ge(pick_turned, t - 1)
                w3 = picked[0:r, t % 2, 2, :].rearrange("p (h n) -> p h n", h=PH)
                nc.vector.tensor_tensor(w3, fv[0:r], fv[0:r, :, 0:1].broadcast_to([r, PH, TOPK]), ALU.subtract).then_inc(gap_done, 1)
                link(nc.vector.tensor_scalar(pos[0:r, 0], fi[0:r], 4, None, ALU.logical_shift_right))
                link(nc.vector.tensor_scalar(pos[0:r, 1], fi[0:r], 15, None, ALU.bitwise_and))
                link(nc.vector.tensor_copy(posf[0:r], pos[0:r]))
                for s in range(2):
                    hot = one_hot[0:r].rearrange("p h a b -> p (h a) b")
                    at = bcast(posf[0:r, s].rearrange("p h a -> p (h a)"), 2, TOPK)
                    link(nc.vector.tensor_tensor(hot, at, bcast(k.iota[0:r, 0:TOPK], 1, PH * TOPK), ALU.is_equal))
                    link(nc.vector.tensor_tensor(one_hot[0:r], one_hot[0:r], bcast(sif[0:r, s], 2, TOPK), ALU.mult))
                    link(nc.vector.tensor_reduce(picked[0:r, t % 2, s, :], hot, AX.X, ALU.add))
                dve.wait_ge(exp_done, t + 1)
                link(nc.vector.tensor_reduce(total[0:r, 0], w3, AX.X, ALU.add))
                link(nc.vector.reciprocal(total[0:r, 1], total[0:r, 0]))
                nc.vector.tensor_tensor(w3, w3, bcast(total[0:r, 1], 2, TOPK), ALU.mult).then_inc(pick_done, 1)


def route(nc, k, hold):
    ps, iota, chosen, route_dram = k.ps, k.iota, k.chosen, k.route_dram
    sem = k.sem
    QUAD = 4
    QUADS = 8
    first = hold("first", [P, QUADS, QUAD, P])
    second = hold("second", [P, QUADS, QUAD, P])
    index = hold("index", [P, 2, GRP // 2])
    dense = hold("dense", [P, 2, P, GRP])
    first_ready, second_ready, product_done, quad_out = (sem(n) for n in (
        "first_ready", "second_ready", "product_done", "quad_out"))
    group_stored = [sem("group_stored0"), sem("group_stored1")]

    def turns(eng, turn):
        turn(0, 0, 0)
        turn(1, 1, 0)
        with eng.Fori(1, NGRP // 2) as j:
            turn(2 * j, 0, j)
            turn(2 * j + 1, 1, j)
        turn(NGRP - 1, 0, NGRP // 2)

    def later(i):
        return not (isinstance(i, int) and i == 0)

    with nc.Block() as block:
        @block.gpsimd
        def _(pool):
            def turn(i, slot, filled):
                for half in range(2):
                    if later(i):
                        pool.wait_ge(product_done, (i - 1) * QUADS + (half + 1) * QUADS // 2)
                    nc.gpsimd.tensor_copy(index[:, half, :], chosen[:, 0, ds(i * GRP + half * GRP // 2, GRP // 2)])
                    pool.drain()
                    for v in range(GRP // 2):
                        q, f = half * QUADS // 2 + v // QUAD, v % QUAD
                        ins = nc.gpsimd.tensor_scalar(first[:, q, f, :], iota[:, :], index[:, half, v:v + 1], None, ALU.is_equal)
                        if f == QUAD - 1:
                            ins.then_inc(first_ready, 1)
            turns(pool, turn)

        @block.vector
        def _(dve):
            def turn(i, slot, filled):
                for q in range(QUADS):
                    if later(i):
                        dve.wait_ge(product_done, (i - 1) * QUADS + q + 1)
                    for f in range(QUAD):
                        n = i * GRP + q * QUAD + f
                        ins = nc.vector.tensor_scalar(second[:, q, f, :], iota[:, :], chosen[:, 1, ds(n, 1)], chosen[:, 2, ds(n, 1)],
                                                      ALU.is_equal, ALU.mult)
                    ins.then_inc(second_ready, 1)
            turns(dve, turn)

        @block.tensor
        def _(pe):
            def turn(i, slot, filled):
                for q in range(QUADS):
                    pe.wait_ge(first_ready, i * QUADS + q + 1)
                    pe.wait_ge(second_ready, i * QUADS + q + 1)
                    if later(i):
                        pe.wait_ge(quad_out, (i - 1) * QUADS + q + 1)
                    for f in range(QUAD):
                        ins = nc.tensor.matmul(ps[:, q, f * P:(f + 1) * P], second[:, q, f, :], first[:, q, f, :], start=True, stop=True)
                    ins.then_inc(product_done, 1)
            turns(pe, turn)

        @block.scalar
        def _(act):
            def turn(i, slot, filled):
                for q in range(QUADS):
                    act.wait_ge(product_done, i * QUADS + q + 1)
                    if q == 0 and not (isinstance(filled, int) and filled == 0):
                        act.wait_ge(group_stored[slot], 16 * filled)
                    nc.scalar.copy(dense[:, slot, :, q * QUAD:(q + 1) * QUAD].rearrange("p i n -> p n i"),
                                   ps[:, q, :].rearrange("p (n i) -> p n i", n=QUAD)).then_inc(quad_out, 1)
            turns(act, turn)

        @block.sync
        def _(sp):
            def turn(i, slot, filled):
                sp.wait_ge(quad_out, (i + 1) * QUADS)
                sp.dma_start(route_dram[ds(i, 1)].rearrange("a j i n -> j (a i n)"), dense[:, slot].rearrange("p i n -> p (i n)")
                             ).then_inc(group_stored[slot], 16)
            turns(sp, turn)
            sp.wait_ge(group_stored[0], 16 * (NGRP // 2 + 1))
            sp.wait_ge(group_stored[1], 16 * (NGRP // 2))


def experts(nc, k, hold, peer_u, peer_v):
    ps, xn2T, ident, acc, route_dram = k.ps, k.xn2T, k.ident, k.acc, k.route_dram
    sem = k.sem
    SUB = 4
    TURN = 2 * SUB
    TURNS = P // TURN
    u_nat = hold("u_nat", [P, 2, SUB, D])
    v_nat = hold("v_nat", [P, 2, SUB, D])
    routing = hold("routing_sb", [P, 2, NGRP, SUB, GRP])
    uT = hold("uT", [P, 2, KD, P])
    act_out = hold("act_out", [P, 2, 2, HALF])
    hid = hold("hid", [P, 2, SUB, T])
    u_loaded = [sem("u_loaded0"), sem("u_loaded1")]
    v_loaded = [sem("v_loaded0"), sem("v_loaded1")]
    r_loaded = [sem("r_loaded0"), sem("r_loaded1")]
    cleared, turned, uT_act, uT_vec, pre_done, gelu_done, hid_done, out_done, out_added = (sem(n) for n in (
        "acc_cleared", "u_turned", "uT_act", "uT_vec", "pre_done", "gelu_done", "hid_done", "expert_out_done", "expert_out_added"))
    UNITS = 2 * KD

    def turns(eng, turn):
        turn(0, True, False)
        with eng.Fori(1, TURNS - 1) as i:
            turn(i, False, False)
        turn(TURNS - 1, False, True)

    with nc.Block() as block:
        @block.sync
        def _(sp):
            def turn(i, first, last):
                for s in range(2):
                    rows = ds((2 * i + s) * SUB * P, SUB * P)
                    if not first:
                        sp.wait_ge(turned, (2 * i + s - 1) * SUB)
                    sp.dma_start(u_nat[:, s], peer_u[0, rows, :].rearrange("(a p) d -> p a d", p=P)).then_inc(u_loaded[s], 16)
                    if not first:
                        sp.wait_ge(out_done, (2 * i + s - 1) * UNITS)
                    sp.dma_start(v_nat[:, s], peer_v[0, rows, :].rearrange("(a p) d -> p a d", p=P)).then_inc(v_loaded[s], 16)
            turns(sp, turn)

        @block.gpsimd
        def _(pool):
            nc.gpsimd.memset(acc[:, :, :], 0.0).then_inc(cleared, 1)

            def turn(i, first, last):
                for s in range(2):
                    if not first:
                        pool.wait_ge(hid_done, (2 * i + s - 1) * SUB)
                    pool.dma_start(routing[:, s].rearrange("j g a n -> j g (a n)"),
                                   route_dram[:, :, ds((2 * i + s) * SUB, SUB), :].rearrange("g j a n -> j g (a n)")).then_inc(r_loaded[s], 16)
            turns(pool, turn)

        @block.tensor
        def _(pe):
            def transposes(i, s, u, first):
                n = 2 * SUB * i + SUB * s + u
                if u == 0:
                    pe.wait_ge(u_loaded[s], 16 * (i + 1))
                if not (first and s == 0 and u == 0):
                    pe.wait_ge(uT_act, n)
                    pe.wait_ge(uT_vec, n)
                for kk in range(KD):
                    ins = nc.tensor.transpose(ps[:, kk // 4, (kk % 4) * P:(kk % 4 + 1) * P], u_nat[:, s, u, kk * P:(kk + 1) * P], ident[:, :])
                ins.then_inc(turned, 1)

            def pre(i, s, u, first):
                n = 2 * SUB * i + SUB * s + u
                b = u % 2
                pe.wait_ge(uT_act, n + 1)
                pe.wait_ge(uT_vec, n + 1)
                if not (first and s == 0 and u < 2):
                    pe.wait_ge(gelu_done, n - 1)
                for h in range(2):
                    for kk in range(KD):
                        ins = nc.tensor.matmul(ps[:, 2 + 2 * b + h, 0:HALF], uT[:, b, kk, :], xn2T[:, kk, h * HALF:(h + 1) * HALF],
                                               start=(kk == 0), stop=(kk == KD - 1))
                ins.then_inc(pre_done, 1)

            def output(i, s, first):
                m = 2 * i + s
                pe.wait_ge(v_loaded[s], 16 * (i + 1))
                pe.wait_ge(hid_done, (m + 1) * SUB)
                for o in range(UNITS):
                    kk, h = divmod(o, 2)
                    if not (first and s == 0 and o < 2):
                        pe.wait_ge(out_added, m * UNITS + o - 1)
                    for u in range(SUB):
                        ins = nc.tensor.matmul(ps[:, 6 + h, 0:HALF], v_nat[:, s, u, kk * P:(kk + 1) * P], hid[:, s, u, h * HALF:(h + 1) * HALF],
                                               start=(u == 0), stop=(u == SUB - 1))
                    ins.then_inc(out_done, 1)

            def turn(i, first, last):
                for s in range(2):
                    for u in range(SUB):
                        if u + 1 < SUB:
                            transposes(i, s, u + 1, first)
                        elif s == 0:
                            transposes(i, 1, 0, first)
                        elif not last:
                            transposes(i + 1, 0, 0, False)
                        pre(i, s, u, first)
                        if u == 0 and not (first and s == 0):
                            output(*((i, 0, first) if s == 1 else (i - 1, 1, False)))
            transposes(0, 0, 0, True)
            turns(pe, turn)
            output(TURNS - 1, 1, False)

        @block.scalar
        def _(act):
            def copy_uT(n, b, first):
                act.wait_ge(turned, n + 1)
                if not first:
                    act.wait_ge(pre_done, n - 1)
                nc.scalar.copy(uT[:, b, 0:4, :], ps[:, 0, :].rearrange("p (g n) -> p g n", g=4)).then_inc(uT_act, 1)

            def turn(i, first, last):
                for v in range(TURN):
                    n = TURN * i + v
                    if not (last and v == TURN - 1):
                        copy_uT(n + 1, (v + 1) % 2, first and v == 0)
                    act.wait_ge(pre_done, n + 1)
                    if not (first and v < 2):
                        act.wait_ge(hid_done, n - 1)
                    nc.scalar.activation(act_out[:, v % 2], ps[:, 2 + 2 * (v % 2):4 + 2 * (v % 2), 0:HALF], ACT.Gelu).then_inc(gelu_done, 1)
            copy_uT(0, 0, True)
            turns(act, turn)

        @block.vector
        def _(dve):
            dve.wait_ge(cleared, 1)

            def copy_uT(n, b, first):
                dve.wait_ge(turned, n + 1)
                if not first:
                    dve.wait_ge(pre_done, n - 1)
                nc.vector.tensor_copy(uT[:, b, 4:8, :], ps[:, 1, :].rearrange("p (g n) -> p g n", g=4)).then_inc(uT_vec, 1)

            def add_output(m):
                for o in range(UNITS):
                    kk, h = divmod(o, 2)
                    dve.wait_ge(out_done, m * UNITS + o + 1)
                    a = acc[:, kk, h * HALF:(h + 1) * HALF]
                    nc.vector.tensor_tensor(a, ps[:, 6 + h, 0:HALF], a, ALU.add).then_inc(out_added, 1)

            def turn(i, first, last):
                for v in range(TURN):
                    n = TURN * i + v
                    s, u = divmod(v, SUB)
                    if not (last and v == TURN - 1):
                        copy_uT(n + 1, (v + 1) % 2, first and v == 0)
                    if u == 0:
                        dve.wait_ge(r_loaded[s], 16 * (i + 1))
                    dve.wait_ge(gelu_done, n + 1)
                    if u == 0 and not first:
                        dve.wait_ge(out_done, (2 * i + s - 1) * UNITS)
                    nc.vector.tensor_tensor(hid[:, s, u, :].rearrange("p (g n) -> p g n", g=NGRP),
                                            act_out[:, v % 2].rearrange("p h n -> p (h n)").rearrange("p (g n) -> p g n", g=NGRP),
                                            routing[:, s, :, u, :], ALU.mult).then_inc(hid_done, 1)
                    if u == 0 and not (first and s == 0):
                        add_output(2 * i + s - 1)
            copy_uT(0, 0, True)
            turns(dve, turn)
            add_output(2 * TURNS - 1)


def finish(nc, k, hold, final_g, y_prompt, y_sample):
    ps, x, acc, ident = k.ps, k.x, k.acc, k.ident
    sem = k.sem
    g = hold("g_final", [P, D])
    y = hold("y", [P, NT, D])
    loaded, turned, added, squared, rooted, chain, scaled, ready, stored = (sem(n) for n in (
        "final_loaded", "turned3", "added3", "squared3", "rooted3", "chain3", "scaled3", "y_ready", "y_stored"))
    with nc.Block() as block:
        @block.sync
        def _(sp):
            sp.dma_start(g[:, :], final_g.partition_broadcast(P)).then_inc(loaded, 16)
            for t in range(NT):
                sp.wait_ge(ready, t + 1)
                out = y_prompt[0, t * P:(t + 1) * P, :] if t < 4 else y_sample[0]
                sp.dma_start(out, y[0:ROWS[t], t, :]).then_inc(stored, 16)
            sp.wait_ge(stored, 16 * NT)

        @block.tensor
        def _(pe):
            for t in range(NT):
                r, b = ROWS[t], 2 * (t % 4)
                if t >= 4:
                    pe.wait_ge(added, t - 3)
                for kk in range(KD):
                    ins = nc.tensor.transpose(ps[0:r, b + kk // 4, (kk % 4) * P:(kk % 4 + 1) * P], acc[:, kk, t * P:t * P + r], ident[:, :])
                ins.then_inc(turned, 1)

        @block.scalar
        def _(act):
            for t in range(NT):
                r = ROWS[t]
                act.wait_ge(added, t + 1)
                nc.scalar.activation(y[0:r, t, :], x[0:r, t, :], ACT.Square, accum_out=k.ss[0:r, t:t + 1]).then_inc(squared, 1)
            act.wait_ge(chain, 1)
            nc.scalar.activation(k.ss[:, 0:NT], k.rstd[:, 0:NT], ACT.Sqrt).then_inc(rooted, 1)
            act.wait_ge(chain, 2)
            for t in range(NT):
                r = ROWS[t]
                nc.scalar.activation(y[0:r, t, :], x[0:r, t, :], ACT.Copy, scale=k.rstd[0:r, t:t + 1]).then_inc(scaled, 1)

        @block.vector
        def _(dve):
            for t in range(NT):
                r, b = ROWS[t], 2 * (t % 4)
                dve.wait_ge(turned, t + 1)
                nc.vector.tensor_tensor(x[0:r, t, :], ps[0:r, b:b + 2, :].rearrange("p b n -> p (b n)"), x[0:r, t, :], ALU.add).then_inc(added, 1)
            dve.wait_ge(squared, NT)
            link = linker(dve, chain)
            link(nc.vector.tensor_scalar(k.rstd[:, 0:NT], k.ss[:, 0:NT], 1.0 / D, EPS, ALU.mult, ALU.add))
            dve.wait_ge(rooted, 1)
            link(nc.vector.reciprocal(k.rstd[:, 0:NT], k.ss[:, 0:NT]))
            dve.wait_ge(loaded, 16)
            for t in range(NT):
                r = ROWS[t]
                dve.wait_ge(scaled, t + 1)
                nc.vector.tensor_tensor(y[0:r, t, :], y[0:r, t, :], g[0:r, :], ALU.mult).then_inc(ready, 1)


_INS = ['x_prompt', 'x_sample', 'cache_att_k', 'cache_att_v', 'state_mlstm_C', 'state_mlstm_n', 'state_mlstm_m',
        'norm1_g', 'w_in', 'b_in', 'ml_f_bias', 'att_rel_bias', 'w_att_branch', 'w_ml_branch', 'w_out',
        'norm2_g', 'peer_wq', 'peer_sub_keys', 'peer_u', 'peer_v', 'final_g']
_OUTS = [(1, S, D), (1, TS, D), (1, 1, S, AH, AD), (1, 1, S, AH, AD), (1, 1, MH, P, P), (1, 1, MH, P), (1, 1, MH),
         (1, 1, TS, AH, AD), (1, 1, TS, AH, AD), (1, 1, MH, P, P), (1, 1, MH, P), (1, 1, MH)]


def kernel(**inputs):
    import numpy as _np
    import concourse.bacc as _bacc
    from concourse import mybir as _mybir
    from concourse.bass_utils import run_bass_kernel_spmd as _run

    nc = _bacc.Bacc("TRN2", target_bir_lowering=False, num_devices=1)
    arrays, args = {}, []
    for name in _INS:
        a = _np.ascontiguousarray(inputs[name])
        arrays[f"in_{name}_dram"] = a
        args.append(nc.dram_tensor(f"in_{name}_dram", a.shape, _mybir.dt.from_np(a.dtype), kind="ExternalInput").ap())
    for i, shape in enumerate(_OUTS):
        args.append(nc.dram_tensor(f"out_{i}_dram", shape, F32, kind="ExternalOutput").ap())
    with nc.allow_non_contiguous_dma(reason="short vectors laid out as columns"):
        program(nc, *args)
    r = _run(nc, [arrays], core_ids=[0])
    return tuple(r.results[0][f"out_{i}_dram"] for i in range(len(_OUTS)))
```

```python
from contextlib import ExitStack

import concourse.bass as bass
from concourse import mybir
from concourse.bass import ds

ALU = mybir.AluOpType
ACT = mybir.ActivationFunctionType
F32 = mybir.dt.float32
F32R = mybir.dt.float32r
U32 = mybir.dt.uint32
AX = mybir.AxisListType

P = 128
D = 1024
KD = D // P
S = 512
TS = 32
T = S + TS
HALF = T // 2
ROWS = [P, P, P, P, TS]
NT = len(ROWS)
AH, AD = 8, 64
MH = 4
BW = S + P
MAX_REL = 128
NEG = -1e30
LOWEST = -3.0e38
EPS = 1e-6
PH, NK, TOPK = 8, 128, 16
CHUNK = 64
ML_SCALE = float(P) ** -0.5
GRP = 32
NGRP = T // GRP
QUAD = 4
AQ, AK, AV, MQ, MK, MV, MO, GATES, GA, GB = 0, 512, 1024, 1536, 2048, 2560, 3072, 3584, 3592, 4616


class Shared:
    pass


def bcast(ap, axis, n):
    u = ap.unsqueeze(axis)
    shape = list(u.shape)
    shape[axis] = n
    return u.broadcast_to(shape)


def after(eng, sem, value):
    if not (isinstance(value, int) and value <= 0):
        eng.wait_ge(sem, value)


def linker(eng, sem):
    count = [0]

    def link(ins):
        count[0] += 1
        ins.then_inc(sem, 1)
        eng.wait_ge(sem, count[0])
    return link


def program(nc, x_prompt, x_sample, cache_att_k, cache_att_v, state_mlstm_C, state_mlstm_n, state_mlstm_m,
            norm1_g, w_in, b_in, ml_f_bias, att_rel_bias, w_att_branch, w_ml_branch, w_out,
            norm2_g, peer_wq, peer_sub_keys, peer_u, peer_v, final_g,
            y_prompt, y_sample, att_k_prompt, att_v_prompt, C_prompt, n_prompt, m_prompt,
            att_k_sample, att_v_sample, C_sample, n_sample, m_sample):
    with ExitStack() as whole:
        def holder(stack):
            return lambda name, shape, dt=F32: stack.enter_context(nc.sbuf_tensor(name, shape, dt))

        keep = holder(whole)
        k = Shared()
        k.sem = lambda name: whole.enter_context(nc.semaphore(name))
        k.ps = whole.enter_context(nc.psum_tensor("ps", [P, 8, 512], F32))
        k.ident = keep("ident", [P, P])
        k.iota = keep("iota_row", [P, P])
        k.ones = keep("ones", [P, P])
        k.x = keep("x", [P, NT, D])
        k.ss = keep("ss", [P, 8])
        k.rstd = keep("rstd", [P, 8])
        k.line_dram = nc.dram_tensor("rel_line", (AH, P, BW + P), F32, kind="Internal").ap()
        k.gelu_dram = nc.dram_tensor("hidden", (P, P, T), F32, kind="Internal").ap()
        k.route_dram = nc.dram_tensor("routing", (NGRP, P, P, GRP), F32, kind="Internal").ap()
        with ExitStack() as early:
            hold = holder(early)
            k.xnT = hold("xnT", [P, KD, T])
            k.aqT = hold("aqT", [P, 4, T])
            k.mqT = hold("mqT", [P, MH, T])
            with ExitStack() as now:
                project(nc, k, holder(now), x_prompt, x_sample, cache_att_k, cache_att_v, state_mlstm_C,
                        state_mlstm_n, state_mlstm_m, norm1_g, w_in, b_in, ml_f_bias, att_rel_bias,
                        att_k_prompt, att_v_prompt, C_prompt, n_prompt, m_prompt,
                        att_k_sample, att_v_sample, C_sample, n_sample, m_sample)
            with ExitStack() as now:
                merge(nc, k, holder(now), w_in, b_in, w_att_branch, w_ml_branch, w_out)
        with ExitStack() as late:
            hold = holder(late)
            k.x_high = hold("x_high", [P, KD, T], F32R)
            k.x_low = hold("x_low", [P, KD, T], F32R)
            k.chosen = hold("chosen", [P, 3, T])
            hidden = Hidden(nc, k, hold, peer_u)
            with ExitStack() as now:
                retrieve(nc, k, holder(now), hidden, norm2_g, peer_wq, peer_sub_keys)
            with ExitStack() as now:
                route(nc, k, holder(now), hidden)
        k.acc = keep("acc", [P, KD, T])
        with ExitStack() as now:
            experts(nc, k, holder(now), peer_v)
        with ExitStack() as now:
            finish(nc, k, holder(now), final_g, y_prompt, y_sample)


def project(nc, k, hold, x_prompt, x_sample, cache_att_k, cache_att_v, state_mlstm_C, state_mlstm_n,
            state_mlstm_m, norm1_g, w_in, b_in, ml_f_bias, att_rel_bias,
            att_k_prompt, att_v_prompt, C_prompt, n_prompt, m_prompt,
            att_k_sample, att_v_sample, C_sample, n_sample, m_sample):
    ps, x, xnT, aqT, mqT, ident = k.ps, k.x, k.xnT, k.aqT, k.mqT, k.ident
    sem = k.sem
    akT = hold("akT", [P, 4, T])
    mkT = hold("mkT", [P, MH, T])
    ak_nat = hold("ak_nat", [P, NT, 512])
    av_nat = hold("av_nat", [P, NT, 512])
    mk_nat = hold("mk_nat", [P, NT, 512])
    mv_nat = hold("mv_nat", [P, NT, 512])
    kc_nat = ak_nat[:, 0:4, :]
    kcT = hold("kcT", [P, 4, S])
    w = hold("w", [P, 2, KD, 512])
    row = w[0:MH, 0, :, :].rearrange("p a b -> p (a b)")[:, 0:7 * T].rearrange("p (r t) -> p r t", r=7)
    vc = w[:, 1, 0:4, :]
    late = w[:, 1, 4:8, :].rearrange("p a b -> p (a b)")
    pT = late[:, 0:10 * P].rearrange("p (b s n) -> p b s n", b=2, s=5)
    em_bc = late[:, 10 * P:10 * P + S]
    w_gate = hold("w_gate", [P, KD, 8])
    bias = hold("bias", [P, AH, BW])
    xn = bias[:, :, :].rearrange("p h j -> p (h j)").rearrange("p (t d) -> p t d", t=NT)
    g1 = hold("g1", [P, KD])
    b_col = hold("b_col", [P, 28])
    b_av = hold("b_av", [P, 512])
    b_mv = hold("b_mv", [P, 512])
    table = hold("table", [P, 2, AH])
    flip = hold("flip", [P, P])
    line = hold("line", [AH, BW + P])
    heads = hold("heads", [MH, MH, P])
    small = hold("small", [MH, 8])
    c_col = hold("c_col", [P, NT, MH])
    work = hold("work", [P, 4, T])
    vw = hold("vw", [P, 2, P + 1])
    samp = hold("samp", [P, 4, TS])
    state = hold("state", [P, MH, P + 1])
    n_rep = hold("n_rep", [P, P])
    c_out = hold("c_out", [P, MH, P + 1])
    amax = hold("amax", [P, 4])
    asum = hold("asum", [P, 4])

    x_loaded, const_loaded, cache_loaded, tab_loaded = sem("x_loaded"), sem("const_loaded"), sem("cache_loaded"), sem("tab_loaded")
    w_loaded = [sem("w_loaded0"), sem("w_loaded1")]
    vc_loaded, wg_loaded, line_stored, bias_loaded, stored = sem("vc_loaded"), sem("wg_loaded"), sem("line_stored"), sem("bias_loaded"), sem("stored")
    pool_const, vec_const = sem("pool_const"), sem("vec_const")
    squared, rooted, vec_chain = sem("squared"), sem("rooted"), sem("vec_chain")
    normed, line_done = sem("normed"), sem("line_done")
    unit_done, vec_evicted, act_evicted = sem("unit_done"), sem("vec_evicted"), sem("act_evicted")
    gate_vec, gate_act = sem("gate_vec"), sem("gate_act")
    c_turned, c_copied = sem("c_turned"), sem("c_copied")
    ml_rows, ml_em, ml_qk, ml_gap, ml_w, ml_masked, ml_wqk, ml_vw = (sem(n) for n in (
        "ml_rows", "ml_em", "ml_qk", "ml_gap", "ml_w", "ml_masked", "ml_wqk", "ml_vw"))
    ml_used, ml_sample, ml_head = sem("ml_used"), sem("ml_sample"), sem("ml_head")
    at_scored, at_max, at_exp, at_norm, at_turned, at_copied, at_pv, at_out = (sem(n) for n in (
        "at_scored", "at_max", "at_exp", "at_norm", "at_turned", "at_copied", "at_pv", "at_out"))
    at_added = sem("at_added")
    bias_masked = sem("bias_masked")

    units = [("xn", (t, g), "vec") for t in range(NT) for g in range(2)]
    units += [("cache", s, "act") for s in range(4)]
    units += [("line", i, "act") for i in range(2)]
    chunks = [("mq", MQ, mqT, "act"), ("mk", MK, mkT, "vec"), ("mv", MV, mv_nat, "vec"),
              ("aq", AQ, aqT, "vec"), ("ak", AK, akT, "act"), ("av", AV, av_nat, "vec")]
    for c, (name, _, _, who) in enumerate(chunks):
        if name in ("mv", "av"):
            units += [(name, (c, t), who) for t in range(NT)]
        else:
            units += [(name, (c, m, h), who) for m in range(4) for h in range(2)]
    units += [("gate", (i, h), "act") for i in range(2) for h in range(2)]
    units += [("mk_turn", t, "act") for t in range(NT)] + [("ak_turn", t, "act") for t in range(NT)]
    BANKS = 4

    def evicted(u):
        who = units[u][2]
        return {"vec": vec_evicted, "act": act_evicted}[who], sum(v[2] == who for v in units[:u + 1])

    def last(name):
        return max(u for u, v in enumerate(units) if v[0] == name)

    DMAS_OUT = 4 + 6

    def wqk_of(q):
        return pT[:, q % 2, :, :].rearrange("p s n -> p (s n)")

    with nc.Block() as block:
        @block.sync
        def _(sp):
            sp.dma_start(x[:, 0:4, :], x_prompt[0].rearrange("(t p) d -> p t d", p=P)).then_inc(x_loaded, 16)
            sp.dma_start(x[0:TS, 4, :], x_sample[0]).then_inc(x_loaded, 16)
            sp.dma_start(g1[:, :], norm1_g[0].rearrange("(k p) -> p k", p=P)).then_inc(const_loaded, 16)
            sp.dma_start(kc_nat, cache_att_k[0, 0].rearrange("(s p) h d -> p s (h d)", p=P)).then_inc(cache_loaded, 16)
            sp.dma_start(table[:, 0, :], att_rel_bias[0, 1:P + 1, :]).then_inc(tab_loaded, 16)
            sp.dma_start(table[:, 1, :], att_rel_bias[0, P + 1:2 * P + 1, :]).then_inc(tab_loaded, 16)
            sp.dma_start(w_gate[:, :, :], w_in[0, :, GATES:GA].rearrange("(k p) n -> p k n", p=P)).then_inc(wg_loaded, 16)
            sp.dma_start(b_col[:, :], b_in[0, 0:GATES].rearrange("(m p) -> p m", p=P)).then_inc(const_loaded, 16)
            sp.dma_start(small[:, 0:2], b_in[0, GATES:GA].rearrange("(i h) -> h i", h=MH)).then_inc(const_loaded, 16)
            sp.dma_start(small[:, 2:3], ml_f_bias.rearrange("a h -> h a")).then_inc(const_loaded, 16)
            sp.dma_start(small[:, 3:4], state_mlstm_m[0].rearrange("a h -> h a")).then_inc(const_loaded, 16)
            sp.dma_start(b_av[:, :], b_in[0, AV:AV + 512].partition_broadcast(P)).then_inc(const_loaded, 16)
            sp.dma_start(b_mv[:, :], b_in[0, MV:MV + 512].partition_broadcast(P)).then_inc(const_loaded, 16)
            for c, (_, col, _, _) in enumerate(chunks):
                if c >= 2:
                    sp.wait_ge(unit_done, last(chunks[c - 2][0]) + 1)
                sp.dma_start(w[:, c % 2, :, :], w_in[0, :, col:col + 512].rearrange("(k p) n -> p k n", p=P)
                             ).then_inc(w_loaded[c % 2], 16)
                if c == 1:
                    sp.dma_start(state[:, :, 0:P], state_mlstm_C[0, 0].rearrange("h d e -> d h e")).then_inc(const_loaded, 16)
                    sp.dma_start(state[:, :, P], state_mlstm_n[0, 0].rearrange("h d -> d h")).then_inc(const_loaded, 16)
                    sp.wait_ge(line_done, 1)
                    sp.dma_start(k.line_dram, bcast(line[:, :], 1, P)).then_inc(line_stored, 16)
                    sp.wait_ge(line_stored, 16)
                    sp.wait_ge(unit_done, last("xn") + 1)
                    for h in range(AH):
                        sp.dma_start(bias[:, h, :], bass.AP(k.line_dram.tensor, h * P * (BW + P) + P, [[BW + P - 1, P], [1, BW]])
                                     ).then_inc(bias_loaded, 16)
            sp.wait_ge(unit_done, last("av") + 1)
            sp.dma_start(vc, cache_att_v[0, 0].rearrange("(s p) h d -> p s (h d)", p=P)).then_inc(vc_loaded, 16)
            n_done, n_val = evicted(last("ak_turn"))
            sp.wait_ge(n_done, n_val)
            sp.dma_start(att_k_prompt[0, 0].rearrange("(t p) h d -> p t (h d)", p=P), ak_nat[:, 0:4, :]).then_inc(stored, 16)
            sp.dma_start(att_k_sample[0, 0].rearrange("p h d -> p (h d)"), ak_nat[0:TS, 4, :]).then_inc(stored, 16)
            n_done, n_val = evicted(last("av"))
            sp.wait_ge(n_done, n_val)
            sp.dma_start(att_v_prompt[0, 0].rearrange("(t p) h d -> p t (h d)", p=P), av_nat[:, 0:4, :]).then_inc(stored, 16)
            sp.dma_start(att_v_sample[0, 0].rearrange("p h d -> p (h d)"), av_nat[0:TS, 4, :]).then_inc(stored, 16)
            sp.wait_ge(ml_head, 2 * MH)
            sp.dma_start(C_prompt[0, 0].rearrange("h d e -> d h e"), c_out[:, :, 0:P]).then_inc(stored, 16)
            sp.dma_start(n_prompt[0, 0].rearrange("h d -> d h"), c_out[:, :, P]).then_inc(stored, 16)
            sp.dma_start(m_prompt[0].rearrange("a h -> h a"), row[:, 4, S - 1:S]).then_inc(stored, 16)
            sp.dma_start(C_sample[0, 0].rearrange("h d e -> d h e"), state[:, :, 0:P]).then_inc(stored, 16)
            sp.dma_start(n_sample[0, 0].rearrange("h d -> d h"), state[:, :, P]).then_inc(stored, 16)
            sp.dma_start(m_sample[0].rearrange("a h -> h a"), row[:, 4, T - 1:T]).then_inc(stored, 16)
            sp.wait_ge(stored, 16 * DMAS_OUT)

        @block.gpsimd
        def _(pool):
            nc.gpsimd.memset(ident[:, :], 0.0).then_inc(pool_const, 1)
            nc.gpsimd.memset(flip[:, :], 0.0).then_inc(pool_const, 1)
            nc.gpsimd.memset(heads[:, :, :], 0.0).then_inc(pool_const, 1)
            pool.wait_ge(pool_const, 3)
            nc.gpsimd.affine_select(out=ident[:, :], in_=ident[:, :], compare_op=ALU.not_equal, fill=1.0, base=0,
                                    pattern=[[-1, P]], channel_multiplier=1).then_inc(pool_const, 1)
            nc.gpsimd.affine_select(out=flip[:, :], in_=flip[:, :], compare_op=ALU.not_equal, fill=1.0, base=1 - P,
                                    pattern=[[1, P]], channel_multiplier=1).then_inc(pool_const, 1)
            nc.gpsimd.affine_select(out=heads[:, :, :], in_=heads[:, :, :], compare_op=ALU.not_equal, fill=1.0, base=0,
                                    pattern=[[-1, MH], [0, P]], channel_multiplier=1).then_inc(pool_const, 1)
            nc.gpsimd.iota(k.iota[:, :], pattern=[[1, P]], base=0, channel_multiplier=0,
                           allow_small_or_imprecise_dtypes=True).then_inc(pool_const, 1)
            q = 0
            for h in range(MH):
                for s in range(NT):
                    n = ROWS[s]
                    lo = P * s if s < 4 else 0
                    pool.wait_ge(ml_w, q + 1)
                    diag = work[0:n, q % 2, lo:lo + n]
                    nc.gpsimd.affine_select(out=diag, in_=diag, compare_op=ALU.is_ge, fill=0.0, base=0,
                                            pattern=[[1, n]], channel_multiplier=-1).then_inc(ml_masked, 1)
                    q += 1

        @block.scalar
        def _(act):
            act.wait_ge(x_loaded, 32)
            act.wait_ge(vec_const, 2)
            for t in range(NT):
                r = ROWS[t]
                nc.scalar.activation(xn[0:r, t, :], x[0:r, t, :], ACT.Square, accum_out=k.ss[0:r, t:t + 1]).then_inc(squared, 1)
            act.wait_ge(vec_chain, 1)
            nc.scalar.activation(k.ss[:, 0:NT], k.rstd[:, 0:NT], ACT.Sqrt).then_inc(rooted, 1)
            act.wait_ge(const_loaded, 144)
            act.wait_ge(cache_loaded, 16)
            for u, (kind, arg, who) in enumerate(units):
                if who != "act":
                    continue
                act.wait_ge(unit_done, u + 1)
                b = u % BANKS
                if kind == "cache":
                    ins = nc.scalar.copy(kcT[:, :, arg * P:(arg + 1) * P], ps[:, b, :].rearrange("p (g n) -> p g n", g=4))
                elif kind == "line":
                    at = BW - P * arg
                    ins = nc.scalar.copy(line[:, at:at + P], ps[0:AH, b, 0:P])
                elif kind == "gate":
                    i, h = arg
                    ins = nc.scalar.activation(row[:, i, h * HALF:(h + 1) * HALF], ps[0:MH, b, 0:HALF], ACT.Identity,
                                               bias=small[:, i:i + 1])
                elif kind in ("mk_turn", "ak_turn"):
                    if kind == "ak_turn" and arg == 0:
                        ev, n = evicted(last("cache"))
                        act.wait_ge(ev, n)
                    r = ROWS[arg]
                    dst = mk_nat if kind == "mk_turn" else ak_nat
                    ins = nc.scalar.copy(dst[0:r, arg, :], ps[0:r, b, :])
                else:
                    c, m, h = arg
                    col = chunks[c][1] // P + m
                    ins = nc.scalar.activation(chunks[c][2][:, m, h * HALF:(h + 1) * HALF], ps[:, b, 0:HALF], ACT.Identity,
                                               bias=b_col[:, col:col + 1])
                ins.then_inc(act_evicted, 1)
            act.wait_ge(gate_vec, 1)
            nc.scalar.activation(row[:, 3, :], row[:, 2, :], ACT.Exp, scale=-1.0).then_inc(gate_act, 1)
            act.wait_ge(gate_vec, 2)
            nc.scalar.activation(row[:, 3, :], row[:, 2, :], ACT.Ln).then_inc(gate_act, 1)
            act.wait_ge(gate_vec, 3)
            nc.scalar.activation(row[:, 6, :], row[:, 4, :], ACT.Exp, scale=-1.0).then_inc(gate_act, 1)
            nc.scalar.activation(row[:, 0, S:T], row[:, 2, S:T], ACT.Exp, scale=-1.0).then_inc(gate_act, 1)
            q = 0
            for h in range(MH):
                act.wait_ge(ml_rows, h + 1)
                if h >= 1:
                    act.wait_ge(ml_head, 2 * h)
                nc.scalar.copy(em_bc[:, :], ps[:, 2, :]).then_inc(ml_em, 1)
                nc.scalar.copy(samp[:, 0:2, :], ps[:, 1, TS:3 * TS].rearrange("p (a n) -> p a n", a=2)).then_inc(ml_em, 1)
                for s in range(NT):
                    n = ROWS[s]
                    lo, hi = (P * s, S) if s < 4 else (0, TS)
                    act.wait_ge(ml_gap, q + 1)
                    if q >= 2:
                        act.wait_ge(ml_wqk, q - 1)
                        act.wait_ge(ml_vw, q - 1)
                    nc.scalar.activation(work[0:n, q % 2, lo:hi], work[0:n, 2 + q % 2, lo:hi], ACT.Exp, scale=-1.0).then_inc(ml_w, 1)
                    q += 1
            def exp_scores(u):
                h, t = divmod(u, NT)
                r, n = ROWS[t], (t + 1) * P if t < 4 else T
                act.wait_ge(at_max, u + 1)
                if u >= 2:
                    act.wait_ge(at_turned, u - 1)
                nc.scalar.activation(work[0:r, u % 2, 0:n], work[0:r, 2 + u % 2, 0:n], ACT.Exp, bias=amax[0:r, u % 2:u % 2 + 1],
                                     accum_out=asum[0:r, u % 2:u % 2 + 1]).then_inc(at_exp, 1)

            def copy_turned(u):
                h, t = divmod(u, NT)
                act.wait_ge(at_turned, u + 1)
                if u >= 2:
                    act.wait_ge(at_pv, u - 1)
                if t < 4:
                    nc.scalar.copy(pT[:, u % 2, 0:t + 1, :], ps[:, 6, 0:(t + 1) * P].rearrange("p (s n) -> p s n", n=P)).then_inc(at_copied, 1)
                else:
                    nc.scalar.copy(pT[:, u % 2, 0:4, 0:TS], ps[:, 6, 0:4 * TS].rearrange("p (s n) -> p s n", n=TS))
                    nc.scalar.copy(pT[0:TS, u % 2, 4, 0:TS], ps[0:TS, 6, 4 * TS:5 * TS]).then_inc(at_copied, 1)
            for u in range(AH * NT + 1):
                if u < AH * NT:
                    exp_scores(u)
                if u >= 1:
                    copy_turned(u - 1)

        @block.vector
        def _(dve):
            nc.vector.memset(k.ones[:, :], 1.0).then_inc(vec_const, 1)
            nc.vector.memset(k.ss[:, :], 1.0).then_inc(vec_const, 1)
            dve.wait_ge(squared, NT)
            link = linker(dve, vec_chain)
            link(nc.vector.tensor_scalar(k.rstd[:, 0:NT], k.ss[:, 0:NT], 1.0 / D, EPS, ALU.mult, ALU.add))
            dve.wait_ge(rooted, 1)
            link(nc.vector.reciprocal(k.rstd[:, 0:NT], k.ss[:, 0:NT]))
            for t in range(NT):
                r = ROWS[t]
                nc.vector.tensor_scalar(xn[0:r, t, :], x[0:r, t, :], k.rstd[0:r, t:t + 1], None, ALU.mult).then_inc(normed, 1)
            dve.wait_ge(const_loaded, 144)
            for u, (kind, arg, who) in enumerate(units):
                if kind == "mk" and arg == (1, 0, 0):
                    ev, n = evicted(last("line"))
                    dve.wait_ge(ev, n)
                    nc.vector.tensor_scalar(line[:, 0:S].rearrange("p (a b) -> p a b", b=P), bcast(k.ones[0:AH, :], 1, S // P),
                                            line[:, S:S + 1], None, ALU.mult).then_inc(line_done, 1)
                if who != "vec":
                    continue
                dve.wait_ge(unit_done, u + 1)
                b = u % BANKS
                if kind == "xn":
                    t, g = arg
                    r = ROWS[t]
                    ins = nc.vector.tensor_tensor(xnT[:, 4 * g:4 * g + 4, t * P:t * P + r],
                                                  ps[:, b, :].rearrange("p (g n) -> p g n", g=4)[:, :, 0:r],
                                                  bcast(g1[:, 4 * g:4 * g + 4], 2, r), ALU.mult)
                elif kind in ("mv", "av"):
                    c, t = arg
                    r = ROWS[t]
                    ins = nc.vector.tensor_tensor(chunks[c][2][0:r, t, :], ps[0:r, b, :], (b_mv if kind == "mv" else b_av)[0:r, :], ALU.add)
                else:
                    c, m, h = arg
                    col = chunks[c][1] // P + m
                    ins = nc.vector.tensor_scalar(chunks[c][2][:, m, h * HALF:(h + 1) * HALF], ps[:, b, 0:HALF],
                                                  b_col[:, col:col + 1], ML_SCALE if kind == "mk" else AD ** -0.5, ALU.add, ALU.mult)
                ins.then_inc(vec_evicted, 1)
            ev, n = evicted(last("gate"))
            dve.wait_ge(ev, n)
            link(nc.vector.tensor_scalar(row[:, 1, :], row[:, 1, :], small[:, 2:3], None, ALU.add))
            link(nc.vector.tensor_scalar(row[:, 4, :], row[:, 1, :], -1.0, None, ALU.mult))
            nc.vector.tensor_tensor(row[:, 2, :], row[:, 1, :], row[:, 4, :], ALU.max).then_inc(gate_vec, 1)
            dve.wait_ge(gate_act, 1)
            nc.vector.tensor_scalar(row[:, 2, :], row[:, 3, :], 1.0, None, ALU.add).then_inc(gate_vec, 1)
            dve.wait_ge(gate_act, 2)
            link(nc.vector.scalar_tensor_tensor(out=row[:, 2, :], in0=row[:, 1, :], scalar=0.0, in1=row[:, 3, :], op0=ALU.min, op1=ALU.subtract))
            link(nc.vector.memset(row[:, 5, :], 1.0))
            for lo, hi in ((0, S), (S, T)):
                link(nc.vector.tensor_tensor_scan(row[:, 3, lo:hi], row[:, 5, lo:hi], row[:, 2, lo:hi], 0.0, ALU.mult, ALU.add))
            link(nc.vector.tensor_tensor(row[:, 1, :], row[:, 0, :], row[:, 3, :], ALU.subtract))
            for lo, hi, first in ((0, S, NEG), (S, T, small[:, 3:4])):
                link(nc.vector.tensor_tensor_scan(row[:, 5, lo:hi], row[:, 1, lo:hi], row[:, 1, lo:hi], first, ALU.max, ALU.max))
            link(nc.vector.tensor_tensor(row[:, 4, :], row[:, 3, :], row[:, 5, :], ALU.add))
            nc.vector.tensor_scalar(row[:, 2, S:T], row[:, 5, S:T], small[:, 3:4], None, ALU.subtract).then_inc(gate_vec, 1)
            dve.wait_ge(c_turned, 1)
            nc.vector.tensor_copy(c_col[:, 0:4, :], ps[:, 7, 0:16].rearrange("p (t h) -> p t h", h=MH)).then_inc(c_copied, 1)
            nc.vector.tensor_copy(c_col[0:TS, 4, :], ps[0:TS, 7, 16:20]).then_inc(c_copied, 1)
            dve.wait_ge(c_copied, 2)

            def gap(q):
                h, s = divmod(q, NT)
                n = ROWS[s]
                lo, hi = (P * s, S) if s < 4 else (0, TS)
                if s == 0:
                    dve.wait_ge(ml_rows, h + 1)
                if q >= 2:
                    dve.wait_ge(ml_w, q - 1)
                nc.vector.tensor_scalar(work[0:n, 2 + q % 2, lo:hi], ps[0:n, 0 if s < 4 else 1, lo:hi], c_col[0:n, s, h:h + 1], 0.0,
                                        ALU.subtract, ALU.max).then_inc(ml_gap, 1)

            def weigh(q):
                h, s = divmod(q, NT)
                n = ROWS[s]
                lo, hi = (P * s, S) if s < 4 else (0, TS)
                dve.wait_ge(ml_masked, q + 1)
                dve.wait_ge(ml_qk, q + 1)
                if q >= 2:
                    dve.wait_ge(ml_used, q - 1)
                end = work[0:n, q % 2, hi - 1:hi]
                nc.vector.tensor_scalar(vw[0:n, q % 2, 0:P], mv_nat[0:n, s, h * P:(h + 1) * P], end, None, ALU.mult)
                nc.vector.tensor_copy(vw[0:n, q % 2, P:P + 1], end).then_inc(ml_vw, 1)
                nc.vector.tensor_tensor(wqk_of(q)[0:n, lo:hi], work[0:n, q % 2, lo:hi], ps[0:n, 3 + q % 2, lo:hi], ALU.mult).then_inc(ml_wqk, 1)

            for h in range(MH):
                dve.wait_ge(ml_em, 2 * h + 2)
                dve.wait_ge(ml_qk, NT * h + 1)
                link(nc.vector.tensor_tensor(samp[:, 2, :], mqT[:, h, S:T], samp[:, 0, :], ALU.mult))
                nc.vector.tensor_scalar(n_rep[:, :], k.ones[:, :], state[:, h, P:P + 1], None, ALU.mult).then_inc(ml_sample, 1)
                gap(NT * h)
                for s in range(NT):
                    if s + 1 < NT:
                        gap(NT * h + s + 1)
                    weigh(NT * h + s)
                dve.wait_ge(ml_used, NT * h + 4)
                link(nc.vector.scalar_tensor_tensor(out=em_bc[:, :], in0=ps[:, 6, :], scalar=-1.0, in1=em_bc[:, :], op0=ALU.mult, op1=ALU.max))
                link(nc.vector.tensor_tensor(em_bc[:, :], ps[:, 6, :], em_bc[:, :], ALU.max))
                link(nc.vector.reciprocal(em_bc[:, :], em_bc[:, :]))
                nc.vector.tensor_tensor(mqT[:, h, 0:S], ps[:, 5, :], em_bc[:, :], ALU.mult)
                nc.vector.tensor_copy(c_out[:, h, :], ps[:, 7, 0:P + 1]).then_inc(ml_head, 1)
                dve.wait_ge(ml_used, NT * h + 5)
                link(nc.vector.scalar_tensor_tensor(out=samp[:, 1, :], in0=ps[:, 2, TS:2 * TS], scalar=-1.0, in1=samp[:, 1, :], op0=ALU.mult, op1=ALU.max))
                link(nc.vector.tensor_tensor(samp[:, 1, :], ps[:, 2, TS:2 * TS], samp[:, 1, :], ALU.max))
                link(nc.vector.reciprocal(samp[:, 1, :], samp[:, 1, :]))
                nc.vector.tensor_tensor(mqT[:, h, S:T], ps[:, 2, 0:TS], samp[:, 1, :], ALU.mult)
                nc.vector.scalar_tensor_tensor(out=state[:, h, :], in0=state[:, h, :], scalar=samp[:, 0, TS - 1:TS], in1=ps[:, 2, 128:129 + P],
                                               op0=ALU.mult, op1=ALU.add).then_inc(ml_head, 1)
            dve.wait_ge(bias_loaded, 16 * AH)
            nc.vector.memset(bias[0:CHUNK, :, BW - CHUNK:BW], NEG).then_inc(bias_masked, 1)
            dve.wait_ge(bias_masked, 1)

            def add_bias(u):
                h, t = divmod(u, NT)
                r, n = ROWS[t], (t + 1) * P if t < 4 else S
                off = BW - n if t < 4 else 0
                dve.wait_ge(at_scored, u + 1)
                if u >= 2:
                    dve.wait_ge(at_exp, u - 1)
                sc = work[0:r, 2 + u % 2, :]
                ins = nc.vector.tensor_tensor(sc[:, 0:n], ps[0:r, 4 + u % 2, 0:n], bias[0:r, h, off:off + n], ALU.add)
                n_inc = 1
                if t == 4:
                    ins.then_inc(at_added, 1)
                    ins = nc.vector.tensor_tensor(sc[:, S:T], ps[0:TS, 3, 0:TS], bias[0:TS, h, S:T], ALU.add)
                ins.then_inc(at_added, 1)
                dve.wait_ge(at_added, u + 1 + sum(1 for v in range(u + 1) if v % NT == 4))
                nc.vector.tensor_reduce(amax[0:r, u % 2:u % 2 + 1], sc[:, 0:n if t < 4 else T], AX.X, ALU.max, negate=True).then_inc(at_max, 1)

            def normalise(u):
                h, t = divmod(u, NT)
                r, n = ROWS[t], (t + 1) * P if t < 4 else T
                dve.wait_ge(at_exp, u + 1)
                link(nc.vector.reciprocal(asum[0:r, 2 + u % 2:3 + u % 2], asum[0:r, u % 2:u % 2 + 1]))
                nc.vector.tensor_scalar(work[0:r, u % 2, 0:n], work[0:r, u % 2, 0:n], asum[0:r, 2 + u % 2:3 + u % 2], None, ALU.mult).then_inc(at_norm, 1)

            def take_out(u):
                h, t = divmod(u, NT)
                r, lo = ROWS[t], AD * (h % 2)
                dve.wait_ge(at_pv, u + 1)
                nc.vector.tensor_copy(aqT[lo:lo + AD, h // 2, t * P:t * P + r], ps[lo:lo + AD, 7, 0:r]).then_inc(at_out, 1)
            for u in range(AH * NT + 2):
                if u < AH * NT:
                    add_bias(u)
                if 1 <= u <= AH * NT:
                    normalise(u - 1)
                if u >= 2:
                    take_out(u - 2)

        @block.tensor
        def _(pe):
            pe.wait_ge(pool_const, 7)
            pe.wait_ge(tab_loaded, 32)
            pe.wait_ge(cache_loaded, 16)
            pe.wait_ge(wg_loaded, 16)
            pe.wait_ge(vec_const, 2)
            for u, (kind, arg, who) in enumerate(units):
                if u >= BANKS:
                    pe.wait_ge(*evicted(u - BANKS))
                b = u % BANKS
                if kind == "xn":
                    t, g = arg
                    r = ROWS[t]
                    pe.wait_ge(normed, t + 1)
                    for i in range(4):
                        kk = 4 * g + i
                        ins = nc.tensor.transpose(ps[:, b, i * P:i * P + r], xn[0:r, t, kk * P:(kk + 1) * P], ident[0:r, 0:r])
                elif kind == "cache":
                    for i in range(4):
                        ins = nc.tensor.transpose(ps[:, b, i * P:(i + 1) * P], kc_nat[:, arg, i * P:(i + 1) * P], ident[:, :])
                elif kind == "line":
                    ins = nc.tensor.matmul(ps[0:AH, b, 0:P], table[:, arg, :], flip[:, :], start=True, stop=True)
                elif kind == "gate":
                    i, h = arg
                    for kk in range(KD):
                        ins = nc.tensor.matmul(ps[0:MH, b, 0:HALF], w_gate[:, kk, i * MH:(i + 1) * MH], xnT[:, kk, h * HALF:(h + 1) * HALF],
                                               start=(kk == 0), stop=(kk == KD - 1))
                elif kind in ("mk_turn", "ak_turn"):
                    src = mkT if kind == "mk_turn" else akT
                    r = ROWS[arg]
                    if arg == 0:
                        pe.wait_ge(*evicted(last(kind[:2])))
                    for i in range(4):
                        ins = nc.tensor.transpose(ps[0:r, b, i * P:(i + 1) * P], src[:, i, arg * P:arg * P + r], ident[:, :])
                else:
                    c = arg[0]
                    if c == 0:
                        pe.wait_ge(*evicted(last("xn")))
                    pe.wait_ge(w_loaded[c % 2], 16 * (c // 2 + 1))
                    if kind in ("mv", "av"):
                        r = ROWS[arg[1]]
                        for kk in range(KD):
                            ins = nc.tensor.matmul(ps[0:r, b, :], xnT[:, kk, arg[1] * P:arg[1] * P + r], w[:, c % 2, kk, :],
                                                   start=(kk == 0), stop=(kk == KD - 1))
                    else:
                        _, m, h = arg
                        for kk in range(KD):
                            ins = nc.tensor.matmul(ps[:, b, 0:HALF], w[:, c % 2, kk, m * P:(m + 1) * P], xnT[:, kk, h * HALF:(h + 1) * HALF],
                                                   start=(kk == 0), stop=(kk == KD - 1))
                ins.then_inc(unit_done, 1)
            for u in range(len(units) - BANKS, len(units)):
                pe.wait_ge(*evicted(u))
            pe.wait_ge(gate_vec, 3)
            for t in range(NT):
                r = ROWS[t]
                ins = nc.tensor.transpose(ps[0:r, 7, t * MH:(t + 1) * MH], row[:, 1, t * P:t * P + r], ident[0:MH, 0:MH])
            ins.then_inc(c_turned, 1)
            pe.wait_ge(gate_act, 4)

            def scores(q):
                h, s = divmod(q, NT)
                n = ROWS[s]
                lo, hi = (P * s, S) if s < 4 else (0, TS)
                if q >= 2:
                    pe.wait_ge(ml_wqk, q - 1)
                nc.tensor.matmul(ps[0:n, 3 + q % 2, lo:hi], mkT[:, h, s * P:s * P + n], mqT[:, h, (s * P if s < 4 else S):(S if s < 4 else T)],
                                 start=True, stop=True).then_inc(ml_qk, 1)
            for h in range(MH):
                if h == 0:
                    pe.wait_ge(c_copied, 2)
                else:
                    pe.wait_ge(ml_head, 2 * h)
                nc.tensor.matmul(ps[:, 0, :], heads[:, h, :], row[:, 5, 0:S], start=True, stop=True)
                for i, r in enumerate((5, 0, 6)):
                    nc.tensor.matmul(ps[:, 1, i * TS:(i + 1) * TS], heads[:, h, :], row[:, r, S:T], start=True, stop=True)
                nc.tensor.matmul(ps[:, 2, :], heads[:, h, :], row[:, 6, 0:S], start=True, stop=True).then_inc(ml_rows, 1)
                scores(NT * h)
                for s in range(NT):
                    q = NT * h + s
                    n = ROWS[s]
                    if s + 1 < NT:
                        scores(q + 1)
                    pe.wait_ge(ml_wqk, q + 1)
                    pe.wait_ge(ml_vw, q + 1)
                    wqk = wqk_of(q)
                    vh = mv_nat[0:n, s, h * P:(h + 1) * P]
                    kh = mk_nat[0:n, s, h * P:(h + 1) * P]
                    if s < 4:
                        nc.tensor.matmul(ps[:, 5, s * P:S], vh, wqk[:, s * P:S], start=(s == 0), stop=(s == 3))
                        nc.tensor.matmul(ps[:, 6, s * P:S], k.ones[:, :], wqk[:, s * P:S], start=(s == 0), stop=(s == 3))
                        nc.tensor.matmul(ps[:, 7, 0:P + 1], kh, vw[:, q % 2, :], start=(s == 0), stop=(s == 3)).then_inc(ml_used, 1)
                    else:
                        pe.wait_ge(ml_sample, h + 1)
                        pe.wait_ge(ml_em, 2 * h + 2)
                        nc.tensor.matmul(ps[:, 2, 0:TS], vh, wqk[0:n, 0:TS], start=True, stop=False)
                        nc.tensor.matmul(ps[:, 2, 0:TS], state[:, h, 0:P], samp[:, 2, :], start=False, stop=True)
                        nc.tensor.matmul(ps[:, 2, TS:2 * TS], k.ones[0:n, :], wqk[0:n, 0:TS], start=True, stop=False)
                        nc.tensor.matmul(ps[:, 2, TS:2 * TS], n_rep[:, :], samp[:, 2, :], start=False, stop=True)
                        nc.tensor.matmul(ps[:, 2, P:2 * P + 1], kh, vw[0:n, q % 2, :], start=True, stop=True).then_inc(ml_used, 1)
            pe.wait_ge(ml_head, 2 * MH)

            def att_scores(u):
                h, t = divmod(u, NT)
                r, n, lo = ROWS[t], (t + 1) * P, AD * (h % 2)
                if u >= 2:
                    pe.wait_ge(at_max, u - 1)
                qh = aqT[lo:lo + AD, h // 2, t * P:t * P + r]
                if t < 4:
                    nc.tensor.matmul(ps[0:r, 4 + u % 2, 0:n], qh, akT[lo:lo + AD, h // 2, 0:n], start=True, stop=True).then_inc(at_scored, 1)
                else:
                    nc.tensor.matmul(ps[0:r, 4 + u % 2, 0:S], qh, kcT[lo:lo + AD, h // 2, :], start=True, stop=True)
                    nc.tensor.matmul(ps[0:r, 3, 0:TS], qh, akT[lo:lo + AD, h // 2, S:T], start=True, stop=True).then_inc(at_scored, 1)

            def turn(u):
                h, t = divmod(u, NT)
                r = ROWS[t]
                pe.wait_ge(at_norm, u + 1)
                if u >= 1:
                    pe.wait_ge(at_copied, u)
                for s in range(t + 1):
                    n = ROWS[s]
                    ins = nc.tensor.transpose(ps[0:n, 6, s * r:(s + 1) * r], work[0:r, u % 2, s * P:s * P + n], ident[0:r, 0:r])
                ins.then_inc(at_turned, 1)

            def weigh_values(u):
                h, t = divmod(u, NT)
                r, lo = ROWS[t], AD * (h % 2)
                if t == 4:
                    pe.wait_ge(vc_loaded, 16)
                pe.wait_ge(at_copied, u + 1)
                if u >= 1:
                    pe.wait_ge(at_out, u)
                for s in range(t + 1):
                    n = ROWS[s]
                    v = (av_nat if t < 4 or s == 4 else vc)[0:n, s, h * AD:(h + 1) * AD]
                    ins = nc.tensor.matmul(ps[lo:lo + AD, 7, 0:r], v, pT[0:n, u % 2, s, 0:r], start=(s == 0), stop=(s == t))
                ins.then_inc(at_pv, 1)
            for u in range(AH * NT + 2):
                if u < AH * NT:
                    att_scores(u)
                if 1 <= u <= AH * NT:
                    turn(u - 1)
                if u >= 2:
                    weigh_values(u - 2)




def merge(nc, k, hold, w_in, b_in, w_att_branch, w_ml_branch, w_out):
    ps, x, xnT, aqT, mqT = k.ps, k.x, k.xnT, k.aqT, k.mqT
    sem = k.sem
    RING = 4
    w = hold("w2", [P, RING, KD, 512])
    w_att = hold("w_att", [P, 4, D])
    w_ml = hold("w_ml", [P, 4, D])
    b_mo = hold("b_mo", [P, 4])
    b_gates = hold("b_gates", [P, 16])
    sig = hold("sig", [P, 4, 512])
    merged = hold("merged", [P, KD, T])
    w_loaded = [sem(f"merge_w_loaded{i}") for i in range(RING)]
    b_loaded, branch_loaded = sem("merge_b_loaded"), sem("branch_loaded")
    mo_done, mo_sig, mo_used = sem("mo_done"), sem("mo_sig"), sem("mo_used")
    g_done, g_sig, a_done, a_used, summed = sem("g_done"), sem("g_sig"), sem("a_done"), sem("a_used"), sem("summed")
    out_done, out_added = sem("out_done"), sem("out_added")
    chunks = [w_in[0, :, c:c + 512] for c in (MO, GA, GB, GA + 512, GB + 512)] + [w_out[0, :, 0:512], w_out[0, :, 512:1024]]
    with nc.Block() as block:
        @block.sync
        def _(sp):
            for c in range(len(chunks)):
                if c == 1:
                    sp.dma_start(b_mo[:, :], b_in[0, MO:GATES].rearrange("(m p) -> p m", p=P)).then_inc(b_loaded, 16)
                    sp.dma_start(b_gates[:, :], b_in[0, GA:GA + 2 * D].rearrange("(m p) -> p m", p=P)).then_inc(b_loaded, 16)
                    sp.dma_start(w_att[:, :, :], w_att_branch[0].rearrange("(k p) n -> p k n", p=P)).then_inc(branch_loaded, 16)
                    sp.dma_start(w_ml[:, :, :], w_ml_branch[0].rearrange("(k p) n -> p k n", p=P)).then_inc(branch_loaded, 16)
                if c == 4:
                    sp.wait_ge(mo_done, 8)
                if c in (5, 6):
                    sp.wait_ge(a_done, 2 * 4 * 2)
                sp.dma_start(w[:, c % RING, :, :], chunks[c].rearrange("(k p) n -> p k n", p=P)).then_inc(w_loaded[c % RING], 16)

        @block.tensor
        def _(pe):
            pe.wait_ge(w_loaded[0], 16)
            for u in range(8):
                m, h = divmod(u, 2)
                if u >= 4:
                    pe.wait_ge(mo_sig, u - 3)
                for kk in range(KD):
                    ins = nc.tensor.matmul(ps[:, u % 4, 0:HALF], w[:, 0, kk, m * P:(m + 1) * P], xnT[:, kk, h * HALF:(h + 1) * HALF],
                                           start=(kk == 0), stop=(kk == KD - 1))
                ins.then_inc(mo_done, 1)
            pe.wait_ge(mo_sig, 8)
            pe.wait_ge(branch_loaded, 32)
            for u in range(16):
                j, h = divmod(u, 2)
                cols = slice(h * HALF, (h + 1) * HALF)
                for g in range(2):
                    c = 1 + g + 2 * (j // 4)
                    if j % 4 == 0 and h == 0:
                        pe.wait_ge(w_loaded[c % RING], 16 * (c // RING + 1))
                    if u >= 1:
                        pe.wait_ge(g_sig, 2 * (u - 1) + g + 1)
                    for kk in range(KD):
                        ins = nc.tensor.matmul(ps[:, g, 0:HALF], w[:, c % RING, kk, (j % 4) * P:(j % 4 + 1) * P], xnT[:, kk, cols],
                                               start=(kk == 0), stop=(kk == KD - 1))
                    ins.then_inc(g_done, 1)
                if u == 0:
                    pe.wait_ge(mo_used, 8)
                for g, (wb, src) in enumerate(((w_att, aqT), (w_ml, mqT))):
                    if u >= 2:
                        pe.wait_ge(a_used, 2 * (u - 2) + g + 1)
                    for kk in range(4):
                        ins = nc.tensor.matmul(ps[:, 4 + 2 * (u % 2) + g, 0:HALF], wb[:, kk, j * P:(j + 1) * P], src[:, kk, cols],
                                               start=(kk == 0), stop=(kk == 3))
                    ins.then_inc(a_done, 1)
            pe.wait_ge(summed, 16)
            for c in (5, 6):
                pe.wait_ge(w_loaded[c % RING], 16 * (c // RING + 1))
            for u in range(2 * NT):
                t, h = divmod(u, 2)
                r = ROWS[t]
                if u >= 4:
                    pe.wait_ge(out_added, u - 3)
                for kk in range(KD):
                    ins = nc.tensor.matmul(ps[0:r, u % 4, :], merged[:, kk, t * P:t * P + r], w[:, (5 + h) % RING, kk, :],
                                           start=(kk == 0), stop=(kk == KD - 1))
                ins.then_inc(out_done, 1)

        @block.scalar
        def _(act):
            act.wait_ge(b_loaded, 32)
            for u in range(8):
                m, h = divmod(u, 2)
                act.wait_ge(mo_done, u + 1)
                if u >= 4:
                    act.wait_ge(mo_used, u - 3)
                nc.scalar.activation(sig[:, u % 4, 0:HALF], ps[:, u % 4, 0:HALF], ACT.Sigmoid, bias=b_mo[:, m:m + 1]).then_inc(mo_sig, 1)
            act.wait_ge(mo_used, 8)
            for u in range(16):
                j = u // 2
                for g in range(2):
                    act.wait_ge(g_done, 2 * u + g + 1)
                    if u >= 2:
                        act.wait_ge(summed, u - 1)
                    nc.scalar.activation(sig[:, 2 * (u % 2) + g, 0:HALF], ps[:, g, 0:HALF], ACT.Sigmoid,
                                         bias=b_gates[:, 8 * g + j:8 * g + j + 1]).then_inc(g_sig, 1)

        @block.vector
        def _(dve):
            for u in range(8):
                m, h = divmod(u, 2)
                dve.wait_ge(mo_sig, u + 1)
                hT = mqT[:, m, h * HALF:(h + 1) * HALF]
                nc.vector.tensor_tensor(hT, hT, sig[:, u % 4, 0:HALF], ALU.mult).then_inc(mo_used, 1)
            for u in range(16):
                for g in range(2):
                    dve.wait_ge(g_sig, 2 * u + g + 1)
                    dve.wait_ge(a_done, 2 * u + g + 1)
                    gate = sig[:, 2 * (u % 2) + g, 0:HALF]
                    nc.vector.tensor_tensor(sig[:, 2 * (u % 2) + g, 0:HALF], ps[:, 4 + 2 * (u % 2) + g, 0:HALF], gate, ALU.mult).then_inc(a_used, 1)
                dve.wait_ge(a_used, 2 * u + 2)
                j, h = divmod(u, 2)
                nc.vector.tensor_tensor(merged[:, j, h * HALF:(h + 1) * HALF], sig[:, 2 * (u % 2), 0:HALF], sig[:, 2 * (u % 2) + 1, 0:HALF],
                                        ALU.add).then_inc(summed, 1)
            for u in range(2 * NT):
                t, h = divmod(u, 2)
                r = ROWS[t]
                dve.wait_ge(out_done, u + 1)
                xs = x[0:r, t, h * 512:(h + 1) * 512]
                nc.vector.tensor_tensor(xs, ps[0:r, u % 4, :], xs, ALU.add).then_inc(out_added, 1)


class Hidden:

    def __init__(self, nc, k, hold, peer_u):
        self.nc, self.k, self.peer_u = nc, k, peer_u
        self.u_nat = hold("u_nat", [P, QUAD, D])
        self.high = hold("uT_high", [P, 2, KD, P], F32R)
        self.low = hold("uT_low", [P, 2, KD, P], F32R)
        self.out = hold("gelu_out", [P, 2, T])
        self.u_loaded = [k.sem(f"u_loaded{v}") for v in range(QUAD)]
        self.turned, self.high_done, self.low_done = k.sem("u_turned"), k.sem("u_high_done"), k.sem("u_low_done")
        self.product_done, self.gelu_done = k.sem("u_product_done"), k.sem("gelu_done")
        self.stored = [k.sem("gelu_stored0"), k.sem("gelu_stored1")]

    def load(self, sp, q, v):
        n = QUAD * q + v
        after(sp, self.turned, n - QUAD + 1)
        sp.dma_start(self.u_nat[:, v, :], self.peer_u[0, ds(n * P, P), :]).then_inc(self.u_loaded[v], 16)

    def transpose(self, pe, q, v):
        n = QUAD * q + v
        pe.wait_ge(self.u_loaded[v], 16 * (q + 1))
        after(pe, self.low_done, 2 * n)
        for kk in range(KD):
            ins = self.nc.tensor.transpose(self.k.ps[:, kk // 4, (kk % 4) * P:(kk % 4 + 1) * P], self.u_nat[:, v, kk * P:(kk + 1) * P],
                                           self.k.ident[:, :])
        ins.then_inc(self.turned, 1)

    def split_high(self, act, q, v):
        n = QUAD * q + v
        act.wait_ge(self.turned, n + 1)
        after(act, self.product_done, n - 1)
        for g in range(2):
            self.nc.scalar.copy(self.high[:, v % 2, 4 * g:4 * g + 4, :], self.k.ps[:, g, :].rearrange("p (a n) -> p a n", a=4)).then_inc(self.high_done, 1)

    def split_low(self, dve, q, v):
        n = QUAD * q + v
        for g in range(2):
            dve.wait_ge(self.high_done, 2 * n + g + 1)
            self.nc.vector.tensor_tensor(self.low[:, v % 2, 4 * g:4 * g + 4, :], self.k.ps[:, g, :].rearrange("p (a n) -> p a n", a=4),
                                         self.high[:, v % 2, 4 * g:4 * g + 4, :], ALU.subtract).then_inc(self.low_done, 1)

    def product(self, pe, q, v):
        n, b = QUAD * q + v, v % 2
        pe.wait_ge(self.low_done, 2 * n + 2)
        after(pe, self.gelu_done, n - 1)
        for h in range(2):
            for kk in range(KD):
                cols = slice(h * HALF, (h + 1) * HALF)
                for p, (w, x) in enumerate(((self.high, self.k.x_high), (self.high, self.k.x_low), (self.low, self.k.x_high))):
                    ins = self.nc.tensor.matmul(self.k.ps[:, 2 + 2 * b + h, 0:HALF], w[:, b, kk, :], x[:, kk, cols],
                                                start=(kk == 0 and p == 0), stop=(kk == KD - 1 and p == 2))
        ins.then_inc(self.product_done, 1)

    def gelu(self, act, q, v):
        n, b = QUAD * q + v, v % 2
        act.wait_ge(self.product_done, n + 1)
        after(act, self.stored[b], 16 * (2 * q + v // 2))
        self.nc.scalar.activation(self.out[:, b, :].rearrange("p (h n) -> p h n", h=2), self.k.ps[:, 2 + 2 * b:4 + 2 * b, 0:HALF], ACT.Gelu
                                  ).then_inc(self.gelu_done, 1)
        act.wait_ge(self.gelu_done, n + 1)
        act.dma_start(self.k.gelu_dram[ds(n, 1)].rearrange("a j n -> j (a n)"), self.out[:, b, :]).then_inc(self.stored[b], 16)

    def step(self, part, eng, q, v, last=False):
        more = not (last and v == QUAD - 1)
        nxt = (q, v + 1) if v + 1 < QUAD else (q + 1, 0)
        if part == "sync":
            if not last:
                self.load(eng, q + 1, v)
        elif part == "tensor":
            if more:
                self.transpose(eng, *nxt)
            self.product(eng, q, v)
        elif part == "scalar":
            if more:
                self.split_high(eng, *nxt)
            self.gelu(eng, q, v)
        elif part == "vector" and more:
            self.split_low(eng, *nxt)


def retrieve(nc, k, hold, hidden, norm2_g, peer_wq, peer_sub_keys):
    ps, x, ident, chosen = k.ps, k.x, k.ident, k.chosen
    sem = k.sem
    STEPS = 2 * QUAD
    xn2T = hold("xn2T", [P, KD, T])
    w = hold("wq", [P, 2, KD, 512])
    g2 = hold("g2", [P, KD])
    xn = hold("xn_b", [P, NT, D])
    sk = hold("sk", [P, PH, P])
    skT = hold("skT", [P, PH, NK])
    qT = xn[:, :, :].rearrange("p t d -> p (t d)")[:, 0:PH * T].rearrange("p (h t) -> p h t", h=PH)
    space = w[:, :, :, :].rearrange("p c a b -> p (c a b)")
    SIDE = PH * NK
    sc = space[:, 0:2 * SIDE].rearrange("p (s h n) -> p s h n", s=2, h=PH)
    rest = space[:, 2 * SIDE:4 * SIDE].rearrange("p (s h n) -> p s h n", s=2, h=PH)
    one_hot = space[:, 4 * SIDE:6 * SIDE].rearrange("p (h a b) -> p h a b", h=PH, a=TOPK)
    q_tile = space[:, 6 * SIDE:7 * SIDE].rearrange("p (h n) -> p h n", h=PH)
    sv = hold("sv", [P, 2, PH, TOPK])
    si = hold("si", [P, 2, PH, TOPK], U32)
    sif = hold("sif", [P, 2, PH, TOPK])
    fv = hold("fv", [P, PH, TOPK])
    fi = hold("fi", [P, PH, TOPK], U32)
    pos = hold("pos", [P, 2, PH, TOPK], U32)
    posf = hold("posf", [P, 2, PH, TOPK])
    picked = hold("picked", [P, 3, P])
    total = hold("total", [P, 2, PH])
    loaded, wq_loaded = sem("retrieve_loaded"), sem("wq_loaded")
    squared, rooted, chain, normed = sem("squared2"), sem("rooted2"), sem("chain2"), sem("normed2")
    turned, vec_out, sk_done, sk_out = sem("turned2"), sem("vec_out2"), sem("sk_done"), sem("sk_out")
    q_done, q_out, q_copied, s_done, s_out = sem("q_done"), sem("q_out"), sem("q_copied"), sem("s_done"), sem("s_out")
    x_split, x_high_done = sem("x_split"), sem("x_high_done")
    tile_sorted, gap_done, exp_done, pick_done, pick_turned, pick_out = (sem(n) for n in (
        "tile_sorted", "gap_done", "exp_done", "pick_done", "pick_turned", "pick_out"))

    def tiles(eng, tile):
        for t in range(NT):
            tile(t, ROWS[t])

    with nc.Block() as block:
        @block.sync
        def _(sp):
            sp.dma_start(g2[:, :], norm2_g[0].rearrange("(k p) -> p k", p=P)).then_inc(loaded, 16)
            sp.dma_start(sk[:, :, :].rearrange("n h (s d) -> n h s d", s=2), peer_sub_keys[0].rearrange("h s n d -> n h s d")).then_inc(loaded, 16)
            for c in range(2):
                sp.dma_start(w[:, c, :, :], peer_wq[0, :, c * 512:(c + 1) * 512].rearrange("(k p) n -> p k n", p=P)).then_inc(wq_loaded, 16)
            for v in range(QUAD):
                hidden.load(sp, 0, v)

            def tile(t, r):
                for v in range(STEPS):
                    hidden.step("sync", sp, 2 * t + v // QUAD, v % QUAD)
            tiles(sp, tile)

        @block.scalar
        def _(act):
            for t in range(NT):
                r = ROWS[t]
                nc.scalar.activation(xn[0:r, t, :], x[0:r, t, :], ACT.Square, accum_out=k.ss[0:r, t:t + 1]).then_inc(squared, 1)
            act.wait_ge(chain, 1)
            nc.scalar.activation(k.ss[:, 0:NT], k.rstd[:, 0:NT], ACT.Sqrt).then_inc(rooted, 1)
            for g in range(2):
                act.wait_ge(sk_done, g + 1)
                nc.scalar.copy(skT[:, 4 * g:4 * g + 4, :], ps[:, 6 + g, :].rearrange("p (h n) -> p h n", h=4)).then_inc(sk_out, 1)
            act.wait_ge(vec_out, 2 * NT)
            for kk in range(KD):
                nc.scalar.copy(k.x_high[:, kk, :], xn2T[:, kk, :]).then_inc(x_high_done, 1)
            for u in range(2 * PH):
                act.wait_ge(q_done, u + 1)
                m, h = divmod(u, 2)
                nc.scalar.copy(qT[:, m, h * HALF:(h + 1) * HALF], ps[:, u % 4, 0:HALF]).then_inc(q_out, 1)
            act.wait_ge(q_out, 2 * PH)
            hidden.split_high(act, 0, 0)

            def tile(t, r):
                def step(v):
                    hidden.step("scalar", act, 2 * t + v // QUAD, v % QUAD)

                after(act, s_done, 2 * t)
                nc.scalar.copy(q_tile[:, :, 0:r], qT[:, :, ds(t * P, r)]).then_inc(q_copied, 1)
                for g in range(2):
                    act.wait_ge(s_done, 2 * t + g + 1)
                    if g == 0:
                        after(act, tile_sorted, t)
                    nc.scalar.copy(sc[0:r, :, 4 * g:4 * g + 4, :], ps[0:r, 6:8, :].rearrange("p s (h n) -> p s h n", h=4)).then_inc(s_out, 1)
                for v in range(STEPS - 1):
                    step(v)
                act.wait_ge(gap_done, t + 1)
                w3 = picked[0:r, 2, :]
                nc.scalar.activation(w3, w3, ACT.Exp).then_inc(exp_done, 1)
                step(STEPS - 1)
                act.wait_ge(pick_turned, t + 1)
                nc.scalar.copy(chosen[:, :, ds(t * P, r)], ps[:, 6, 0:3 * P].rearrange("p (a n) -> p a n", a=3)[:, :, 0:r]).then_inc(pick_out, 1)
            tiles(act, tile)

        @block.tensor
        def _(pe):
            for u in range(2 * NT):
                t, g = divmod(u, 2)
                r = ROWS[t]
                pe.wait_ge(normed, t + 1)
                if u >= 4:
                    pe.wait_ge(vec_out, u - 3)
                for i in range(4):
                    kk = 4 * g + i
                    ins = nc.tensor.transpose(ps[:, u % 4, i * P:i * P + r], xn[0:r, t, kk * P:(kk + 1) * P], ident[0:r, 0:r])
                ins.then_inc(turned, 1)
            pe.wait_ge(loaded, 32)
            for g in range(2):
                for i in range(4):
                    ins = nc.tensor.transpose(ps[:, 6 + g, i * P:(i + 1) * P], sk[:, 4 * g + i, :], ident[:, :])
                ins.then_inc(sk_done, 1)
            pe.wait_ge(vec_out, 2 * NT)
            pe.wait_ge(wq_loaded, 32)
            for u in range(2 * PH):
                m, h = divmod(u, 2)
                if u >= 4:
                    pe.wait_ge(q_out, u - 3)
                for kk in range(KD):
                    ins = nc.tensor.matmul(ps[:, u % 4, 0:HALF], w[:, m // 4, kk, (m % 4) * P:(m % 4 + 1) * P], xn2T[:, kk, h * HALF:(h + 1) * HALF],
                                           start=(kk == 0), stop=(kk == KD - 1))
                ins.then_inc(q_done, 1)
            pe.wait_ge(q_out, 2 * PH)
            pe.wait_ge(sk_out, 2)
            hidden.transpose(pe, 0, 0)
            pe.wait_ge(x_split, KD)

            def tile(t, r):
                pe.wait_ge(q_copied, t + 1)
                after(pe, pick_out, t)
                for g in range(2):
                    after(pe, s_out, 2 * t + g)
                    for h in range(4 * g, 4 * g + 4):
                        for s in range(2):
                            lo = CHUNK * s
                            ins = nc.tensor.matmul(ps[0:r, 6 + s, (h % 4) * NK:(h % 4 + 1) * NK], q_tile[lo:lo + CHUNK, h, 0:r],
                                                   skT[lo:lo + CHUNK, h, :], start=True, stop=True)
                    ins.then_inc(s_done, 1)
                for v in range(STEPS):
                    hidden.step("tensor", pe, 2 * t + v // QUAD, v % QUAD)
                pe.wait_ge(pick_done, t + 1)
                for i in range(3):
                    ins = nc.tensor.transpose(ps[:, 6, i * P:i * P + r], picked[0:r, i, :], ident[0:r, 0:r])
                ins.then_inc(pick_turned, 1)
            tiles(pe, tile)

        @block.vector
        def _(dve):
            start = linker(dve, chain)
            dve.wait_ge(squared, NT)
            start(nc.vector.tensor_scalar(k.rstd[:, 0:NT], k.ss[:, 0:NT], 1.0 / D, EPS, ALU.mult, ALU.add))
            dve.wait_ge(rooted, 1)
            start(nc.vector.reciprocal(k.rstd[:, 0:NT], k.ss[:, 0:NT]))
            for t in range(NT):
                r = ROWS[t]
                nc.vector.tensor_scalar(xn[0:r, t, :], x[0:r, t, :], k.rstd[0:r, t:t + 1], None, ALU.mult).then_inc(normed, 1)
            dve.wait_ge(loaded, 32)
            for u in range(2 * NT):
                t, g = divmod(u, 2)
                r = ROWS[t]
                dve.wait_ge(turned, u + 1)
                nc.vector.tensor_tensor(xn2T[:, 4 * g:4 * g + 4, t * P:t * P + r], ps[:, u % 4, :].rearrange("p (g n) -> p g n", g=4)[:, :, 0:r],
                                        bcast(g2[:, 4 * g:4 * g + 4], 2, r), ALU.mult).then_inc(vec_out, 1)
            for kk in range(KD):
                dve.wait_ge(x_high_done, kk + 1)
                nc.vector.tensor_tensor(k.x_low[:, kk, :], xn2T[:, kk, :], k.x_high[:, kk, :], ALU.subtract).then_inc(x_split, 1)
            hidden.split_low(dve, 0, 0)

            def sort_tile(t, r):
                base, count = LINKS * t, [0]

                def link(ins):
                    count[0] += 1
                    ins.then_inc(sorting, 1)
                    dve.wait_ge(sorting, base + count[0])

                def top16(values, left, best, index, done=None):
                    for v, b in zip(values, best):
                        ins = nc.vector.max(b[:, 0:8], v)
                    link(ins)
                    for v, l, b in zip(values, left, best):
                        ins = nc.vector.match_replace(l, b[:, 0:8], v, LOWEST)
                    link(ins)
                    yield
                    for v, b, i in zip(values, best, index):
                        ins = nc.vector.max_index(i[:, 0:8], b[:, 0:8], v)
                    if done is not None:
                        ins.then_inc(done, 1)
                    for l, b in zip(left, best):
                        ins = nc.vector.max(b[:, 8:16], l)
                    link(ins)
                    yield
                    for l, b, i in zip(left, best, index):
                        ins = nc.vector.max_index(i[:, 8:16], b[:, 8:16], l)
                    link(ins)

                dve.wait_ge(s_out, 2 * t + 2)
                both = [(s, h) for s in range(2) for h in range(PH)]
                yield from top16([sc[0:r, s, h, :] for s, h in both], [rest[0:r, s, h, :] for s, h in both],
                                 [sv[0:r, s, h, :] for s, h in both], [si[0:r, s, h, :] for s, h in both], tile_sorted)
                link(nc.vector.tensor_copy(sif[0:r], si[0:r]))
                flat = rest[0:r].rearrange("p s h n -> p (s h n)")
                link(nc.vector.tensor_tensor(flat.rearrange("p (h a b) -> p h a b", h=PH, a=TOPK), bcast(sv[0:r, 0], 3, TOPK),
                                             bcast(sv[0:r, 1], 2, TOPK), ALU.add))
                yield
                sums = flat.rearrange("p (h m) -> p h m", h=PH)
                spare = one_hot[0:r].rearrange("p h a b -> p h (a b)")
                yield from top16([sums[:, h, :] for h in range(PH)], [spare[:, h, :] for h in range(PH)],
                                 [fv[0:r, h, :] for h in range(PH)], [fi[0:r, h, :] for h in range(PH)])
                w3 = picked[0:r, 2, :].rearrange("p (h n) -> p h n", h=PH)
                after(dve, pick_turned, t)
                nc.vector.tensor_tensor(w3, fv[0:r], fv[0:r, :, 0:1].broadcast_to([r, PH, TOPK]), ALU.subtract).then_inc(gap_done, 1)
                link(nc.vector.tensor_scalar(pos[0:r, 0], fi[0:r], 4, None, ALU.logical_shift_right))
                link(nc.vector.tensor_scalar(pos[0:r, 1], fi[0:r], 15, None, ALU.bitwise_and))
                link(nc.vector.tensor_copy(posf[0:r], pos[0:r]))
                yield
                for s in range(2):
                    hot = one_hot[0:r].rearrange("p h a b -> p (h a) b")
                    at = bcast(posf[0:r, s].rearrange("p h a -> p (h a)"), 2, TOPK)
                    link(nc.vector.tensor_tensor(hot, at, bcast(k.iota[0:r, 0:TOPK], 1, PH * TOPK), ALU.is_equal))
                    link(nc.vector.tensor_tensor(one_hot[0:r], one_hot[0:r], bcast(sif[0:r, s], 2, TOPK), ALU.mult))
                    link(nc.vector.tensor_reduce(picked[0:r, s, :], hot, AX.X, ALU.add))
                    yield
                dve.wait_ge(exp_done, t + 1)
                link(nc.vector.tensor_reduce(total[0:r, 0], w3, AX.X, ALU.add))
                link(nc.vector.reciprocal(total[0:r, 1], total[0:r, 0]))
                nc.vector.tensor_tensor(w3, w3, bcast(total[0:r, 1], 2, TOPK), ALU.mult).then_inc(pick_done, 1)
                assert count[0] == LINKS

            LINKS = 4 + 2 + 4 + 3 + 6 + 2
            sorting = sem("sorting")

            def tile(t, r):
                v = 0
                for _ in sort_tile(t, r):
                    hidden.step("vector", dve, 2 * t + v // QUAD, v % QUAD)
                    v += 1
                assert v == STEPS
            tiles(dve, tile)


def route(nc, k, hold, hidden):
    ps, iota, chosen, route_dram = k.ps, k.iota, k.chosen, k.route_dram
    sem = k.sem
    FEW = 4
    BATCHES = GRP // FEW
    EARLY = 2 * NT
    first = hold("first", [P, BATCHES, FEW, P])
    second = hold("second", [P, BATCHES, FEW, P])
    index = hold("index", [P, 2, GRP // 2])
    dense = hold("dense", [P, 2, P, GRP])
    first_ready, second_ready, product_done, batch_out = (sem(n) for n in (
        "first_ready", "second_ready", "route_product_done", "batch_out"))
    group_stored = [sem("group_stored0"), sem("group_stored1")]

    def turns(eng, turn):
        turn(0, 0, 0)
        turn(1, 1, 0)
        with eng.Fori(1, NGRP // 2) as j:
            turn(2 * j, 0, j)
            turn(2 * j + 1, 1, j)
        turn(NGRP - 1, 0, NGRP // 2)

    def remaining(part, eng):
        with eng.Fori(EARLY + NGRP, P // QUAD - 1) as q:
            for v in range(QUAD):
                hidden.step(part, eng, q, v)
        for v in range(QUAD):
            hidden.step(part, eng, P // QUAD - 1, v, last=True)

    with nc.Block() as block:
        @block.gpsimd
        def _(pool):
            def turn(i, slot, filled):
                for half in range(2):
                    after(pool, product_done, (i - 1) * BATCHES + (half + 1) * BATCHES // 2)
                    nc.gpsimd.tensor_copy(index[:, half, :], chosen[:, 0, ds(i * GRP + half * GRP // 2, GRP // 2)])
                    pool.drain()
                    for v in range(GRP // 2):
                        b, f = half * BATCHES // 2 + v // FEW, v % FEW
                        ins = nc.gpsimd.tensor_scalar(first[:, b, f, :], iota[:, :], index[:, half, v:v + 1], None, ALU.is_equal)
                        if f == FEW - 1:
                            ins.then_inc(first_ready, 1)
            turns(pool, turn)

        @block.vector
        def _(dve):
            def turn(i, slot, filled):
                for b in range(BATCHES):
                    if b % 2 == 0:
                        hidden.step("vector", dve, EARLY + i, b // 2)
                    after(dve, product_done, (i - 1) * BATCHES + b + 1)
                    for f in range(FEW):
                        n = i * GRP + b * FEW + f
                        ins = nc.vector.tensor_scalar(second[:, b, f, :], iota[:, :], chosen[:, 1, ds(n, 1)], chosen[:, 2, ds(n, 1)],
                                                      ALU.is_equal, ALU.mult)
                    ins.then_inc(second_ready, 1)
            turns(dve, turn)
            remaining("vector", dve)

        @block.tensor
        def _(pe):
            def batch(i, b):
                pe.wait_ge(first_ready, i * BATCHES + b + 1)
                pe.wait_ge(second_ready, i * BATCHES + b + 1)
                after(pe, batch_out, i * BATCHES + b - 1)
                for f in range(FEW):
                    ins = nc.tensor.matmul(ps[:, 6 + b % 2, f * P:(f + 1) * P], second[:, b, f, :], first[:, b, f, :], start=True, stop=True)
                ins.then_inc(product_done, 1)

            def turn(i, slot, filled):
                for v in range(QUAD):
                    hidden.step("tensor", pe, EARLY + i, v)
                    batch(i, 2 * v)
                    batch(i, 2 * v + 1)
            turns(pe, turn)
            remaining("tensor", pe)

        @block.scalar
        def _(act):
            def turn(i, slot, filled):
                for b in range(BATCHES):
                    if b % 2 == 0:
                        hidden.step("scalar", act, EARLY + i, b // 2)
                    act.wait_ge(product_done, i * BATCHES + b + 1)
                    if b == 0:
                        after(act, group_stored[slot], 16 * filled)
                    nc.scalar.copy(dense[:, slot, :, b * FEW:(b + 1) * FEW].rearrange("p i n -> p n i"),
                                   ps[:, 6 + b % 2, :].rearrange("p (n i) -> p n i", n=FEW)).then_inc(batch_out, 1)
            turns(act, turn)
            remaining("scalar", act)
            for b in range(2):
                act.wait_ge(hidden.stored[b], 16 * P // 2)

        @block.sync
        def _(sp):
            def turn(i, slot, filled):
                for v in range(QUAD):
                    hidden.step("sync", sp, EARLY + i, v)
                sp.wait_ge(batch_out, (i + 1) * BATCHES)
                sp.dma_start(route_dram[ds(i, 1)].rearrange("a j i n -> j (a i n)"), dense[:, slot].rearrange("p i n -> p (i n)")
                             ).then_inc(group_stored[slot], 16)
            turns(sp, turn)
            remaining("sync", sp)
            sp.wait_ge(group_stored[0], 16 * (NGRP // 2 + 1))
            sp.wait_ge(group_stored[1], 16 * (NGRP // 2))


def experts(nc, k, hold, peer_v):
    ps, acc = k.ps, k.acc
    sem = k.sem
    QUADS = P // QUAD
    UNITS = 2 * KD
    BANKS = 8
    v_nat = hold("v_nat", [P, QUAD, D])
    v_high = hold("v_high", [P, 2, QUAD, D], F32R)
    v_low = hold("v_low", [P, 2, QUAD, D], F32R)
    gelu = hold("gelu_in", [P, 2, QUAD, T])
    routing = hold("routing_in", [P, 2, NGRP, QUAD, GRP])
    hid_high = hold("hid_high", [P, 2, QUAD, T], F32R)
    hid_low = hold("hid_low", [P, 2, QUAD, T], F32R)
    v_loaded = [sem(f"v_loaded{v}") for v in range(QUAD)]
    in_loaded = [sem("in_loaded0"), sem("in_loaded1")]
    cleared, v_high_done, v_low_done, hid_done, hid_high_done, hid_low_done, out_done, out_added = (sem(n) for n in (
        "acc_cleared", "v_high_done", "v_low_done", "hid_done", "hid_high_done", "hid_low_done", "expert_out_done", "expert_out_added"))

    def quads(eng, quad):
        for s in range(2):
            quad(s, s, 0)
        with eng.Fori(1, QUADS // 2) as j:
            for s in range(2):
                quad(2 * j + s, s, j)

    with nc.Block() as block:
        @block.sync
        def _(sp):
            def quad(q, s, j):
                after(sp, hid_low_done, QUAD * (q - 1))
                sp.dma_start(gelu[:, s], k.gelu_dram[ds(q * QUAD, QUAD)].rearrange("a j n -> j a n")).then_inc(in_loaded[s], 16)
                sp.dma_start(routing[:, s].rearrange("j g a n -> j g (a n)"),
                             k.route_dram[:, :, ds(q * QUAD, QUAD), :].rearrange("g j a n -> j g (a n)")).then_inc(in_loaded[s], 16)
                for v in range(QUAD):
                    after(sp, v_low_done, QUAD * (q - 1) + v + 1)
                    sp.dma_start(v_nat[:, v, :], peer_v[0, ds((q * QUAD + v) * P, P), :]).then_inc(v_loaded[v], 16)
            quads(sp, quad)

        @block.gpsimd
        def _(pool):
            nc.gpsimd.memset(acc[:, :, :], 0.0).then_inc(cleared, 1)

            def quad(q, s, j):
                for v in range(QUAD):
                    pool.wait_ge(v_high_done, QUAD * q + v + 1)
                    nc.gpsimd.tensor_tensor(v_low[:, s, v, :], v_nat[:, v, :], v_high[:, s, v, :], ALU.subtract).then_inc(v_low_done, 1)
            quads(pool, quad)

        @block.scalar
        def _(act):
            def quad(q, s, j):
                for v in range(QUAD):
                    act.wait_ge(v_loaded[v], 16 * (q + 1))
                    if v == 0:
                        after(act, out_done, UNITS * (q - 1))
                    nc.scalar.copy(v_high[:, s, v, :], v_nat[:, v, :]).then_inc(v_high_done, 1)
                    act.wait_ge(hid_done, QUAD * q + v + 1)
                    nc.scalar.copy(hid_high[:, s, v, :], gelu[:, s, v, :]).then_inc(hid_high_done, 1)
            quads(act, quad)

        @block.vector
        def _(dve):
            dve.wait_ge(cleared, 1)

            def weigh(q, s, j):
                dve.wait_ge(in_loaded[s], 32 * (j + 1))
                for v in range(QUAD):
                    g = gelu[:, s, v, :].rearrange("p (g n) -> p g n", g=NGRP)
                    nc.vector.tensor_tensor(g, g, routing[:, s, :, v, :], ALU.mult).then_inc(hid_done, 1)
                for v in range(QUAD):
                    dve.wait_ge(hid_high_done, QUAD * q + v + 1)
                    nc.vector.tensor_tensor(hid_low[:, s, v, :], gelu[:, s, v, :], hid_high[:, s, v, :], ALU.subtract).then_inc(hid_low_done, 1)

            def add(q):
                for o in range(UNITS):
                    kk, h = divmod(o, 2)
                    dve.wait_ge(out_done, q * UNITS + o + 1)
                    a = acc[:, kk, h * HALF:(h + 1) * HALF]
                    nc.vector.tensor_tensor(a, ps[:, o % BANKS, 0:HALF], a, ALU.add).then_inc(out_added, 1)

            weigh(0, 0, 0)
            weigh(1, 1, 0)
            add(0)
            with dve.Fori(1, QUADS // 2) as j:
                weigh(2 * j, 0, j)
                add(2 * j - 1)
                weigh(2 * j + 1, 1, j)
                add(2 * j)
            add(QUADS - 1)

        @block.tensor
        def _(pe):
            def quad(q, s, j):
                pe.wait_ge(v_low_done, QUAD * (q + 1))
                pe.wait_ge(hid_low_done, QUAD * (q + 1))
                for o in range(UNITS):
                    kk, h = divmod(o, 2)
                    after(pe, out_added, q * UNITS + o - BANKS + 1)
                    for v in range(QUAD):
                        w = slice(kk * P, (kk + 1) * P)
                        cols = slice(h * HALF, (h + 1) * HALF)
                        for p, (a, b) in enumerate(((v_high, hid_high), (v_high, hid_low), (v_low, hid_high))):
                            ins = nc.tensor.matmul(ps[:, o % BANKS, 0:HALF], a[:, s, v, w], b[:, s, v, cols],
                                                   start=(v == 0 and p == 0), stop=(v == QUAD - 1 and p == 2))
                    ins.then_inc(out_done, 1)
            quads(pe, quad)


def finish(nc, k, hold, final_g, y_prompt, y_sample):
    ps, x, acc, ident = k.ps, k.x, k.acc, k.ident
    sem = k.sem
    g = hold("g_final", [P, D])
    y = hold("y", [P, NT, D])
    loaded, turned, added, squared, rooted, chain, scaled, ready, stored = (sem(n) for n in (
        "final_loaded", "turned3", "added3", "squared3", "rooted3", "chain3", "scaled3", "y_ready", "y_stored"))
    with nc.Block() as block:
        @block.sync
        def _(sp):
            sp.dma_start(g[:, :], final_g.partition_broadcast(P)).then_inc(loaded, 16)
            for t in range(NT):
                sp.wait_ge(ready, t + 1)
                out = y_prompt[0, t * P:(t + 1) * P, :] if t < 4 else y_sample[0]
                sp.dma_start(out, y[0:ROWS[t], t, :]).then_inc(stored, 16)
            sp.wait_ge(stored, 16 * NT)

        @block.tensor
        def _(pe):
            for t in range(NT):
                r, b = ROWS[t], 2 * (t % 4)
                if t >= 4:
                    pe.wait_ge(added, t - 3)
                for kk in range(KD):
                    ins = nc.tensor.transpose(ps[0:r, b + kk // 4, (kk % 4) * P:(kk % 4 + 1) * P], acc[:, kk, t * P:t * P + r], ident[:, :])
                ins.then_inc(turned, 1)

        @block.scalar
        def _(act):
            for t in range(NT):
                r = ROWS[t]
                act.wait_ge(added, t + 1)
                nc.scalar.activation(y[0:r, t, :], x[0:r, t, :], ACT.Square, accum_out=k.ss[0:r, t:t + 1]).then_inc(squared, 1)
            act.wait_ge(chain, 1)
            nc.scalar.activation(k.ss[:, 0:NT], k.rstd[:, 0:NT], ACT.Sqrt).then_inc(rooted, 1)
            act.wait_ge(chain, 2)
            for t in range(NT):
                r = ROWS[t]
                nc.scalar.activation(y[0:r, t, :], x[0:r, t, :], ACT.Copy, scale=k.rstd[0:r, t:t + 1]).then_inc(scaled, 1)

        @block.vector
        def _(dve):
            for t in range(NT):
                r, b = ROWS[t], 2 * (t % 4)
                dve.wait_ge(turned, t + 1)
                nc.vector.tensor_tensor(x[0:r, t, :], ps[0:r, b:b + 2, :].rearrange("p b n -> p (b n)"), x[0:r, t, :], ALU.add).then_inc(added, 1)
            dve.wait_ge(squared, NT)
            link = linker(dve, chain)
            link(nc.vector.tensor_scalar(k.rstd[:, 0:NT], k.ss[:, 0:NT], 1.0 / D, EPS, ALU.mult, ALU.add))
            dve.wait_ge(rooted, 1)
            link(nc.vector.reciprocal(k.rstd[:, 0:NT], k.ss[:, 0:NT]))
            dve.wait_ge(loaded, 16)
            for t in range(NT):
                r = ROWS[t]
                dve.wait_ge(scaled, t + 1)
                nc.vector.tensor_tensor(y[0:r, t, :], y[0:r, t, :], g[0:r, :], ALU.mult).then_inc(ready, 1)


_INS = ['x_prompt', 'x_sample', 'cache_att_k', 'cache_att_v', 'state_mlstm_C', 'state_mlstm_n', 'state_mlstm_m',
        'norm1_g', 'w_in', 'b_in', 'ml_f_bias', 'att_rel_bias', 'w_att_branch', 'w_ml_branch', 'w_out',
        'norm2_g', 'peer_wq', 'peer_sub_keys', 'peer_u', 'peer_v', 'final_g']
_OUTS = [(1, S, D), (1, TS, D), (1, 1, S, AH, AD), (1, 1, S, AH, AD), (1, 1, MH, P, P), (1, 1, MH, P), (1, 1, MH),
         (1, 1, TS, AH, AD), (1, 1, TS, AH, AD), (1, 1, MH, P, P), (1, 1, MH, P), (1, 1, MH)]


def kernel(**inputs):
    import numpy as _np
    import concourse.bacc as _bacc
    from concourse import mybir as _mybir
    from concourse.bass_utils import run_bass_kernel_spmd as _run

    nc = _bacc.Bacc("TRN2", target_bir_lowering=False, num_devices=1)
    arrays, args = {}, []
    for name in _INS:
        a = _np.ascontiguousarray(inputs[name])
        arrays[f"in_{name}_dram"] = a
        args.append(nc.dram_tensor(f"in_{name}_dram", a.shape, _mybir.dt.from_np(a.dtype), kind="ExternalInput").ap())
    for i, shape in enumerate(_OUTS):
        args.append(nc.dram_tensor(f"out_{i}_dram", shape, F32, kind="ExternalOutput").ap())
    with nc.allow_non_contiguous_dma(reason="short vectors laid out as columns"):
        program(nc, *args)
    r = _run(nc, [arrays], core_ids=[0])
    return tuple(r.results[0][f"out_{i}_dram"] for i in range(len(_OUTS)))
```

```python
from contextlib import ExitStack

import concourse.bass as bass
from concourse import mybir
from concourse.bass import ds

ALU = mybir.AluOpType
ACT = mybir.ActivationFunctionType
F32 = mybir.dt.float32
BF16 = mybir.dt.bfloat16
F32R = mybir.dt.float32r
U32 = mybir.dt.uint32
AX = mybir.AxisListType

P = 128
D = 1024
KD = D // P
S = 512
TS = 32
T = S + TS
HALF = T // 2
ROWS = [P, P, P, P, TS]
NT = len(ROWS)
AH, AD = 8, 64
MH = 4
BW = S + P
NEG = -1e30
LOWEST = -3.0e38
EPS = 1e-6
PH, NK, TOPK = 8, 128, 16
CHUNK = 64
ML_SCALE = float(P) ** -0.5
QUARTERS, BLK = 4, 32
GRP = 32
NGRP = T // GRP
QUAD = 4
AQ, AK, AV, MQ, MK, MV, MO, GATES, GA, GB = 0, 512, 1024, 1536, 2048, 2560, 3072, 3584, 3592, 4616
GATE_TILES = 4 + 2 * KD


class Shared:
    pass


def bcast(ap, axis, n):
    u = ap.unsqueeze(axis)
    shape = list(u.shape)
    shape[axis] = n
    return u.broadcast_to(shape)


def after(eng, sem, value):
    if not (isinstance(value, int) and value <= 0):
        eng.wait_ge(sem, value)


def linker(eng, sem):
    count = [0]

    def link(ins):
        count[0] += 1
        ins.then_inc(sem, 1)
        eng.wait_ge(sem, count[0])
    return link


def program(nc, x_prompt, x_sample, cache_att_k, cache_att_v, state_mlstm_C, state_mlstm_n, state_mlstm_m,
            norm1_g, w_in, b_in, ml_f_bias, att_rel_bias, w_att_branch, w_ml_branch, w_out,
            norm2_g, peer_wq, peer_sub_keys, peer_u, peer_v, final_g,
            y_prompt, y_sample, att_k_prompt, att_v_prompt, C_prompt, n_prompt, m_prompt,
            att_k_sample, att_v_sample, C_sample, n_sample, m_sample):
    with ExitStack() as whole:
        def holder(stack):
            return lambda name, shape, dt=F32: stack.enter_context(nc.sbuf_tensor(name, shape, dt))

        keep = holder(whole)
        k = Shared()
        k.sem = lambda name: whole.enter_context(nc.semaphore(name))
        k.squared, k.averaged, k.rooted, k.inverted = (k.sem(n) for n in ("squared", "averaged", "rooted", "inverted"))
        k.ps = whole.enter_context(nc.psum_tensor("ps", [P, 8, 512], F32))
        k.ident = keep("ident", [P, P])
        k.iota = keep("iota_row", [P, P])
        k.ones = keep("ones", [P, P])
        k.x = keep("x", [P, NT, D])
        k.ss = keep("ss", [P, 8])
        k.rstd = keep("rstd", [P, 8])
        k.line_dram = nc.dram_tensor("rel_line", (AH, P, BW + P), F32, kind="Internal").ap()
        k.gates_dram = nc.dram_tensor("gates", (GATE_TILES, P, T), F32, kind="Internal").ap()
        k.gelu_dram = nc.dram_tensor("hidden", (P, P, T), F32, kind="Internal").ap()
        k.route_dram = nc.dram_tensor("routing", (NGRP, P, P, GRP), F32, kind="Internal").ap()
        with ExitStack() as early:
            hold = holder(early)
            k.aqT = hold("aqT", [P, 4, T])
            k.w_high = hold("w_high", [P, 2, KD, 2 * P], F32R)
            k.w_low = hold("w_low", [P, 2, KD, 2 * P], F32R)
            k.mqT = hold("mqT", [P, MH, T])
            with ExitStack() as now:
                project(nc, k, holder(now), x_prompt, x_sample, cache_att_k, cache_att_v, state_mlstm_C,
                        state_mlstm_n, state_mlstm_m, norm1_g, w_in, b_in, ml_f_bias, att_rel_bias,
                        w_att_branch, w_ml_branch,
                        att_k_prompt, att_v_prompt, C_prompt, n_prompt, m_prompt,
                        att_k_sample, att_v_sample, C_sample, n_sample, m_sample)
            with ExitStack() as now:
                merge(nc, k, holder(now), x_prompt, x_sample, w_att_branch, w_ml_branch, w_out)
        k.v_nat = keep("v_nat", [P, QUAD, D])
        k.quad_in = keep("quad_in0", [P, 2, QUAD, T])
        k.gelu = k.quad_in[:, 0]
        k.routing = k.quad_in[:, 1].rearrange("p a t -> p (a t)").rearrange("p (g a n) -> p g a n", g=NGRP, a=QUAD)
        k.v_loaded = [k.sem(f"v_loaded{v}") for v in range(QUAD)]
        k.in_loaded = [k.sem("in_loaded0"), k.sem("in_loaded1")]
        with ExitStack() as late:
            hold = holder(late)
            k.x_high = hold("x_high", [P, KD, T], F32R)
            k.x_low = hold("x_low", [P, KD, T], F32R)
            k.chosen = hold("chosen", [P, 3, T])
            hidden = Hidden(nc, k, hold, peer_u)
            with ExitStack() as now:
                retrieve(nc, k, holder(now), hidden, norm2_g, peer_wq, peer_sub_keys)
            with ExitStack() as now:
                route(nc, k, holder(now), hidden, peer_v)
        k.acc = keep("acc", [P, KD, T])
        with ExitStack() as now:
            experts(nc, k, holder(now), peer_v)
        with ExitStack() as now:
            finish(nc, k, holder(now), final_g, y_prompt, y_sample)


def norm_scalar(nc, k, act, which, spare, ready, counts=None):
    base = NT * which
    for i in range(NT + 1):
        if i < NT:
            r = ROWS[i]
            if ready is not None:
                act.wait_ge(ready[i], counts[i])
            nc.scalar.activation(spare[0:r, i, :], k.x[0:r, i, :], ACT.Square, accum_out=k.ss[0:r, i:i + 1]).then_inc(k.squared, 1)
        if i >= 1:
            r = ROWS[i - 1]
            act.wait_ge(k.averaged, base + i)
            nc.scalar.activation(k.ss[0:r, i - 1:i], k.rstd[0:r, i - 1:i], ACT.Sqrt).then_inc(k.rooted, 1)


def norm_vector(nc, k, dve, which):
    base = NT * which
    for i in range(NT + 1):
        if i < NT:
            r = ROWS[i]
            dve.wait_ge(k.squared, base + i + 1)
            nc.vector.tensor_scalar(k.rstd[0:r, i:i + 1], k.ss[0:r, i:i + 1], 1.0 / D, EPS, ALU.mult, ALU.add).then_inc(k.averaged, 1)
        if i >= 1:
            r = ROWS[i - 1]
            dve.wait_ge(k.rooted, base + i)
            nc.vector.reciprocal(k.rstd[0:r, i - 1:i], k.ss[0:r, i - 1:i]).then_inc(k.inverted, 1)
            dve.wait_ge(k.inverted, base + i)
            yield i - 1


def xn_high(nc, bank, high, g, t, half):
    r = ROWS[t]
    for i in range(4):
        kk = 4 * half + i
        ins = nc.scalar.activation(high[:, kk, t * P:t * P + r], bank[:, i * P:i * P + r], ACT.Copy, scale=g[:, kk:kk + 1])
    return ins


def xn_low(nc, bank, high, low, g, t, half):
    r = ROWS[t]
    for i in range(4):
        kk = 4 * half + i
        ins = nc.vector.scalar_tensor_tensor(out=low[:, kk, t * P:t * P + r], in0=bank[:, i * P:i * P + r], scalar=g[:, kk:kk + 1],
                                             in1=high[:, kk, t * P:t * P + r], op0=ALU.mult, op1=ALU.subtract)
    return ins


def project(nc, k, hold, x_prompt, x_sample, cache_att_k, cache_att_v, state_mlstm_C, state_mlstm_n,
            state_mlstm_m, norm1_g, w_in, b_in, ml_f_bias, att_rel_bias, w_att_branch, w_ml_branch,
            att_k_prompt, att_v_prompt, C_prompt, n_prompt, m_prompt,
            att_k_sample, att_v_sample, C_sample, n_sample, m_sample):
    ps, x, aqT, mqT, ident = k.ps, k.x, k.aqT, k.mqT, k.ident
    xnT_high = hold("xnT_high", [P, KD, T], F32R)
    xnT_low = hold("xnT_low", [P, KD, T], F32R)
    sem = k.sem
    akT = hold("akT", [P, 4, T])
    mkT = hold("mkT", [P, MH, T])
    kv = x[:, :, :].rearrange("p t d -> p (t d)").rearrange("p (i t d) -> p i t d", i=2, t=NT)
    ak_nat, av_nat = kv[:, 0], kv[:, 1]
    mk_nat = hold("mk_nat", [P, NT, 512])
    mv_nat = hold("mv_nat", [P, NT, 512])
    kc_nat = mv_nat[:, 0:4, :]
    vc = mk_nat[:, 0:4, :]
    kcT = hold("kcT", [P, 4, S])
    w_raw = hold("w_raw", [P, 2, KD, P])
    w_high, w_low = k.w_high, k.w_low
    wg_raw = hold("wg_raw", [P, KD, 8])
    wg_high = hold("wg_high", [P, KD, 8], F32R)
    wg_low = hold("wg_low", [P, KD, 8], F32R)
    bias = hold("bias", [P, AH, BW])
    space = bias[:, :, :].rearrange("p h j -> p (h j)")
    xn = space.rearrange("p (t d) -> p t d", t=NT)
    row = space[0:MH, 0:7 * T].rearrange("p (r t) -> p r t", r=7)
    em_bc = space[:, 7 * T:7 * T + S]
    M_bc = space[:, 7 * T + S:7 * T + 2 * S]
    pT = hold("pT", [P, 2, NT, P])
    z_out = mkT[:, :, :].rearrange("p m t -> p (m t)")[:, 0:T].rearrange("p (b t) -> p b t", b=2)
    g1 = hold("g1", [P, KD])
    b_col = hold("b_col", [P, 28])
    b_aq = hold("b_aq", [P, 4])
    b_gates = hold("b_gates", [P, 2 * KD])
    b_av = hold("b_av", [P, 512])
    b_mv = hold("b_mv", [P, 512])
    table = hold("table", [P, 2, AH])
    flip = hold("flip", [P, P])
    heads = hold("heads", [MH, MH, P])
    small = hold("small", [MH, 8])
    c_col = hold("c_col", [P, NT, MH])
    work = hold("work", [P, 4, T])
    line = work[:, :, :].rearrange("p a t -> p (a t)")[0:AH, 0:BW + P]
    vw = hold("vw", [P, 2, P + 1])
    samp = hold("samp", [P, 4, TS])
    state = hold("state", [P, MH, P + 1])
    n_rep = hold("n_rep", [P, P])
    c_out = hold("c_out", [P, MH, P + 1])
    amax = hold("amax", [P, 4])
    asum = hold("asum", [P, 4])

    x_loaded = [sem(f"x_loaded{t}") for t in range(NT)]
    const_loaded, cache_loaded, tab_loaded = sem("const_loaded"), sem("cache_loaded"), sem("tab_loaded")
    raw_loaded = [sem("raw_loaded0"), sem("raw_loaded1")]
    w_high_done, w_low_done, wg_split = sem("w_high_done"), sem("w_low_done"), sem("wg_split")
    z_done, z_evicted, m_stored = sem("z_done"), sem("z_evicted"), sem("m_stored")
    z_stored = [sem("z_stored0"), sem("z_stored1")]
    vc_loaded, wg_loaded, line_stored, stored = sem("vc_loaded"), sem("wg_loaded"), sem("line_stored"), sem("stored")
    bias_loaded = [sem(f"bias_loaded{h}") for h in range(AH)]
    pool_const, vec_const = sem("pool_const"), sem("vec_const")
    g1_loaded, vec_chain, high_out = sem("g1_loaded"), sem("vec_chain"), sem("xn_high_out")
    normed, line_done = sem("normed"), sem("line_done")
    unit_done, vec_evicted, act_evicted = sem("unit_done"), sem("vec_evicted"), sem("act_evicted")
    gate_vec, gate_act = sem("gate_vec"), sem("gate_act")
    side_done, side_vec, side_act, aq_bias = sem("side_done"), sem("side_vec"), sem("side_act"), sem("aq_bias")
    c_turned, c_copied = sem("c_turned"), sem("c_copied")
    ml_rows, ml_em, ml_qk, ml_gap, ml_w, ml_masked, ml_wqk, ml_vw = (sem(n) for n in (
        "ml_rows", "ml_em", "ml_qk", "ml_gap", "ml_w", "ml_masked", "ml_wqk", "ml_vw"))
    ml_used, ml_sample, ml_head = sem("ml_used"), sem("ml_sample"), sem("ml_head")
    at_scored, at_max, at_exp, at_norm, at_turned, at_copied, at_pv, at_out = (sem(n) for n in (
        "at_scored", "at_max", "at_exp", "at_norm", "at_turned", "at_copied", "at_pv", "at_out"))
    at_added = sem("at_added")
    bias_masked = sem("bias_masked")

    units = [("xn", (t, g), "vec") for t in range(NT) for g in range(2)]
    units += [("cache", s, "act") for s in range(4)]
    units += [("line", i, "act") for i in range(2)]
    sections = [("mq", MQ, mqT, "act"), ("mk", MK, mkT, "vec"), ("mv", MV, mv_nat, "vec"),
                ("aq", AQ, aqT, "act"), ("ak", AK, akT, "act"), ("av", AV, av_nat, "vec")]
    def input_tile(col):
        return [w_in[0, :, col:col + P]]
    w_tiles = [input_tile(col + P * m) for _, col, _, _ in sections for m in range(4)]
    EARLY = len(w_tiles)
    w_tiles += [input_tile(MO + P * m) for m in range(4)] + [input_tile(GA + P * m) for m in range(2 * KD)]
    w_tiles += [[w_att_branch[0, :, P * m:P * (m + 1)], w_ml_branch[0, :, P * m:P * (m + 1)]] for m in range(2)]
    side = []
    for c, (name, _, _, who) in enumerate(sections):
        if name in ("mv", "av"):
            new = [(name, (c, j, t), who) for j in range(2) for t in range(NT)]
        else:
            new = [(name, (c, m, h), who) for m in range(4) for h in range(2)]
        if c < 3:
            units += new
        else:
            side += new
    units += [("gate", (i, h), "act") for i in range(2) for h in range(2)]
    units += [("mk_turn", t, "act") for t in range(NT)]
    side += [("ak_turn", t, "act") for t in range(NT)]
    BANKS = 4
    FIRST, STEPS = 4, MH * NT
    beside, n = [], FIRST
    for q in range(STEPS):
        count = min(2 if q % NT in (1, NT - 1) else 1, len(side) - n)
        beside.append(range(n, n + count))
        n += count
    assert n == len(side)

    def step_of(u):
        return next((q for q in range(STEPS) if u in beside[q]), -1)

    def evicted(u):
        who = units[u][2]
        return {"vec": vec_evicted, "act": act_evicted}[who], sum(v[2] == who for v in units[:u + 1])

    def side_evicted(u):
        who = side[u][2]
        return {"vec": side_vec, "act": side_act}[who], sum(v[2] == who for v in side[:u + 1])

    def last(name):
        return max(u for u, v in enumerate(units) if v[0] == name)

    def pair_used(p):
        if 2 * p >= EARLY:
            return z_done, 4 * (p - EARLY // 2) + 4
        c, half = divmod(p, 2)
        among, done = (units, unit_done) if c < 3 else (side, side_done)
        mine = [u for u, v in enumerate(among) if v[0] == sections[c][0]]
        return done, mine[(half + 1) * len(mine) // 2 - 1] + 1

    def products(pe_out, weights, inputs):
        parts = ((weights[0], inputs[0]), (weights[0], inputs[1]), (weights[1], inputs[0]))
        for kk in range(KD):
            for p, (a, b) in enumerate(parts):
                ins = nc.tensor.matmul(pe_out, a(kk), b(kk), start=(kk == 0 and p == 0), stop=(kk == KD - 1 and p == 2))
        return ins

    def cut(high, low, view):
        return tuple((lambda kk, part=part: view(part, kk)) for part in (high, low))

    def weight_cols(i, n=P):
        lo = P * (i % 2)
        return cut(w_high, w_low, lambda part, kk: part[:, (i // 2) % 2, kk, lo:lo + n])

    def frames(lo, n):
        return cut(xnT_high, xnT_low, lambda part, kk: part[:, kk, lo:lo + n])

    DMAS_OUT = 4 + 6

    def wqk_of(q):
        return pT[:, q % 2, :, :].rearrange("p s n -> p (s n)")

    with nc.Block() as block:
        @block.sync
        def _(sp):
            for t in range(NT):
                sp.dma_start(x[0:ROWS[t], t, :], x_prompt[0, t * P:(t + 1) * P, :] if t < 4 else x_sample[0]).then_inc(x_loaded[t], 16)
                if t == 0:
                    sp.dma_start(g1[:, :], norm1_g[0].rearrange("(k p) -> p k", p=P)).then_inc(g1_loaded, 16)
            sp.dma_start(kc_nat, cache_att_k[0, 0].rearrange("(s p) h d -> p s (h d)", p=P)).then_inc(cache_loaded, 16)
            sp.dma_start(table[:, 0, :], att_rel_bias[0, 1:P + 1, :]).then_inc(tab_loaded, 16)
            sp.dma_start(table[:, 1, :], att_rel_bias[0, P + 1:2 * P + 1, :]).then_inc(tab_loaded, 16)
            def load_tile(i):
                if i >= 2:
                    sp.wait_ge(w_low_done, i - 1)
                parts = w_tiles[i]
                for j, part in enumerate(parts):
                    rows = slice(j * KD // len(parts), (j + 1) * KD // len(parts))
                    sp.dma_start(w_raw[:, i % 2, rows], part.rearrange("(k p) n -> p k n", p=P)).then_inc(raw_loaded[i % 2], 16)
            for i in range(2):
                load_tile(i)
            sp.dma_start(wg_raw[:, :, :], w_in[0, :, GATES:GA].rearrange("(k p) n -> p k n", p=P)).then_inc(wg_loaded, 16)
            sp.dma_start(b_gates[:, :], b_in[0, GA:GA + 2 * D].rearrange("(m p) -> p m", p=P)).then_inc(const_loaded, 16)
            sp.dma_start(b_col[:, :], b_in[0, 0:GATES].rearrange("(m p) -> p m", p=P)).then_inc(const_loaded, 16)
            sp.dma_start(small[:, 0:2], b_in[0, GATES:GA].rearrange("(i h) -> h i", h=MH)).then_inc(const_loaded, 16)
            sp.dma_start(small[:, 2:3], ml_f_bias.rearrange("a h -> h a")).then_inc(const_loaded, 16)
            sp.dma_start(small[:, 3:4], state_mlstm_m[0].rearrange("a h -> h a")).then_inc(const_loaded, 16)
            sp.dma_start(b_av[:, :], b_in[0, AV:AV + 512].partition_broadcast(P)).then_inc(const_loaded, 16)
            sp.dma_start(b_mv[:, :], b_in[0, MV:MV + 512].partition_broadcast(P)).then_inc(const_loaded, 16)
            sp.dma_start(state[:, :, 0:P], state_mlstm_C[0, 0].rearrange("h d e -> d h e")).then_inc(const_loaded, 16)
            sp.dma_start(state[:, :, P], state_mlstm_n[0, 0].rearrange("h d -> d h")).then_inc(const_loaded, 16)
            for i in range(2, EARLY + 4):
                load_tile(i)
                if i == 5:
                    sp.wait_ge(line_done, 1)
                    sp.dma_start(k.line_dram, bcast(line, 1, P)).then_inc(line_stored, 16)
            sp.wait_ge(*side_evicted(len(side) - 1))
            sp.dma_start(att_k_prompt[0, 0].rearrange("(t p) h d -> p t (h d)", p=P), ak_nat[:, 0:4, :]).then_inc(stored, 16)
            sp.dma_start(att_k_sample[0, 0].rearrange("p h d -> p (h d)"), ak_nat[0:TS, 4, :]).then_inc(stored, 16)
            sp.wait_ge(side_vec, sum(v[2] == "vec" for v in side))
            sp.dma_start(att_v_prompt[0, 0].rearrange("(t p) h d -> p t (h d)", p=P), av_nat[:, 0:4, :]).then_inc(stored, 16)
            sp.dma_start(att_v_sample[0, 0].rearrange("p h d -> p (h d)"), av_nat[0:TS, 4, :]).then_inc(stored, 16)
            sp.wait_ge(ml_head, 2 * MH)
            sp.dma_start(m_prompt[0].rearrange("a h -> h a"), row[:, 4, S - 1:S]).then_inc(m_stored, 16)
            sp.dma_start(m_sample[0].rearrange("a h -> h a"), row[:, 4, T - 1:T]).then_inc(m_stored, 16)
            sp.dma_start(vc, cache_att_v[0, 0].rearrange("(s p) h d -> p s (h d)", p=P)).then_inc(vc_loaded, 16)
            sp.wait_ge(m_stored, 32)
            sp.wait_ge(line_stored, 16)
            for h in range(AH):
                sp.dma_start(bias[:, h, :], bass.AP(k.line_dram.tensor, h * P * (BW + P) + P, [[BW + P - 1, P], [1, BW]])
                             ).then_inc(bias_loaded[h], 16)
            sp.dma_start(C_prompt[0, 0].rearrange("h d e -> d h e"), c_out[:, :, 0:P]).then_inc(stored, 16)
            sp.dma_start(n_prompt[0, 0].rearrange("h d -> d h"), c_out[:, :, P]).then_inc(stored, 16)
            sp.dma_start(C_sample[0, 0].rearrange("h d e -> d h e"), state[:, :, 0:P]).then_inc(stored, 16)
            sp.dma_start(n_sample[0, 0].rearrange("h d -> d h"), state[:, :, P]).then_inc(stored, 16)
            for u in range(2 * GATE_TILES):
                m, h = divmod(u, 2)
                if h == 0 and EARLY + 4 + m < len(w_tiles):
                    load_tile(EARLY + 4 + m)
                sp.wait_ge(z_evicted, u + 1)
                sp.dma_start(k.gates_dram[m, :, h * HALF:(h + 1) * HALF], z_out[:, h, :]).then_inc(z_stored[h], 16)
            for h in range(2):
                sp.wait_ge(z_stored[h], 16 * GATE_TILES)
            sp.wait_ge(stored, 16 * (DMAS_OUT - 2))

        @block.gpsimd
        def _(pool):
            nc.gpsimd.memset(ident[:, :], 0.0).then_inc(pool_const, 1)
            nc.gpsimd.memset(flip[:, :], 0.0).then_inc(pool_const, 1)
            nc.gpsimd.memset(heads[:, :, :], 0.0).then_inc(pool_const, 1)
            pool.wait_ge(pool_const, 3)
            nc.gpsimd.affine_select(out=ident[:, :], in_=ident[:, :], compare_op=ALU.not_equal, fill=1.0, base=0,
                                    pattern=[[-1, P]], channel_multiplier=1).then_inc(pool_const, 1)
            nc.gpsimd.affine_select(out=flip[:, :], in_=flip[:, :], compare_op=ALU.not_equal, fill=1.0, base=1 - P,
                                    pattern=[[1, P]], channel_multiplier=1).then_inc(pool_const, 1)
            nc.gpsimd.affine_select(out=heads[:, :, :], in_=heads[:, :, :], compare_op=ALU.not_equal, fill=1.0, base=0,
                                    pattern=[[-1, MH], [0, P]], channel_multiplier=1).then_inc(pool_const, 1)
            nc.gpsimd.iota(k.iota[:, :], pattern=[[1, P]], base=0, channel_multiplier=0,
                           allow_small_or_imprecise_dtypes=True).then_inc(pool_const, 1)

            def split(i):
                pool.wait_ge(raw_loaded[i % 2], 16 * sum(len(parts) for parts in w_tiles[i % 2:i + 1:2]))
                if i % 2 == 0 and i >= 4:
                    pool.wait_ge(*pair_used(i // 2 - 2))
                high, low = (part[:, (i // 2) % 2, :, P * (i % 2):P * (i % 2) + P] for part in (w_high, w_low))
                nc.gpsimd.tensor_copy(high, w_raw[:, i % 2]).then_inc(w_high_done, 1)
                pool.wait_ge(w_high_done, i + 1)
                nc.gpsimd.tensor_tensor(low, w_raw[:, i % 2], high, ALU.subtract).then_inc(w_low_done, 1)

            BEFORE = 4 * 3 + 4
            for i in range(BEFORE):
                split(i)
                if i == 1:
                    pool.wait_ge(wg_loaded, 16)
                    nc.gpsimd.tensor_copy(wg_high[:, :, :], wg_raw[:, :, :]).then_inc(wg_split, 1)
                    pool.wait_ge(wg_split, 1)
                    nc.gpsimd.tensor_tensor(wg_low[:, :, :], wg_raw[:, :, :], wg_high[:, :, :], ALU.subtract).then_inc(wg_split, 1)
            q, tile = 0, BEFORE
            for h in range(MH):
                for s in range(NT):
                    n = ROWS[s]
                    lo = P * s if s < 4 else 0
                    pool.wait_ge(ml_w, q + 1)
                    diag = work[0:n, q % 2, lo:lo + n]
                    nc.gpsimd.affine_select(out=diag, in_=diag, compare_op=ALU.is_ge, fill=0.0, base=0,
                                            pattern=[[1, n]], channel_multiplier=-1).then_inc(ml_masked, 1)
                    if tile < EARLY + 4 and step_of(pair_used(tile // 2 - 2)[1] - 1) < q:
                        split(tile)
                        tile += 1
                    q += 1
            for i in range(tile, len(w_tiles)):
                split(i)

        @block.scalar
        def _(act):
            norm_scalar(nc, k, act, 0, xn, x_loaded, [16] * NT)
            act.wait_ge(g1_loaded, 16)
            for u, (kind, arg, who) in enumerate(units):
                if kind == "mq" and arg == (0, 0, 0):
                    act.wait_ge(const_loaded, 144)
                if kind == "xn":
                    act.wait_ge(unit_done, u + 1)
                    xn_high(nc, ps[:, u % BANKS], xnT_high, g1, *arg).then_inc(high_out, 1)
                if who != "act":
                    continue
                act.wait_ge(unit_done, u + 1)
                b = u % BANKS
                if kind == "cache":
                    ins = nc.scalar.copy(kcT[:, :, arg * P:(arg + 1) * P], ps[:, b, :].rearrange("p (g n) -> p g n", g=4))
                elif kind == "line":
                    at = BW - P * arg
                    ins = nc.scalar.copy(line[:, at:at + P], ps[0:AH, b, 0:P])
                elif kind == "gate":
                    i, h = arg
                    ins = nc.scalar.activation(row[:, i, h * HALF:(h + 1) * HALF], ps[0:MH, b, 0:HALF], ACT.Identity,
                                               bias=small[:, i:i + 1])
                elif kind == "mk_turn":
                    r = ROWS[arg]
                    ins = nc.scalar.copy(mk_nat[0:r, arg, :], ps[0:r, b, :])
                else:
                    c, m, h = arg
                    col = sections[c][1] // P + m
                    ins = nc.scalar.activation(sections[c][2][:, m, h * HALF:(h + 1) * HALF], ps[:, b, 0:HALF], ACT.Identity,
                                               bias=b_col[:, col:col + 1])
                ins.then_inc(act_evicted, 1)

            def side_out(u):
                kind, arg, who = side[u]
                if who != "act":
                    return
                act.wait_ge(side_done, u + 1)
                if kind == "ak_turn":
                    r = ROWS[arg]
                    ins = nc.scalar.copy(ak_nat[0:r, arg, :], ps[0:r, u % 2, :])
                else:
                    c, m, h = arg
                    b, scale = (b_aq[:, m:m + 1], AD ** -0.5) if kind == "aq" else (b_col[:, AK // P + m:AK // P + m + 1], 1.0)
                    ins = nc.scalar.activation(sections[c][2][:, m, h * HALF:(h + 1) * HALF], ps[:, u % 2, 0:HALF], ACT.Identity, bias=b, scale=scale)
                ins.then_inc(side_act, 1)
            act.wait_ge(gate_vec, 1)
            nc.scalar.activation(row[:, 3, :], row[:, 2, :], ACT.Exp, scale=-1.0).then_inc(gate_act, 1)
            act.wait_ge(aq_bias, 1)
            side_out(0)
            act.wait_ge(gate_vec, 2)
            nc.scalar.activation(row[:, 3, :], row[:, 2, :], ACT.Ln).then_inc(gate_act, 1)
            for u in range(1, FIRST):
                side_out(u)
            act.wait_ge(gate_vec, 3)
            nc.scalar.activation(row[:, 6, :], row[:, 4, :], ACT.Exp, scale=-1.0).then_inc(gate_act, 1)
            nc.scalar.activation(row[:, 0, S:T], row[:, 2, S:T], ACT.Exp, scale=-1.0).then_inc(gate_act, 1)
            for h in range(MH):
                act.wait_ge(ml_rows, h + 1)
                if h >= 1:
                    act.wait_ge(ml_head, 2 * h)
                nc.scalar.copy(M_bc, ps[:, 0, :]).then_inc(ml_em, 1)
                nc.scalar.copy(em_bc, ps[:, 2, :]).then_inc(ml_em, 1)
                nc.scalar.copy(samp[:, 0:3, :], ps[:, 7, 2 * P:2 * P + 3 * TS].rearrange("p (a n) -> p a n", a=3)).then_inc(ml_em, 1)

                def decay(q):
                    s = q % NT
                    n = ROWS[s]
                    lo, hi = (P * s, S) if s < 4 else (0, TS)
                    act.wait_ge(ml_gap, q + 1)
                    if q >= 2:
                        act.wait_ge(ml_wqk, q - 1)
                        act.wait_ge(ml_vw, q - 1)
                    nc.scalar.activation(work[0:n, q % 2, lo:hi], work[0:n, 2 + q % 2, lo:hi], ACT.Exp, scale=-1.0).then_inc(ml_w, 1)
                decay(NT * h)
                for s in range(NT):
                    if s + 1 < NT:
                        decay(NT * h + s + 1)
                    for u in beside[NT * h + s]:
                        side_out(u)
            def exp_scores(u):
                h, t = divmod(u, NT)
                r, n = ROWS[t], (t + 1) * P if t < 4 else T
                act.wait_ge(at_max, u + 1)
                if u >= 2:
                    act.wait_ge(at_turned, u - 1)
                nc.scalar.activation(work[0:r, u % 2, 0:n], work[0:r, 2 + u % 2, 0:n], ACT.Exp, bias=amax[0:r, u % 2:u % 2 + 1],
                                     accum_out=asum[0:r, u % 2:u % 2 + 1]).then_inc(at_exp, 1)

            def copy_turned(u):
                h, t = divmod(u, NT)
                act.wait_ge(at_turned, u + 1)
                if u >= 2:
                    act.wait_ge(at_pv, u - 1)
                if t < 4:
                    nc.scalar.copy(pT[:, u % 2, 0:t + 1, :], ps[:, 6, 0:(t + 1) * P].rearrange("p (s n) -> p s n", n=P)).then_inc(at_copied, 1)
                else:
                    nc.scalar.copy(pT[:, u % 2, 0:4, 0:TS], ps[:, 6, 0:4 * TS].rearrange("p (s n) -> p s n", n=TS))
                    nc.scalar.copy(pT[0:TS, u % 2, 4, 0:TS], ps[0:TS, 6, 4 * TS:5 * TS]).then_inc(at_copied, 1)

            def gate_out(u):
                m, h = divmod(u, 2)
                b = b_col[:, MO // P + m:MO // P + m + 1] if m < 4 else b_gates[:, m - 4:m - 3]
                act.wait_ge(z_done, u + 1)
                if m >= 1:
                    act.wait_ge(z_stored[h], 16 * m)
                nc.scalar.activation(z_out[:, h, :], ps[:, u % 3, 0:HALF], ACT.Identity, bias=b).then_inc(z_evicted, 1)
            for u in range(AH * NT + 1):
                if u < AH * NT:
                    exp_scores(u)
                    gate_out(u)
                if u >= 1:
                    copy_turned(u - 1)

        @block.vector
        def _(dve):
            nc.vector.memset(k.ones[:, :], 1.0).then_inc(vec_const, 1)
            link = linker(dve, vec_chain)
            for t in norm_vector(nc, k, dve, 0):
                r = ROWS[t]
                nc.vector.tensor_scalar(xn[0:r, t, :], x[0:r, t, :], k.rstd[0:r, t:t + 1], None, ALU.mult).then_inc(normed, 1)
            for u, (kind, arg, who) in enumerate(units):
                if kind == "mk" and arg == (1, 0, 0):
                    dve.wait_ge(const_loaded, 144)
                    ev, n = evicted(last("line"))
                    dve.wait_ge(ev, n)
                    nc.vector.tensor_scalar(line[:, 0:S].rearrange("p (a b) -> p a b", b=P), bcast(k.ones[0:AH, :], 1, S // P),
                                            line[:, S:S + 1], None, ALU.mult).then_inc(line_done, 1)
                if who != "vec":
                    continue
                dve.wait_ge(unit_done, u + 1)
                b = u % BANKS
                if kind == "xn":
                    dve.wait_ge(high_out, u + 1)
                    ins = xn_low(nc, ps[:, b], xnT_high, xnT_low, g1, *arg)
                elif kind == "mv":
                    c, j, t = arg
                    r, cols = ROWS[t], slice(2 * P * j, 2 * P * (j + 1))
                    ins = nc.vector.tensor_tensor(mv_nat[0:r, t, cols], ps[0:r, b, 0:2 * P], b_mv[0:r, cols], ALU.add)
                else:
                    c, m, h = arg
                    col = sections[c][1] // P + m
                    ins = nc.vector.tensor_scalar(sections[c][2][:, m, h * HALF:(h + 1) * HALF], ps[:, b, 0:HALF],
                                                  b_col[:, col:col + 1], ML_SCALE, ALU.add, ALU.mult)
                ins.then_inc(vec_evicted, 1)
            nc.vector.tensor_scalar(b_aq[:, :], b_col[:, AQ // P:AQ // P + 4], AD ** -0.5, None, ALU.mult).then_inc(aq_bias, 1)
            ev, n = evicted(last("gate"))
            dve.wait_ge(ev, n)
            link(nc.vector.tensor_scalar(row[:, 1, :], row[:, 1, :], small[:, 2:3], None, ALU.add))
            link(nc.vector.tensor_scalar(row[:, 4, :], row[:, 1, :], -1.0, None, ALU.mult))
            nc.vector.tensor_tensor(row[:, 2, :], row[:, 1, :], row[:, 4, :], ALU.max).then_inc(gate_vec, 1)
            dve.wait_ge(gate_act, 1)
            nc.vector.tensor_scalar(row[:, 2, :], row[:, 3, :], 1.0, None, ALU.add).then_inc(gate_vec, 1)
            dve.wait_ge(gate_act, 2)
            link(nc.vector.scalar_tensor_tensor(out=row[:, 2, :], in0=row[:, 1, :], scalar=0.0, in1=row[:, 3, :], op0=ALU.min, op1=ALU.subtract))
            link(nc.vector.memset(row[:, 5, :], 1.0))
            for lo, hi in ((0, S), (S, T)):
                link(nc.vector.tensor_tensor_scan(row[:, 3, lo:hi], row[:, 5, lo:hi], row[:, 2, lo:hi], 0.0, ALU.mult, ALU.add))
            link(nc.vector.tensor_tensor(row[:, 1, :], row[:, 0, :], row[:, 3, :], ALU.subtract))
            for lo, hi, first in ((0, S, NEG), (S, T, small[:, 3:4])):
                link(nc.vector.tensor_tensor_scan(row[:, 5, lo:hi], row[:, 1, lo:hi], row[:, 1, lo:hi], first, ALU.max, ALU.max))
            link(nc.vector.tensor_tensor(row[:, 4, :], row[:, 3, :], row[:, 5, :], ALU.add))
            nc.vector.tensor_scalar(row[:, 2, S:T], row[:, 5, S:T], small[:, 3:4], None, ALU.subtract).then_inc(gate_vec, 1)
            dve.wait_ge(c_turned, 1)
            nc.vector.tensor_copy(c_col[:, 0:4, :], ps[:, 7, 0:16].rearrange("p (t h) -> p t h", h=MH)).then_inc(c_copied, 1)
            nc.vector.tensor_copy(c_col[0:TS, 4, :], ps[0:TS, 7, 16:20]).then_inc(c_copied, 1)
            dve.wait_ge(c_copied, 2)

            def gap(q):
                h, s = divmod(q, NT)
                n = ROWS[s]
                lo, hi = (P * s, S) if s < 4 else (0, TS)
                if q >= 2:
                    dve.wait_ge(ml_w, q - 1)
                nc.vector.tensor_scalar(work[0:n, 2 + q % 2, lo:hi], M_bc[0:n, lo:hi] if s < 4 else samp[0:n, 0, :], c_col[0:n, s, h:h + 1], 0.0,
                                        ALU.subtract, ALU.max).then_inc(ml_gap, 1)

            def weigh(q):
                h, s = divmod(q, NT)
                n = ROWS[s]
                lo, hi = (P * s, S) if s < 4 else (0, TS)
                dve.wait_ge(ml_masked, q + 1)
                dve.wait_ge(ml_qk, q + 1)
                if q >= 2:
                    dve.wait_ge(ml_used, q - 1)
                end = work[0:n, q % 2, hi - 1:hi]
                nc.vector.tensor_scalar(vw[0:n, q % 2, 0:P], mv_nat[0:n, s, h * P:(h + 1) * P], end, None, ALU.mult)
                nc.vector.tensor_copy(vw[0:n, q % 2, P:P + 1], end).then_inc(ml_vw, 1)
                nc.vector.tensor_tensor(wqk_of(q)[0:n, lo:hi], work[0:n, q % 2, lo:hi], ps[0:n, 3 + q % 2, lo:hi], ALU.mult).then_inc(ml_wqk, 1)

            def side_out(u):
                kind, arg, who = side[u]
                if who == "vec":
                    _, j, t = arg
                    r, cols = ROWS[t], slice(2 * P * j, 2 * P * (j + 1))
                    dve.wait_ge(side_done, u + 1)
                    nc.vector.tensor_tensor(av_nat[0:r, t, cols], ps[0:r, u % 2, 0:2 * P], b_av[0:r, cols], ALU.add).then_inc(side_vec, 1)

            dve.wait_ge(line_stored, 16)
            for h in range(MH):
                dve.wait_ge(ml_em, 3 * h + 3)
                dve.wait_ge(ml_qk, NT * h + 1)
                link(nc.vector.tensor_tensor(samp[:, 3, :], mqT[:, h, S:T], samp[:, 1, :], ALU.mult))
                nc.vector.tensor_scalar(n_rep[:, :], k.ones[:, :], state[:, h, P:P + 1], None, ALU.mult).then_inc(ml_sample, 1)
                gap(NT * h)
                for s in range(NT):
                    if s + 1 < NT:
                        gap(NT * h + s + 1)
                    weigh(NT * h + s)
                    if s + 1 < NT:
                        for u in beside[NT * h + s]:
                            side_out(u)
                dve.wait_ge(ml_used, NT * h + 4)
                link(nc.vector.scalar_tensor_tensor(out=em_bc, in0=ps[:, 6, :], scalar=-1.0, in1=em_bc, op0=ALU.mult, op1=ALU.max))
                link(nc.vector.tensor_tensor(em_bc, ps[:, 6, :], em_bc, ALU.max))
                link(nc.vector.reciprocal(em_bc, em_bc))
                nc.vector.tensor_tensor(mqT[:, h, 0:S], ps[:, 5, :], em_bc, ALU.mult)
                nc.vector.tensor_copy(c_out[:, h, :], ps[:, 7, 0:P + 1]).then_inc(ml_head, 1)
                dve.wait_ge(ml_used, NT * h + 5)
                link(nc.vector.scalar_tensor_tensor(out=samp[:, 2, :], in0=ps[:, 2, TS:2 * TS], scalar=-1.0, in1=samp[:, 2, :], op0=ALU.mult, op1=ALU.max))
                link(nc.vector.tensor_tensor(samp[:, 2, :], ps[:, 2, TS:2 * TS], samp[:, 2, :], ALU.max))
                link(nc.vector.reciprocal(samp[:, 2, :], samp[:, 2, :]))
                nc.vector.tensor_tensor(mqT[:, h, S:T], ps[:, 2, 0:TS], samp[:, 2, :], ALU.mult)
                nc.vector.scalar_tensor_tensor(out=state[:, h, :], in0=state[:, h, :], scalar=samp[:, 1, TS - 1:TS], in1=ps[:, 2, 128:129 + P],
                                               op0=ALU.mult, op1=ALU.add).then_inc(ml_head, 1)
                for u in beside[NT * h + NT - 1]:
                    side_out(u)
            def add_bias(u):
                h, t = divmod(u, NT)
                if t == 0:
                    dve.wait_ge(bias_loaded[h], 16)
                    nc.vector.memset(bias[0:CHUNK, h, BW - CHUNK:BW], NEG).then_inc(bias_masked, 1)
                    dve.wait_ge(bias_masked, h + 1)
                r, n = ROWS[t], (t + 1) * P if t < 4 else S
                off = BW - n if t < 4 else 0
                dve.wait_ge(at_scored, u + 1)
                if u >= 2:
                    dve.wait_ge(at_exp, u - 1)
                sc = work[0:r, 2 + u % 2, :]
                ins = nc.vector.tensor_tensor(sc[:, 0:n], ps[0:r, 4 + u % 2, 0:n], bias[0:r, h, off:off + n], ALU.add)
                if t == 4:
                    ins.then_inc(at_added, 1)
                    ins = nc.vector.tensor_tensor(sc[:, S:T], ps[0:TS, 3, 0:TS], bias[0:TS, h, S:T], ALU.add)
                ins.then_inc(at_added, 1)
                dve.wait_ge(at_added, u + 1 + sum(1 for v in range(u + 1) if v % NT == 4))
                nc.vector.tensor_reduce(amax[0:r, u % 2:u % 2 + 1], sc[:, 0:n if t < 4 else T], AX.X, ALU.max, negate=True).then_inc(at_max, 1)

            def normalise(u):
                h, t = divmod(u, NT)
                r, n = ROWS[t], (t + 1) * P if t < 4 else T
                dve.wait_ge(at_exp, u + 1)
                link(nc.vector.reciprocal(asum[0:r, 2 + u % 2:3 + u % 2], asum[0:r, u % 2:u % 2 + 1]))
                nc.vector.tensor_scalar(work[0:r, u % 2, 0:n], work[0:r, u % 2, 0:n], asum[0:r, 2 + u % 2:3 + u % 2], None, ALU.mult).then_inc(at_norm, 1)

            def take_out(u):
                h, t = divmod(u, NT)
                r, lo = ROWS[t], AD * (h % 2)
                dve.wait_ge(at_pv, u + 1)
                nc.vector.tensor_copy(aqT[lo:lo + AD, h // 2, t * P:t * P + r], ps[lo:lo + AD, 7, 0:r]).then_inc(at_out, 1)
            for u in range(AH * NT + 2):
                if u < AH * NT:
                    add_bias(u)
                if 1 <= u <= AH * NT:
                    normalise(u - 1)
                if u >= 2:
                    take_out(u - 2)

        @block.tensor
        def _(pe):
            pe.wait_ge(pool_const, 7)
            pe.wait_ge(vec_const, 1)

            def turn_back(src, t, b):
                r = ROWS[t]
                for i in range(4):
                    ins = nc.tensor.transpose(ps[0:r, b, i * P:(i + 1) * P], src[:, i, t * P:t * P + r], ident[:, :])
                return ins

            def section(kind, arg, b):
                c = arg[0]
                if kind in ("mv", "av"):
                    _, j, t = arg
                    r = ROWS[t]
                    pe.wait_ge(w_low_done, 4 * c + 2 * j + 2)
                    return products(ps[0:r, b, 0:2 * P], frames(t * P, r), weight_cols(4 * c + 2 * j, 2 * P))
                _, m, h = arg
                pe.wait_ge(w_low_done, 4 * c + m + 1)
                return products(ps[:, b, 0:HALF], weight_cols(4 * c + m), frames(h * HALF, HALF))

            def side_unit(u):
                kind, arg, who = side[u]
                if u >= 2:
                    pe.wait_ge(*side_evicted(u - 2))
                if kind == "ak_turn":
                    if arg == 0:
                        pe.wait_ge(*side_evicted(max(v for v, w in enumerate(side) if w[0] == "ak")))
                    ins = turn_back(akT, arg, u % 2)
                else:
                    ins = section(kind, arg, u % 2)
                ins.then_inc(side_done, 1)
            for u, (kind, arg, who) in enumerate(units):
                if u >= BANKS:
                    pe.wait_ge(*evicted(u - BANKS))
                b = u % BANKS
                if kind == "xn":
                    t, g = arg
                    r = ROWS[t]
                    pe.wait_ge(normed, t + 1)
                    for i in range(4):
                        kk = 4 * g + i
                        ins = nc.tensor.transpose(ps[:, b, i * P:i * P + r], xn[0:r, t, kk * P:(kk + 1) * P], ident[0:r, 0:r])
                elif kind == "cache":
                    pe.wait_ge(cache_loaded, 16)
                    for i in range(4):
                        ins = nc.tensor.transpose(ps[:, b, i * P:(i + 1) * P], kc_nat[:, arg, i * P:(i + 1) * P], ident[:, :])
                elif kind == "line":
                    pe.wait_ge(tab_loaded, 32)
                    ins = nc.tensor.matmul(ps[0:AH, b, 0:P], table[:, arg, :], flip[:, :], start=True, stop=True)
                elif kind == "gate":
                    i, h = arg
                    pe.wait_ge(wg_split, 2)
                    ins = products(ps[0:MH, b, 0:HALF], cut(wg_high, wg_low, lambda part, kk: part[:, kk, i * MH:(i + 1) * MH]),
                                   frames(h * HALF, HALF))
                elif kind == "mk_turn":
                    if arg == 0:
                        pe.wait_ge(*evicted(last("mk")))
                    ins = turn_back(mkT, arg, b)
                else:
                    if arg[0] == 0:
                        pe.wait_ge(*evicted(last("xn")))
                    ins = section(kind, arg, b)
                ins.then_inc(unit_done, 1)
            for u in range(len(units) - BANKS, len(units)):
                pe.wait_ge(*evicted(u))
            for u in range(FIRST):
                side_unit(u)
            pe.wait_ge(gate_vec, 3)
            for t in range(NT):
                r = ROWS[t]
                ins = nc.tensor.transpose(ps[0:r, 7, t * MH:(t + 1) * MH], row[:, 1, t * P:t * P + r], ident[0:MH, 0:MH])
            ins.then_inc(c_turned, 1)
            pe.wait_ge(gate_act, 4)

            def side_before(h):
                return beside[NT * h].start

            def scores(q):
                h, s = divmod(q, NT)
                n = ROWS[s]
                lo, hi = (P * s, S) if s < 4 else (0, TS)
                if q >= 2:
                    pe.wait_ge(ml_wqk, q - 1)
                nc.tensor.matmul(ps[0:n, 3 + q % 2, lo:hi], mkT[:, h, s * P:s * P + n], mqT[:, h, (s * P if s < 4 else S):(S if s < 4 else T)],
                                 start=True, stop=True).then_inc(ml_qk, 1)
            for h in range(MH):
                if h == 0:
                    pe.wait_ge(c_copied, 2)
                else:
                    pe.wait_ge(ml_head, 2 * h)
                for u in range(max(side_before(h) - 2, 0), side_before(h)):
                    pe.wait_ge(*side_evicted(u))
                nc.tensor.matmul(ps[:, 0, :], heads[:, h, :], row[:, 5, 0:S], start=True, stop=True)
                for i, r in enumerate((5, 0, 6)):
                    nc.tensor.matmul(ps[:, 7, 2 * P + i * TS:2 * P + (i + 1) * TS], heads[:, h, :], row[:, r, S:T], start=True, stop=True)
                nc.tensor.matmul(ps[:, 2, :], heads[:, h, :], row[:, 6, 0:S], start=True, stop=True).then_inc(ml_rows, 1)
                scores(NT * h)
                for s in range(NT):
                    q = NT * h + s
                    n = ROWS[s]
                    if s + 1 < NT:
                        scores(q + 1)
                    if s == 0:
                        pe.wait_ge(ml_em, 3 * h + 3)
                    for u in beside[q][0:1]:
                        side_unit(u)
                    pe.wait_ge(ml_wqk, q + 1)
                    pe.wait_ge(ml_vw, q + 1)
                    wqk = wqk_of(q)
                    vh = mv_nat[0:n, s, h * P:(h + 1) * P]
                    kh = mk_nat[0:n, s, h * P:(h + 1) * P]
                    if s < 4:
                        nc.tensor.matmul(ps[:, 5, s * P:S], vh, wqk[:, s * P:S], start=(s == 0), stop=(s == 3))
                        nc.tensor.matmul(ps[:, 6, s * P:S], k.ones[:, :], wqk[:, s * P:S], start=(s == 0), stop=(s == 3))
                        nc.tensor.matmul(ps[:, 7, 0:P + 1], kh, vw[:, q % 2, :], start=(s == 0), stop=(s == 3)).then_inc(ml_used, 1)
                    else:
                        pe.wait_ge(ml_sample, h + 1)
                        nc.tensor.matmul(ps[:, 2, 0:TS], vh, wqk[0:n, 0:TS], start=True, stop=False)
                        nc.tensor.matmul(ps[:, 2, 0:TS], state[:, h, 0:P], samp[:, 3, :], start=False, stop=True)
                        nc.tensor.matmul(ps[:, 2, TS:2 * TS], k.ones[0:n, :], wqk[0:n, 0:TS], start=True, stop=False)
                        nc.tensor.matmul(ps[:, 2, TS:2 * TS], n_rep[:, :], samp[:, 3, :], start=False, stop=True)
                        nc.tensor.matmul(ps[:, 2, P:2 * P + 1], kh, vw[0:n, q % 2, :], start=True, stop=True).then_inc(ml_used, 1)
                    for u in beside[q][1:]:
                        side_unit(u)
            pe.wait_ge(ml_head, 2 * MH)
            for u in range(len(side) - 2, len(side)):
                pe.wait_ge(*side_evicted(u))

            def att_scores(u):
                h, t = divmod(u, NT)
                r, n, lo = ROWS[t], (t + 1) * P, AD * (h % 2)
                if u >= 2:
                    pe.wait_ge(at_max, u - 1)
                qh = aqT[lo:lo + AD, h // 2, t * P:t * P + r]
                if t < 4:
                    nc.tensor.matmul(ps[0:r, 4 + u % 2, 0:n], qh, akT[lo:lo + AD, h // 2, 0:n], start=True, stop=True).then_inc(at_scored, 1)
                else:
                    nc.tensor.matmul(ps[0:r, 4 + u % 2, 0:S], qh, kcT[lo:lo + AD, h // 2, :], start=True, stop=True)
                    nc.tensor.matmul(ps[0:r, 3, 0:TS], qh, akT[lo:lo + AD, h // 2, S:T], start=True, stop=True).then_inc(at_scored, 1)

            def turn(u):
                h, t = divmod(u, NT)
                r = ROWS[t]
                pe.wait_ge(at_norm, u + 1)
                if u >= 1:
                    pe.wait_ge(at_copied, u)
                for s in range(t + 1):
                    n = ROWS[s]
                    ins = nc.tensor.transpose(ps[0:n, 6, s * r:(s + 1) * r], work[0:r, u % 2, s * P:s * P + n], ident[0:r, 0:r])
                ins.then_inc(at_turned, 1)

            def weigh_values(u):
                h, t = divmod(u, NT)
                r, lo = ROWS[t], AD * (h % 2)
                if t == 4:
                    pe.wait_ge(vc_loaded, 16)
                pe.wait_ge(at_copied, u + 1)
                if u >= 1:
                    pe.wait_ge(at_out, u)
                for s in range(t + 1):
                    n = ROWS[s]
                    v = (av_nat if t < 4 or s == 4 else vc)[0:n, s, h * AD:(h + 1) * AD]
                    ins = nc.tensor.matmul(ps[lo:lo + AD, 7, 0:r], v, pT[0:n, u % 2, s, 0:r], start=(s == 0), stop=(s == t))
                ins.then_inc(at_pv, 1)

            def gate_unit(u):
                m, h = divmod(u, 2)
                pe.wait_ge(w_low_done, EARLY + m + 1)
                if u >= 3:
                    pe.wait_ge(z_evicted, u - 2)
                products(ps[:, u % 3, 0:HALF], weight_cols(EARLY + m), frames(h * HALF, HALF)).then_inc(z_done, 1)
            assert 2 * GATE_TILES == AH * NT
            for u in range(AH * NT + 2):
                if u < AH * NT:
                    att_scores(u)
                    gate_unit(u)
                if 1 <= u <= AH * NT:
                    turn(u - 1)
                if u >= 2:
                    weigh_values(u - 2)




def merge(nc, k, hold, x_prompt, x_sample, w_att_branch, w_ml_branch, w_out):
    ps, x, aqT, mqT = k.ps, k.x, k.aqT, k.mqT
    sem = k.sem
    W = 2 * P
    CHUNKS = 2 * D // W
    w_raw = hold("w2_raw", [P, 2, KD, W])
    w_high, w_low = k.w_high, k.w_low
    in_high = hold("in_high", [P, KD, T], F32R)
    in_low = hold("in_low", [P, KD, T], F32R)
    gate = hold("gate", [P, 4, 2, T])
    mo = gate[:, 0:2].rearrange("p a g t -> p (a g) t")
    gated = hold("gated", [P, 2, 2, HALF])
    merged = hold("merged", [P, 2, HALF])
    merged_high = hold("merged_high", [P, KD, T], F32R)
    merged_low = hold("merged_low", [P, KD, T], F32R)
    RING = 4
    w_loaded = [sem("merge_w_loaded0"), sem("merge_w_loaded1")]
    gate_loaded = [sem(f"gate_loaded{i}") for i in range(RING)]
    mo_loaded, x_loaded = sem("mo_loaded"), sem("x_reloaded")
    w_high_done, w_low_done = sem("w2_high_done"), sem("w2_low_done")
    mo_sig, mo_used, in_high_done, in_low_done = sem("mo_sig"), sem("mo_used"), sem("in_high_done"), sem("in_low_done")
    g_sig, a_done, a_used, summed, merged_high_done, merged_low_done = (sem(n) for n in (
        "g_sig", "a_done", "a_used", "summed", "merged_high_done", "merged_low_done"))
    out_done, out_added = sem("out_done"), sem("out_added")
    OUTS = NT * D // W

    with nc.Block() as block:
        @block.sync
        def _(sp):
            def load_gates(j):
                for g in range(2):
                    sp.dma_start(gate[:, j % RING, g, :], k.gates_dram[4 + KD * g + j]).then_inc(gate_loaded[j % RING], 16)

            sp.dma_start(mo, k.gates_dram[0:4].rearrange("m p t -> p m t")).then_inc(mo_loaded, 16)
            for c in range(1, CHUNKS):
                if c >= 3:
                    sp.wait_ge(w_low_done, c - 2)
                if c < CHUNKS // 2:
                    for i, wb in enumerate((w_att_branch, w_ml_branch)):
                        sp.dma_start(w_raw[:, c % 2, 4 * i:4 * i + 4, :], wb[0, :, c * W:(c + 1) * W].rearrange("(k p) n -> p k n", p=P)
                                     ).then_inc(w_loaded[c % 2], 16)
                else:
                    for i in range(2):
                        col = (c - CHUNKS // 2) * W
                        sp.dma_start(w_raw[:, c % 2, 4 * i:4 * i + 4, :], w_out[0, i * 512:(i + 1) * 512, col:col + W].rearrange("(k p) n -> p k n", p=P)
                                     ).then_inc(w_loaded[c % 2], 16)
                if c == 1:
                    sp.wait_ge(mo_used, 4)
                    for j in range(RING):
                        load_gates(j)
                    sp.dma_start(x[:, 0:4, :], x_prompt[0].rearrange("(t p) d -> p t d", p=P)).then_inc(x_loaded, 16)
                    sp.dma_start(x[0:TS, 4, :], x_sample[0]).then_inc(x_loaded, 16)
                if c in (3, 4):
                    for j in (2 * c - 2, 2 * c - 1):
                        sp.wait_ge(summed, 2 * (j - RING) + 2)
                        load_gates(j)

        @block.gpsimd
        def _(pool):
            for c in range(1, CHUNKS):
                pool.wait_ge(w_high_done, c)
                nc.gpsimd.tensor_tensor(w_low[:, c % 2], w_raw[:, c % 2], w_high[:, c % 2], ALU.subtract).then_inc(w_low_done, 1)

        @block.tensor
        def _(pe):
            for u in range(2 * KD):
                j, h = divmod(u, 2)
                c, lo = j // 2, (j % 2) * P
                cols = slice(h * HALF, (h + 1) * HALF)
                if c >= 1:
                    pe.wait_ge(w_low_done, c)
                for g in range(2):
                    if u == 0:
                        pe.wait_ge(in_low_done, 4 * (g + 1))
                    if u >= 2:
                        pe.wait_ge(a_used, 2 * (u - 2) + g + 1)
                    for kk in range(4 * g, 4 * g + 4):
                        for p, (w, v) in enumerate(((w_high, in_high), (w_high, in_low), (w_low, in_high))):
                            ins = nc.tensor.matmul(ps[:, 2 * (u % 2) + g, 0:HALF], w[:, c % 2, kk, lo:lo + P], v[:, kk, cols],
                                                   start=(kk == 4 * g and p == 0), stop=(kk == 4 * g + 3 and p == 2))
                    ins.then_inc(a_done, 1)
            pe.wait_ge(merged_low_done, 2 * KD)
            for u in range(OUTS):
                i, t = divmod(u, NT)
                c, r = CHUNKS // 2 + i, ROWS[t]
                pe.wait_ge(w_low_done, c)
                if u >= 4:
                    pe.wait_ge(out_added, u - 3)
                for kk in range(KD):
                    for p, (v, w) in enumerate(((merged_high, w_high), (merged_high, w_low), (merged_low, w_high))):
                        ins = nc.tensor.matmul(ps[0:r, 4 + u % 4, 0:W], v[:, kk, t * P:t * P + r], w[:, c % 2, kk, :],
                                               start=(kk == 0 and p == 0), stop=(kk == KD - 1 and p == 2))
                ins.then_inc(out_done, 1)

        @block.scalar
        def _(act):
            def split_weights(c):
                act.wait_ge(w_loaded[c % 2], 32 * ((c + 1) // 2))
                if 2 <= c < 2 + CHUNKS // 2:
                    act.wait_ge(a_done, 2 * 4 * (c - 1))
                elif c >= 2:
                    act.wait_ge(out_done, NT * (c - 1 - CHUNKS // 2))
                nc.scalar.copy(w_high[:, c % 2], w_raw[:, c % 2]).then_inc(w_high_done, 1)

            for m in range(4):
                nc.scalar.copy(in_high[:, m, :], aqT[:, m, :]).then_inc(in_high_done, 1)
            act.wait_ge(mo_loaded, 16)
            for m in range(4):
                nc.scalar.activation(mo[:, m, :], mo[:, m, :], ACT.Sigmoid).then_inc(mo_sig, 1)
            for m in range(4):
                act.wait_ge(mo_used, m + 1)
                nc.scalar.copy(in_high[:, 4 + m, :], mqT[:, m, :]).then_inc(in_high_done, 1)
            split_weights(1)
            for j in range(KD):
                act.wait_ge(gate_loaded[j % RING], 32 * (j // RING + 1))
                nc.scalar.activation(gate[:, j % RING], gate[:, j % RING], ACT.Sigmoid).then_inc(g_sig, 1)
                for h in range(2):
                    u = 2 * j + h
                    act.wait_ge(summed, u + 1)
                    nc.scalar.copy(merged_high[:, j, h * HALF:(h + 1) * HALF], merged[:, h, :]).then_inc(merged_high_done, 1)
                if j % 2 == 1:
                    split_weights(2 + j // 2)
            for c in range(2 + CHUNKS // 2, CHUNKS):
                split_weights(c)

        @block.vector
        def _(dve):
            for m in range(4):
                dve.wait_ge(in_high_done, m + 1)
                nc.vector.tensor_tensor(in_low[:, m, :], aqT[:, m, :], in_high[:, m, :], ALU.subtract).then_inc(in_low_done, 1)
            for m in range(4):
                dve.wait_ge(mo_sig, m + 1)
                nc.vector.tensor_tensor(mqT[:, m, :], mqT[:, m, :], mo[:, m, :], ALU.mult).then_inc(mo_used, 1)
            for m in range(4):
                dve.wait_ge(in_high_done, 4 + m + 1)
                nc.vector.tensor_tensor(in_low[:, 4 + m, :], mqT[:, m, :], in_high[:, 4 + m, :], ALU.subtract).then_inc(in_low_done, 1)
            for u in range(2 * KD):
                j, h = divmod(u, 2)
                dve.wait_ge(g_sig, j + 1)
                for g in range(2):
                    dve.wait_ge(a_done, 2 * u + g + 1)
                    nc.vector.tensor_tensor(gated[:, u % 2, g, :], ps[:, 2 * (u % 2) + g, 0:HALF], gate[:, j % RING, g, h * HALF:(h + 1) * HALF],
                                            ALU.mult).then_inc(a_used, 1)
                dve.wait_ge(a_used, 2 * u + 2)
                nc.vector.tensor_tensor(merged[:, h, :], gated[:, u % 2, 0, :], gated[:, u % 2, 1, :], ALU.add).then_inc(summed, 1)
                dve.wait_ge(merged_high_done, u + 1)
                nc.vector.tensor_tensor(merged_low[:, j, h * HALF:(h + 1) * HALF], merged[:, h, :], merged_high[:, j, h * HALF:(h + 1) * HALF],
                                        ALU.subtract).then_inc(merged_low_done, 1)
            dve.wait_ge(x_loaded, 32)
            for u in range(OUTS):
                i, t = divmod(u, NT)
                r = ROWS[t]
                dve.wait_ge(out_done, u + 1)
                xs = x[0:r, t, i * W:(i + 1) * W]
                nc.vector.tensor_tensor(xs, ps[0:r, 4 + u % 4, 0:W], xs, ALU.add).then_inc(out_added, 1)


def fold(ap):
    return ap.rearrange("r (a b j) -> r b a j", a=QUARTERS, j=BLK)


class Hidden:

    def __init__(self, nc, k, hold, peer_u):
        self.nc, self.k, self.peer_u = nc, k, peer_u
        self.u_nat = hold("u_nat", [P, QUAD, D])
        self.u_turned = hold("u_turned", [P, 2, KD, P])
        self.high = hold("uT_high", [P, 2, KD, P], F32R)
        self.low = hold("uT_low", [P, 2, KD, P], F32R)
        self.out = hold("gelu_out", [P, 2, T])
        self.u_loaded = [k.sem(f"u_loaded{v}") for v in range(QUAD)]
        self.turned, self.high_done, self.low_done = k.sem("u_turned_done"), k.sem("u_high_done"), k.sem("u_low_done")
        self.product_done, self.gelu_done = k.sem("u_product_done"), k.sem("gelu_done")
        self.stored = [k.sem("gelu_stored0"), k.sem("gelu_stored1")]

    def load(self, sp, q, v):
        n = QUAD * q + v
        after(sp, self.turned, n - QUAD + 1)
        for a in range(QUARTERS):
            sp.dma_start(self.u_nat[a * BLK:(a + 1) * BLK, v, :].rearrange("i (g d) -> i g d", g=P // BLK),
                         self.peer_u[0, ds(n * P, P), a * D // QUARTERS:(a + 1) * D // QUARTERS].rearrange("(g i) d -> i g d", i=BLK)
                         ).then_inc(self.u_loaded[v], 16)

    def transpose(self, dve, q, v):
        n = QUAD * q + v
        dve.wait_ge(self.u_loaded[v], 16 * QUARTERS * (q + 1))
        after(dve, self.low_done, n - 1)
        self.nc.vector.transpose(self.u_turned[:, v % 2, :, :].bitcast(U32).rearrange("p b (g i) -> p g b i", i=BLK),
                                 self.u_nat[:, v, :].bitcast(U32).rearrange("p (g b j) -> p g b j", g=P // BLK, j=BLK)).then_inc(self.turned, 1)

    def split_high(self, act, q, v):
        n = QUAD * q + v
        act.wait_ge(self.turned, n + 1)
        after(act, self.product_done, n - 1)
        self.nc.scalar.copy(self.high[:, v % 2], self.u_turned[:, v % 2]).then_inc(self.high_done, 1)

    def split_low(self, eng, q, v):
        eng.wait_ge(self.high_done, QUAD * q + v + 1)
        eng.tensor_tensor(self.low[:, v % 2], self.u_turned[:, v % 2], self.high[:, v % 2], ALU.subtract).then_inc(self.low_done, 1)

    def product(self, pe, q, v):
        n, b = QUAD * q + v, v % 2
        pe.wait_ge(self.low_done, n + 1)
        after(pe, self.gelu_done, n - 1)
        for h in range(2):
            for kk in range(KD):
                cols = slice(h * HALF, (h + 1) * HALF)
                for p, (w, x) in enumerate(((self.high, self.k.x_high), (self.high, self.k.x_low), (self.low, self.k.x_high))):
                    ins = self.nc.tensor.matmul(self.k.ps[:, 2 + 2 * b + h, 0:HALF], w[:, b, kk, :], x[:, kk, cols],
                                                start=(kk == 0 and p == 0), stop=(kk == KD - 1 and p == 2))
        ins.then_inc(self.product_done, 1)

    def gelu(self, act, q, v):
        n, b = QUAD * q + v, v % 2
        act.wait_ge(self.product_done, n + 1)
        after(act, self.stored[b], 16 * (2 * q + v // 2))
        self.nc.scalar.activation(self.out[:, b, :].rearrange("p (h n) -> p h n", h=2), self.k.ps[:, 2 + 2 * b:4 + 2 * b, 0:HALF], ACT.Gelu
                                  ).then_inc(self.gelu_done, 1)
        act.wait_ge(self.gelu_done, n + 1)
        act.dma_start(self.k.gelu_dram[ds(n, 1)].rearrange("a j n -> j (a n)"), self.out[:, b, :]).then_inc(self.stored[b], 16)

    def step(self, part, eng, q, v, last=False):
        def ahead(by):
            return (q, v + by) if v + by < QUAD else (q + 1, v + by - QUAD)

        def exists(by):
            return not (last and v + by >= QUAD)
        if part == "load" and not last:
            self.load(eng, q + 1, v)
        elif part == "product":
            self.product(eng, q, v)
        elif part == "gelu":
            if exists(1):
                self.split_high(eng, *ahead(1))
            self.gelu(eng, q, v)
        elif part == "transpose" and exists(2):
            self.transpose(eng, *ahead(2))
        elif part == "low" and exists(1):
            self.split_low(eng, *ahead(1))


def retrieve(nc, k, hold, hidden, norm2_g, peer_wq, peer_sub_keys):
    ps, x, ident, chosen = k.ps, k.x, k.ident, k.chosen
    sem = k.sem
    SUMS = 4 * TOPK + 4 * (TOPK - 4)
    STEPS = 2 * QUAD
    w_high = hold("wq_high", [P, 2, KD, P], F32R)
    w_low = hold("wq_low", [P, 2, KD, P], F32R)
    space = [k.v_nat[:, :, :].rearrange("p a b -> p (a b)"), k.quad_in[:, :, :, :].rearrange("p i a b -> p (i a b)")]
    w = [half[:, 0:KD * 512].rearrange("p (k n) -> p k n", k=KD) for half in space]
    g2 = hold("g2", [P, KD])
    xn = hold("xn_b", [P, NT, D])
    sk = hold("sk", [P, PH, P])
    skT = hold("skT", [P, PH, NK])
    qT = xn[:, :, :].rearrange("p t d -> p (t d)")[:, 0:PH * T].rearrange("p (h t) -> p h t", h=PH)
    SIDE = PH * NK
    sc = space[0][:, 0:2 * SIDE].rearrange("p (s h n) -> p s h n", s=2, h=PH)
    rest = space[0][:, 2 * SIDE:4 * SIDE].rearrange("p (s h n) -> p s h n", s=2, h=PH)
    one_hot = space[1][:, 0:SIDE].bitcast(BF16).rearrange("p (h a b) -> p h a b", h=PH, a=TOPK)
    left = space[1][:, 0:PH * SUMS].rearrange("p (h m) -> p h m", h=PH)
    q_tile = space[1][:, 2 * SIDE:3 * SIDE].rearrange("p (h n) -> p h n", h=PH)
    sv = hold("sv", [P, 2, PH, TOPK])
    si = hold("si", [P, 2, PH, TOPK], U32)
    sif = hold("sif", [P, 2, PH, TOPK], BF16)
    places = hold("places", [P, 2, PH, TOPK], BF16)
    iota16 = hold("iota16", [P, TOPK], BF16)
    fv = hold("fv", [P, PH, TOPK])
    fi = hold("fi", [P, PH, TOPK], U32)
    pos = hold("pos", [P, 3, PH, TOPK], U32)
    posf = hold("posf", [P, 3, PH, TOPK])
    picked = hold("picked", [P, 3, P])
    total = hold("total", [P, 2, PH])
    loaded, wq_loaded = sem("retrieve_loaded"), [sem("wq_loaded0"), sem("wq_loaded1")]
    normed = sem("normed2")
    turned, vec_out, sk_done, sk_out = sem("turned2"), sem("vec_out2"), sem("sk_done"), sem("sk_out")
    q_done, q_out, q_copied, s_done, s_out = sem("q_done"), sem("q_out"), sem("q_copied"), sem("s_done"), sem("s_out")
    x_high_out, w_high_done, w_low_done = sem("x_high_out"), sem("wq_high_done"), sem("wq_low_done")
    tile_sorted, gap_done, exp_done, pick_done, pick_turned, pick_out = (sem(n) for n in (
        "tile_sorted", "gap_done", "exp_done", "pick_done", "pick_turned", "pick_out"))

    BACK, AHEAD = 1, 4

    def score_bank(g):
        return 6 if g == 0 else 0

    def tiles(eng, tile):
        for t in range(NT):
            tile(t, ROWS[t])

    with nc.Block() as block:
        @block.gpsimd
        def _(pool):
            def tile(t, r):
                for v in range(STEPS):
                    hidden.step("low", pool, 2 * t + v // QUAD, v % QUAD)
            for m in range(PH):
                pool.wait_ge(w_high_done, m + 1)
                nc.gpsimd.tensor_tensor(w_low[:, m % 2], w[m // 4][:, :, (m % 4) * P:(m % 4 + 1) * P], w_high[:, m % 2], ALU.subtract
                                        ).then_inc(w_low_done, 1)
            hidden.split_low(pool, 0, 0)
            tiles(pool, tile)

        @block.sync
        def _(sp):
            for a in range(QUARTERS):
                sp.dma_start(g2[a * BLK:(a + 1) * BLK, :], norm2_g[0, a * D // QUARTERS:(a + 1) * D // QUARTERS].rearrange("(b j) -> j b", j=BLK)
                             ).then_inc(loaded, 16)
            sp.dma_start(sk[:, :, :].rearrange("n h (s d) -> n h s d", s=2), peer_sub_keys[0].rearrange("h s n d -> n h s d")).then_inc(loaded, 16)
            for c in range(2):
                for a in range(QUARTERS):
                    sp.dma_start(w[c][a * BLK:(a + 1) * BLK, :, :],
                                 peer_wq[0, a * D // QUARTERS:(a + 1) * D // QUARTERS, c * 512:(c + 1) * 512].rearrange("(b j) n -> j b n", j=BLK)
                                 ).then_inc(wq_loaded[c], 16)
            for v in range(QUAD):
                hidden.load(sp, 0, v)

            def tile(t, r):
                for v in range(STEPS):
                    hidden.step("load", sp, 2 * t + v // QUAD, v % QUAD)
            tiles(sp, tile)

        @block.scalar
        def _(act):
            norm_scalar(nc, k, act, 1, xn, None)
            act.wait_ge(loaded, 16 * (QUARTERS + 1))

            def split_weights(m):
                if m % 4 == 0:
                    act.wait_ge(wq_loaded[m // 4], 16 * QUARTERS)
                if m >= 2:
                    act.wait_ge(q_done, 2 * m - 2)
                nc.scalar.copy(w_high[:, m % 2], w[m // 4][:, :, (m % 4) * P:(m % 4 + 1) * P]).then_inc(w_high_done, 1)
            for u in range(2 * NT):
                act.wait_ge(turned, u + 1)
                xn_high(nc, ps[:, u % 4], k.x_high, g2, *divmod(u, 2)).then_inc(x_high_out, 1)
                if u in (2, 5):
                    split_weights(u // 3)
            for g in range(2):
                act.wait_ge(sk_done, g + 1)
                nc.scalar.copy(skT[:, 4 * g:4 * g + 4, :], ps[:, 6 + g, :].rearrange("p (h n) -> p h n", h=4)).then_inc(sk_out, 1)
            for u in range(2 * PH):
                act.wait_ge(q_done, u + 1)
                m, h = divmod(u, 2)
                if h == 1 and m + 2 < PH:
                    split_weights(m + 2)
                if u == 0:
                    act.wait_ge(turned, 2 * NT)
                nc.scalar.copy(qT[:, m, h * HALF:(h + 1) * HALF], ps[:, u % 4, 0:HALF]).then_inc(q_out, 1)
            act.wait_ge(q_out, 2 * PH)
            hidden.split_high(act, 0, 0)

            def queries_in(t):
                if t >= 1:
                    act.wait_ge(s_done, 2 * t)
                r = ROWS[t]
                nc.scalar.copy(q_tile[:, :, 0:r], qT[:, :, t * P:t * P + r]).then_inc(q_copied, 1)

            def scores_out(t):
                if t >= 1:
                    act.wait_ge(tile_sorted, t)
                r = ROWS[t]
                for g in range(2):
                    act.wait_ge(s_done, 2 * t + g + 1)
                    b = score_bank(g)
                    nc.scalar.copy(sc[0:r, :, 4 * g:4 * g + 4, :], ps[0:r, b:b + 2, :].rearrange("p s (h n) -> p s h n", h=4)).then_inc(s_out, 1)

            def pick_to_chosen(t):
                act.wait_ge(pick_turned, t + 1)
                r = ROWS[t]
                nc.scalar.copy(chosen[:, :, t * P:t * P + r], ps[:, 0, 0:3 * P].rearrange("p (a n) -> p a n", a=3)[:, :, 0:r]).then_inc(pick_out, 1)

            queries_in(0)
            scores_out(0)
            for t in range(NT):
                for v in range(STEPS):
                    if v == AHEAD and t + 1 < NT:
                        queries_in(t + 1)
                    if v == STEPS - 1:
                        act.wait_ge(gap_done, t + 1)
                        w3 = picked[0:ROWS[t], 2, :]
                        nc.scalar.activation(w3, w3, ACT.Exp).then_inc(exp_done, 1)
                    hidden.step("gelu", act, 2 * t + v // QUAD, v % QUAD)
                    if v == BACK and t >= 1:
                        pick_to_chosen(t - 1)
                    if v == AHEAD and t + 1 < NT:
                        scores_out(t + 1)
            pick_to_chosen(NT - 1)

        @block.tensor
        def _(pe):
            for u in range(2 * NT):
                t, g = divmod(u, 2)
                r = ROWS[t]
                pe.wait_ge(normed, t + 1)
                if u >= 4:
                    pe.wait_ge(vec_out, u - 3)
                for i in range(4):
                    kk = 4 * g + i
                    ins = nc.tensor.transpose(ps[:, u % 4, i * P:i * P + r], xn[0:r, t, kk * P:(kk + 1) * P], ident[0:r, 0:r])
                ins.then_inc(turned, 1)
            pe.wait_ge(loaded, 16 * (QUARTERS + 1))
            for g in range(2):
                for i in range(4):
                    ins = nc.tensor.transpose(ps[:, 6 + g, i * P:(i + 1) * P], sk[:, 4 * g + i, :], ident[:, :])
                ins.then_inc(sk_done, 1)
            pe.wait_ge(vec_out, 2 * NT)
            for u in range(2 * PH):
                m, h = divmod(u, 2)
                if u >= 4:
                    pe.wait_ge(q_out, u - 3)
                pe.wait_ge(w_low_done, m + 1)
                for kk in range(KD):
                    for p, (a, b) in enumerate(((w_high, k.x_high), (w_high, k.x_low), (w_low, k.x_high))):
                        ins = nc.tensor.matmul(ps[:, u % 4, 0:HALF], a[:, m % 2, kk, :], b[:, kk, h * HALF:(h + 1) * HALF],
                                               start=(kk == 0 and p == 0), stop=(kk == KD - 1 and p == 2))
                ins.then_inc(q_done, 1)
            pe.wait_ge(q_out, 2 * PH)
            pe.wait_ge(sk_out, 2)

            def scores(t):
                r = ROWS[t]
                pe.wait_ge(q_copied, t + 1)
                if t >= 1:
                    pe.wait_ge(s_out, 2 * t)
                if t >= 2:
                    pe.wait_ge(pick_out, t - 1)
                for g in range(2):
                    for h in range(4 * g, 4 * g + 4):
                        for s in range(2):
                            lo = CHUNK * s
                            ins = nc.tensor.matmul(ps[0:r, score_bank(g) + s, (h % 4) * NK:(h % 4 + 1) * NK], q_tile[lo:lo + CHUNK, h, 0:r],
                                                   skT[lo:lo + CHUNK, h, :], start=True, stop=True)
                    ins.then_inc(s_done, 1)

            def turn_picks(t):
                r = ROWS[t]
                pe.wait_ge(pick_done, t + 1)
                pe.wait_ge(s_out, 2 * min(t + 2, NT))
                for i in range(3):
                    ins = nc.tensor.transpose(ps[:, 0, i * P:i * P + r], picked[0:r, i, :], ident[0:r, 0:r])
                ins.then_inc(pick_turned, 1)

            scores(0)
            for t in range(NT):
                for v in range(STEPS):
                    hidden.step("product", pe, 2 * t + v // QUAD, v % QUAD)
                    if v == BACK and t >= 1:
                        turn_picks(t - 1)
                    if v == AHEAD and t + 1 < NT:
                        scores(t + 1)
            turn_picks(NT - 1)

        @block.vector
        def _(dve):
            for t in norm_vector(nc, k, dve, 1):
                r = ROWS[t]
                nc.vector.tensor_scalar(xn[0:r, t, :].rearrange("r (b a j) -> r b a j", b=KD, a=QUARTERS), fold(x[0:r, t, :]),
                                        k.rstd[0:r, t:t + 1], None, ALU.mult).then_inc(normed, 1)
            dve.wait_ge(loaded, 16 * (QUARTERS + 1))
            for u in range(2 * NT):
                dve.wait_ge(x_high_out, u + 1)
                xn_low(nc, ps[:, u % 4], k.x_high, k.x_low, g2, *divmod(u, 2)).then_inc(vec_out, 1)
            for v in range(2):
                hidden.transpose(dve, 0, v)

            def sort_tile(t, r):
                base, count = LINKS * t, [0]

                def link(ins):
                    count[0] += 1
                    ins.then_inc(sorting, 1)
                    dve.wait_ge(sorting, base + count[0])

                def top16(values, left, best, index, done=None):
                    for v, b in zip(values, best):
                        ins = nc.vector.max(b[:, 0:8], v)
                    link(ins)
                    for v, l, b in zip(values, left, best):
                        ins = nc.vector.match_replace(l, b[:, 0:8], v, LOWEST)
                    link(ins)
                    yield
                    for v, b, i in zip(values, best, index):
                        ins = nc.vector.max_index(i[:, 0:8], b[:, 0:8], v)
                    if done is not None:
                        ins.then_inc(done, 1)
                    for l, b in zip(left, best):
                        ins = nc.vector.max(b[:, 8:16], l)
                    link(ins)
                    yield
                    for l, b, i in zip(left, best, index):
                        ins = nc.vector.max_index(i[:, 8:16], b[:, 8:16], l)
                    link(ins)

                dve.wait_ge(s_out, 2 * t + 2)
                both = [(s, h) for s in range(2) for h in range(PH)]
                yield from top16([sc[0:r, s, h, :] for s, h in both], [rest[0:r, s, h, :] for s, h in both],
                                 [sv[0:r, s, h, :] for s, h in both], [si[0:r, s, h, :] for s, h in both], tile_sorted)
                link(nc.vector.tensor_copy(sif[0:r], si[0:r]))
                sums = rest[0:r].rearrange("p s h n -> p (s h n)")[:, 0:PH * SUMS].rearrange("p (h m) -> p h m", h=PH)
                link(nc.vector.tensor_tensor(sums[:, :, 0:4 * TOPK].rearrange("p h (a b) -> p h a b", a=4), bcast(sv[0:r, 0, :, 0:4], 3, TOPK),
                                             bcast(sv[0:r, 1], 2, 4), ALU.add))
                link(nc.vector.tensor_tensor(sums[:, :, 4 * TOPK:SUMS].rearrange("p h (a b) -> p h a b", b=4), bcast(sv[0:r, 0, :, 4:TOPK], 3, 4),
                                             bcast(sv[0:r, 1, :, 0:4], 2, TOPK - 4), ALU.add))
                yield
                yield from top16([sums[:, h, :] for h in range(PH)], [left[0:r, h, :] for h in range(PH)],
                                 [fv[0:r, h, :] for h in range(PH)], [fi[0:r, h, :] for h in range(PH)])
                w3 = picked[0:r, 2, :].rearrange("p (h n) -> p h n", h=PH)
                after(dve, pick_turned, t)
                nc.vector.tensor_tensor(w3, fv[0:r], fv[0:r, :, 0:1].broadcast_to([r, PH, TOPK]), ALU.subtract).then_inc(gap_done, 1)
                nc.vector.tensor_copy(pos[0:r, 2], fi[0:r])
                nc.vector.tensor_scalar(pos[0:r, 0], fi[0:r], 4, None, ALU.logical_shift_right)
                link(nc.vector.tensor_scalar(pos[0:r, 1], fi[0:r], 2, None, ALU.logical_shift_right))
                link(nc.vector.tensor_copy(posf[0:r], pos[0:r]))
                link(nc.vector.scalar_tensor_tensor(out=posf[0:r, 0], in0=posf[0:r, 1], scalar=-12.0, in1=posf[0:r, 0], op0=ALU.add, op1=ALU.max))
                link(nc.vector.tensor_scalar(posf[0:r, 1], posf[0:r, 0], 4.0, 48.0, ALU.mult, ALU.add))
                nc.vector.tensor_copy(places[0:r, 0], posf[0:r, 0])
                link(nc.vector.scalar_tensor_tensor(out=posf[0:r, 1], in0=posf[0:r, 0], scalar=16.0, in1=posf[0:r, 1], op0=ALU.mult, op1=ALU.min))
                link(nc.vector.tensor_tensor(places[0:r, 1], posf[0:r, 2], posf[0:r, 1], ALU.subtract))
                yield
                for s in range(2):
                    hot = one_hot[0:r].rearrange("p h a b -> p (h a) b")
                    at = bcast(places[0:r, s].rearrange("p h a -> p (h a)"), 2, TOPK)
                    link(nc.vector.tensor_tensor(hot, at, bcast(iota16[0:r, :], 1, PH * TOPK), ALU.is_equal))
                    link(nc.vector.tensor_tensor(one_hot[0:r], one_hot[0:r], bcast(sif[0:r, s], 2, TOPK), ALU.mult))
                    link(nc.vector.tensor_reduce(picked[0:r, s, :], hot, AX.X, ALU.add))
                    yield
                dve.wait_ge(exp_done, t + 1)
                link(nc.vector.tensor_reduce(total[0:r, 0], w3, AX.X, ALU.add))
                link(nc.vector.reciprocal(total[0:r, 1], total[0:r, 0]))
                nc.vector.tensor_tensor(w3, w3, bcast(total[0:r, 1], 2, TOPK), ALU.mult).then_inc(pick_done, 1)
                assert count[0] == LINKS

            nc.vector.tensor_copy(iota16[:, :], k.iota[:, 0:TOPK])
            LINKS = 4 + 3 + 4 + 6 + 6 + 2
            sorting = sem("sorting")

            def tile(t, r):
                v = 0
                for _ in sort_tile(t, r):
                    hidden.step("transpose", dve, 2 * t + v // QUAD, v % QUAD)
                    v += 1
                assert v == STEPS
            tiles(dve, tile)


def route(nc, k, hold, hidden, peer_v):
    ps, iota, chosen, route_dram = k.ps, k.iota, k.chosen, k.route_dram
    sem = k.sem
    FEW = 4
    BATCHES = GRP // FEW
    EARLY = 2 * NT
    first = hold("first", [P, BATCHES, FEW, P])
    second = hold("second", [P, BATCHES, FEW, P])
    index = hold("index", [P, 2, GRP // 2])
    dense = hold("dense", [P, 2, P, GRP])
    first_ready, second_ready, product_done, batch_out = (sem(n) for n in (
        "first_ready", "second_ready", "route_product_done", "batch_out"))
    group_stored = [sem("group_stored0"), sem("group_stored1")]

    def turns(eng, turn):
        turn(0, 0, 0)
        turn(1, 1, 0)
        with eng.Fori(1, NGRP // 2) as j:
            turn(2 * j, 0, j)
            turn(2 * j + 1, 1, j)
        turn(NGRP - 1, 0, NGRP // 2)

    def remaining(eng, *parts):
        with eng.Fori(EARLY + NGRP, P // QUAD - 1) as q:
            for v in range(QUAD):
                for part in parts:
                    hidden.step(part, eng, q, v)
        for v in range(QUAD):
            for part in parts:
                hidden.step(part, eng, P // QUAD - 1, v, last=True)

    with nc.Block() as block:
        @block.gpsimd
        def _(pool):
            def turn(i, slot, filled):
                for half in range(2):
                    after(pool, product_done, (i - 1) * BATCHES + (half + 1) * BATCHES // 2)
                    nc.gpsimd.tensor_copy(index[:, half, :], chosen[:, 0, ds(i * GRP + half * GRP // 2, GRP // 2)])
                    pool.drain()
                    for v in range(GRP // 2):
                        b, f = half * BATCHES // 2 + v // FEW, v % FEW
                        ins = nc.gpsimd.tensor_scalar(first[:, b, f, :], iota[:, :], index[:, half, v:v + 1], None, ALU.is_equal)
                        if f == FEW - 1:
                            ins.then_inc(first_ready, 1)
            turns(pool, turn)

        @block.vector
        def _(dve):
            def turn(i, slot, filled):
                for b in range(BATCHES):
                    if b % 2 == 0:
                        hidden.step("transpose", dve, EARLY + i, b // 2)
                        hidden.step("low", dve, EARLY + i, b // 2)
                    after(dve, product_done, (i - 1) * BATCHES + b + 1)
                    for f in range(FEW):
                        n = i * GRP + b * FEW + f
                        ins = nc.vector.tensor_scalar(second[:, b, f, :], iota[:, :], chosen[:, 1, ds(n, 1)], chosen[:, 2, ds(n, 1)],
                                                      ALU.is_equal, ALU.mult)
                    ins.then_inc(second_ready, 1)
            turns(dve, turn)
            remaining(dve, "transpose", "low")

        @block.tensor
        def _(pe):
            def batch(i, b):
                pe.wait_ge(first_ready, i * BATCHES + b + 1)
                pe.wait_ge(second_ready, i * BATCHES + b + 1)
                after(pe, batch_out, i * BATCHES + b - 1)
                for f in range(FEW):
                    ins = nc.tensor.matmul(ps[:, 6 + b % 2, f * P:(f + 1) * P], second[:, b, f, :], first[:, b, f, :], start=True, stop=True)
                ins.then_inc(product_done, 1)

            def turn(i, slot, filled):
                for v in range(QUAD):
                    hidden.step("product", pe, EARLY + i, v)
                    batch(i, 2 * v)
                    batch(i, 2 * v + 1)
            turns(pe, turn)
            remaining(pe, "product")

        @block.scalar
        def _(act):
            def turn(i, slot, filled):
                for b in range(BATCHES):
                    if b % 2 == 0:
                        hidden.step("gelu", act, EARLY + i, b // 2)
                    act.wait_ge(product_done, i * BATCHES + b + 1)
                    if b == 0:
                        after(act, group_stored[slot], 16 * filled)
                    nc.scalar.copy(dense[:, slot, :, b * FEW:(b + 1) * FEW].rearrange("p i n -> p n i"),
                                   ps[:, 6 + b % 2, :].rearrange("p (n i) -> p n i", n=FEW)).then_inc(batch_out, 1)
            turns(act, turn)
            remaining(act, "gelu")
            for b in range(2):
                act.wait_ge(hidden.stored[b], 16 * P // 2)

        @block.sync
        def _(sp):
            def turn(i, slot, filled):
                for v in range(QUAD):
                    hidden.step("load", sp, EARLY + i, v)
                sp.wait_ge(batch_out, (i + 1) * BATCHES)
                sp.dma_start(route_dram[ds(i, 1)].rearrange("a j i n -> j (a i n)"), dense[:, slot].rearrange("p i n -> p (i n)")
                             ).then_inc(group_stored[slot], 16)
            turns(sp, turn)
            remaining(sp, "load")
            sp.wait_ge(group_stored[0], 16 * (NGRP // 2 + 1))
            sp.wait_ge(group_stored[1], 16 * (NGRP // 2))
            for b in range(2):
                sp.wait_ge(hidden.stored[b], 16 * QUAD // 2)
            load_quad_in(sp, k, 0, k.gelu, k.routing, k.in_loaded[0])
            for v in range(QUAD):
                load_v(sp, k, peer_v, 0, v)


def load_quad_in(sp, k, q, gelu, routing, loaded):
    sp.dma_start(gelu, k.gelu_dram[ds(q * QUAD, QUAD)].rearrange("a j n -> j a n")).then_inc(loaded, 16)
    sp.dma_start(routing.rearrange("j g a n -> j g (a n)"),
                 k.route_dram[:, :, ds(q * QUAD, QUAD), :].rearrange("g j a n -> j g (a n)")).then_inc(loaded, 16)


def load_v(sp, k, peer_v, q, v):
    sp.dma_start(k.v_nat[:, v, :], peer_v[0, ds((q * QUAD + v) * P, P), :]).then_inc(k.v_loaded[v], 16)


def experts(nc, k, hold, peer_v):
    ps, acc = k.ps, k.acc
    sem = k.sem
    QUADS = P // QUAD
    UNITS = 2 * KD
    BANKS = 8
    v_nat, v_loaded, in_loaded = k.v_nat, k.v_loaded, k.in_loaded
    v_high = hold("v_high", [P, 2, QUAD, D], F32R)
    v_low = hold("v_low", [P, 2, QUAD, D], F32R)
    gelu = (k.gelu, hold("gelu_in1", [P, QUAD, T])[:, :, :])
    routing = (k.routing, hold("routing_in1", [P, NGRP, QUAD, GRP])[:, :, :, :])
    hid_high = hold("hid_high", [P, 2, QUAD, T], F32R)
    hid_low = hold("hid_low", [P, 2, QUAD, T], F32R)
    v_high_done, v_low_done, hid_done, hid_high_done, hid_low_done, out_done, out_added = (sem(n) for n in (
        "v_high_done", "v_low_done", "hid_done", "hid_high_done", "hid_low_done", "expert_out_done", "expert_out_added"))

    def quads(eng, quad):
        for s in range(2):
            quad(s, s, 0)
        with eng.Fori(1, QUADS // 2) as j:
            for s in range(2):
                quad(2 * j + s, s, j)

    with nc.Block() as block:
        @block.sync
        def _(sp):
            def quad(q, s, j):
                after(sp, hid_low_done, QUAD * (q - 1))
                load_quad_in(sp, k, q, gelu[s], routing[s], in_loaded[s])
                for v in range(QUAD):
                    sp.wait_ge(v_low_done, QUAD * (q - 1) + v + 1 if j is not None else QUAD)
                    load_v(sp, k, peer_v, q, v)
            quad(1, 1, None)
            with sp.Fori(1, QUADS // 2) as j:
                for s in range(2):
                    quad(2 * j + s, s, j)

        @block.gpsimd
        def _(pool):
            def low(q, s, v):
                pool.wait_ge(v_high_done, QUAD * q + v + 1)
                nc.gpsimd.tensor_tensor(v_low[:, s, v, :], v_nat[:, v, :], v_high[:, s, v, :], ALU.subtract).then_inc(v_low_done, 1)

            def quad(q, s, j):
                for v in range(QUAD):
                    low(q, s, v)
            for v in range(QUAD // 2):
                low(0, 0, v)
            pool.wait_ge(v_low_done, QUAD)
            quad(1, 1, 0)
            with pool.Fori(1, QUADS // 2) as j:
                for s in range(2):
                    quad(2 * j + s, s, j)

        @block.scalar
        def _(act):
            def split_v(q, s, v):
                act.wait_ge(v_loaded[v], 16 * (q + 1))
                if v == 0:
                    after(act, out_done, UNITS * (q - 1))
                nc.scalar.copy(v_high[:, s, v, :], v_nat[:, v, :]).then_inc(v_high_done, 1)

            def split_hidden(q, s, v):
                act.wait_ge(hid_done, QUAD * q + v + 1)
                nc.scalar.copy(hid_high[:, s, v, :], gelu[s][:, v, :]).then_inc(hid_high_done, 1)

            def quad(q, s, j):
                for v in range(QUAD):
                    split_v(q, s, v)
                    split_hidden(q, s, v)
            for v in range(QUAD):
                split_v(0, 0, v)
            for v in range(QUAD):
                split_hidden(0, 0, v)
            quad(1, 1, 0)
            with act.Fori(1, QUADS // 2) as j:
                for s in range(2):
                    quad(2 * j + s, s, j)

        @block.vector
        def _(dve):
            def weigh(q, s, j, first=False):
                dve.wait_ge(in_loaded[s], 32 * (j + 1))
                for v in range(QUAD):
                    g = gelu[s][:, v, :].rearrange("p (g n) -> p g n", g=NGRP)
                    nc.vector.tensor_tensor(g, g, routing[s][:, :, v, :], ALU.mult).then_inc(hid_done, 1)
                if first:
                    for v in range(QUAD // 2, QUAD):
                        dve.wait_ge(v_high_done, v + 1)
                        nc.vector.tensor_tensor(v_low[:, 0, v, :], v_nat[:, v, :], v_high[:, 0, v, :], ALU.subtract).then_inc(v_low_done, 1)
                for v in range(QUAD):
                    dve.wait_ge(hid_high_done, QUAD * q + v + 1)
                    nc.vector.tensor_tensor(hid_low[:, s, v, :], gelu[s][:, v, :], hid_high[:, s, v, :], ALU.subtract).then_inc(hid_low_done, 1)

            def add(q, first=False):
                for o in range(UNITS):
                    kk, h = divmod(o, 2)
                    dve.wait_ge(out_done, q * UNITS + o + 1)
                    a = acc[:, kk, h * HALF:(h + 1) * HALF]
                    if first:
                        nc.vector.tensor_copy(a, ps[:, o % BANKS, 0:HALF]).then_inc(out_added, 1)
                    else:
                        nc.vector.tensor_tensor(a, ps[:, o % BANKS, 0:HALF], a, ALU.add).then_inc(out_added, 1)

            weigh(0, 0, 0, first=True)
            weigh(1, 1, 0)
            add(0, first=True)
            with dve.Fori(1, QUADS // 2) as j:
                weigh(2 * j, 0, j)
                add(2 * j - 1)
                weigh(2 * j + 1, 1, j)
                add(2 * j)
            add(QUADS - 1)

        @block.tensor
        def _(pe):
            def quad(q, s, j):
                pe.wait_ge(v_low_done, QUAD * (q + 1))
                pe.wait_ge(hid_low_done, QUAD * (q + 1))
                for o in range(UNITS):
                    kk, h = divmod(o, 2)
                    after(pe, out_added, q * UNITS + o - BANKS + 1)
                    for v in range(QUAD):
                        w = slice(kk * P, (kk + 1) * P)
                        cols = slice(h * HALF, (h + 1) * HALF)
                        for p, (a, b) in enumerate(((v_high, hid_high), (v_high, hid_low), (v_low, hid_high))):
                            ins = nc.tensor.matmul(ps[:, o % BANKS, 0:HALF], a[:, s, v, w], b[:, s, v, cols],
                                                   start=(v == 0 and p == 0), stop=(v == QUAD - 1 and p == 2))
                    ins.then_inc(out_done, 1)
            quads(pe, quad)


def finish(nc, k, hold, final_g, y_prompt, y_sample):
    ps, x, acc, ident = k.ps, k.x, k.acc, k.ident
    sem = k.sem
    g = hold("g_final", [P, D])
    y = hold("y", [P, NT, D])
    loaded, turned, added, ready, stored = (sem(n) for n in ("final_loaded", "turned3", "added3", "y_ready", "y_stored"))
    with nc.Block() as block:
        @block.sync
        def _(sp):
            sp.dma_start(g[:, :], final_g.partition_broadcast(P)).then_inc(loaded, 16)
            for t in range(NT):
                sp.wait_ge(ready, t + 1)
                out = y_prompt[0, t * P:(t + 1) * P, :] if t < 4 else y_sample[0]
                sp.dma_start(out, y[0:ROWS[t], t, :]).then_inc(stored, 16)
            sp.wait_ge(stored, 16 * NT)

        @block.tensor
        def _(pe):
            for t in range(NT):
                r, b = ROWS[t], 2 * (t % 4)
                if t >= 4:
                    pe.wait_ge(added, t - 3)
                for kk in range(KD):
                    ins = nc.tensor.transpose(ps[0:r, b + kk // 4, (kk % 4) * P:(kk % 4 + 1) * P], acc[:, kk, t * P:t * P + r], ident[:, :])
                ins.then_inc(turned, 1)

        @block.scalar
        def _(act):
            norm_scalar(nc, k, act, 2, y, [added] * NT, [t + 1 for t in range(NT)])

        @block.vector
        def _(dve):
            for t in range(NT):
                r, b = ROWS[t], 2 * (t % 4)
                dve.wait_ge(turned, t + 1)
                nc.vector.tensor_tensor(x[0:r, t, :], ps[0:r, b:b + 2, :].rearrange("p b n -> p (b n)"), x[0:r, t, :], ALU.add).then_inc(added, 1)
            dve.wait_ge(loaded, 16)
            for t in norm_vector(nc, k, dve, 2):
                r = ROWS[t]
                nc.vector.scalar_tensor_tensor(out=y[0:r, t, :], in0=x[0:r, t, :], scalar=k.rstd[0:r, t:t + 1], in1=g[0:r, :],
                                               op0=ALU.mult, op1=ALU.mult).then_inc(ready, 1)


_INS = ['x_prompt', 'x_sample', 'cache_att_k', 'cache_att_v', 'state_mlstm_C', 'state_mlstm_n', 'state_mlstm_m',
        'norm1_g', 'w_in', 'b_in', 'ml_f_bias', 'att_rel_bias', 'w_att_branch', 'w_ml_branch', 'w_out',
        'norm2_g', 'peer_wq', 'peer_sub_keys', 'peer_u', 'peer_v', 'final_g']
_OUTS = [(1, S, D), (1, TS, D), (1, 1, S, AH, AD), (1, 1, S, AH, AD), (1, 1, MH, P, P), (1, 1, MH, P), (1, 1, MH),
         (1, 1, TS, AH, AD), (1, 1, TS, AH, AD), (1, 1, MH, P, P), (1, 1, MH, P), (1, 1, MH)]


def kernel(**inputs):
    import numpy as _np
    import concourse.bacc as _bacc
    from concourse import mybir as _mybir
    from concourse.bass_utils import run_bass_kernel_spmd as _run

    nc = _bacc.Bacc("TRN2", target_bir_lowering=False, num_devices=1)
    arrays, args = {}, []
    for name in _INS:
        a = _np.ascontiguousarray(inputs[name])
        arrays[f"in_{name}_dram"] = a
        args.append(nc.dram_tensor(f"in_{name}_dram", a.shape, _mybir.dt.from_np(a.dtype), kind="ExternalInput").ap())
    for i, shape in enumerate(_OUTS):
        args.append(nc.dram_tensor(f"out_{i}_dram", shape, F32, kind="ExternalOutput").ap())
    with nc.allow_non_contiguous_dma(reason="short vectors laid out as columns"):
        program(nc, *args)
    r = _run(nc, [arrays], core_ids=[0])
    return tuple(r.results[0][f"out_{i}_dram"] for i in range(len(_OUTS)))
```
